# Optimizing a Trainium2 kernel written in Bass

```python
import math
import jax, jax.numpy as jnp
from jax import lax
import numpy as np

D_MODEL = 1024
BATCH = 1
SEQ = 512
DEPTH = 1

N_GROUPS = 4
GROUP_WIDTH = D_MODEL // N_GROUPS
HEAD_DIM = 64
GROUP_HEADS = GROUP_WIDTH // HEAD_DIM
CONV_CH = GROUP_WIDTH
CONV_WIDTH = 3
NSA_HEADS = GROUP_HEADS
CMP_LEN = 32
CMP_STRIDE = 16
SLC_LEN = 64
N_SLC = 16
WINDOW = 512
CMP_HIDDEN = GROUP_WIDTH
MLA_HEADS = GROUP_HEADS
Q_LORA = 3 * GROUP_WIDTH // 4
KV_LORA = GROUP_WIDTH // 2
NOPE_DIM = HEAD_DIM
ROPE_DIM = HEAD_DIM // 2
V_DIM = HEAD_DIM
ROPE_THETA = 10000.0
SB_HEADS = GROUP_HEADS
N_BUCKETS = 32
MAX_DISTANCE = 128
D_FF = 4 * D_MODEL
Q_BLOCK = 128
EPS = 1e-6

A_SIZES = [CONV_CH] * 3
NSA_SIZES = [NSA_HEADS * HEAD_DIM] + [HEAD_DIM] * 6 + [3 * NSA_HEADS]
MLA_SIZES = [Q_LORA, KV_LORA, ROPE_DIM]
SB_SIZES = [SB_HEADS * HEAD_DIM] * 3
IN_SIZES = A_SIZES + NSA_SIZES + MLA_SIZES + SB_SIZES
IN_COLS = sum(IN_SIZES)


f32 = jnp.float32

def rms_norm(x, w):
    x32 = x.astype(f32)
    y = x32 * lax.rsqrt(jnp.mean(x32 * x32, axis=-1, keepdims=True) + EPS)
    return (y * w.astype(f32)).astype(x.dtype)

def masked_softmax(logits, mask):
    logits = jnp.where(mask, logits, -jnp.inf)
    m = jnp.max(logits, axis=-1, keepdims=True)
    m = jnp.where(jnp.isfinite(m), m, 0.0)
    p = jnp.exp(logits - m)
    s = jnp.sum(p, axis=-1, keepdims=True)
    return p / jnp.where(s > 0, s, 1.0)

def t5_bucket(dist):
    max_exact = N_BUCKETS // 2
    d = jnp.maximum(dist, 0)
    large = max_exact + (jnp.log(jnp.maximum(d, 1).astype(f32) / max_exact)
                         / math.log(MAX_DISTANCE / max_exact) * (N_BUCKETS - max_exact)).astype(jnp.int32)
    large = jnp.minimum(large, N_BUCKETS - 1)
    return jnp.where(d < max_exact, d, large)

def rope_tables(S):
    inv = 1.0 / (ROPE_THETA ** (jnp.arange(0, ROPE_DIM, 2, dtype=f32) / ROPE_DIM))
    ang = jnp.arange(S, dtype=f32)[:, None] * inv[None, :]
    return jnp.cos(ang), jnp.sin(ang)

def apply_rope(x, cos, sin):
    x32 = x.astype(f32)
    x1, x2 = jnp.split(x32, 2, axis=-1)
    c = cos[:, None, :]
    s = sin[:, None, :]
    return jnp.concatenate([x1 * c - x2 * s, x1 * s + x2 * c], axis=-1).astype(x.dtype)

def split_cols(h, sizes):
    return jnp.split(h, np.cumsum(sizes)[:-1].tolist(), axis=-1)

def short_conv_mixer(b_gate, c_gate, u, conv_w, conv_b):
    v = c_gate * u
    y = lax.conv_general_dilated(v, conv_w[:, None, :].astype(v.dtype), window_strides=(1,),
                                 padding=[(CONV_WIDTH - 1, 0)], dimension_numbers=('NWC', 'WIO', 'NWC'),
                                 feature_group_count=v.shape[-1])
    return b_gate * (y + conv_b)

def compress_tokens(kv, cmp_idx, pos, w1, w2):
    B = kv.shape[0]
    blocks = kv[:, cmp_idx] + pos
    hdn = jax.nn.silu(blocks.reshape(B, blocks.shape[1], -1) @ w1)
    return hdn @ w2

def cmp_slc_overlap(n_cmp, n_slc):
    starts = np.arange(n_cmp) * CMP_STRIDE
    ends = starts + CMP_LEN
    s0 = np.arange(n_slc) * SLC_LEN
    s1 = s0 + SLC_LEN
    ov = np.clip(np.minimum(ends[:, None], s1[None]) - np.maximum(starts[:, None], s0[None]), 0, None)
    return (ov / CMP_LEN).astype(np.float32)

def nsa_mixer(q, kc_raw, vc_raw, ks, vs, kw, vw, gate_logits, qn, kn, cmp_pos, cmp_w1, cmp_w2, rel_bias):
    B, S, H, Dh = q.shape
    scale = Dh ** -0.5
    q = rms_norm(q, qn)
    tpos = jnp.arange(S)
    n_cmp = (S - CMP_LEN) // CMP_STRIDE + 1
    cmp_idx = np.arange(n_cmp)[:, None] * CMP_STRIDE + np.arange(CMP_LEN)[None, :]
    kc = rms_norm(compress_tokens(kc_raw, cmp_idx, cmp_pos[0], cmp_w1[0], cmp_w2[0]), kn[0])
    vc = compress_tokens(vc_raw, cmp_idx, cmp_pos[1], cmp_w1[1], cmp_w2[1])
    cmp_end = jnp.arange(n_cmp) * CMP_STRIDE + CMP_LEN - 1
    dist_c = tpos[:, None] - cmp_end[None, :]
    bias_c = rel_bias[t5_bucket(dist_c)].transpose(2, 0, 1)
    logits_c = jnp.einsum('bshd,bnd->bhsn', q, kc).astype(f32) * scale + bias_c
    p_c = masked_softmax(logits_c, dist_c >= 0)
    o_cmp = jnp.einsum('bhsn,bnd->bshd', p_c.astype(vc.dtype), vc)
    n_slc = S // SLC_LEN
    n_sel = min(N_SLC, n_slc)
    score = jnp.einsum('bhsn,nj->bsj', p_c, jnp.asarray(cmp_slc_overlap(n_cmp, n_slc)))
    blk = jnp.arange(n_slc)[None, :]
    t_blk = (tpos // SLC_LEN)[:, None]
    valid = blk * SLC_LEN <= tpos[:, None]
    forced = (blk == 0) | (blk == t_blk) | (blk == t_blk - 1)
    score = jnp.where(forced, jnp.inf, jnp.where(valid, score, -jnp.inf))
    _, sel = lax.top_k(score, n_sel)
    nq = S // Q_BLOCK
    ks_blocks = rms_norm(ks, kn[1]).reshape(B, n_slc, SLC_LEN, Dh)
    vs_blocks = vs.reshape(B, n_slc, SLC_LEN, Dh)
    kw_pad = jnp.pad(rms_norm(kw, kn[2]), ((0, 0), (WINDOW, 0), (0, 0)))
    vw_pad = jnp.pad(vw, ((0, 0), (WINDOW, 0), (0, 0)))
    band = WINDOW + Q_BLOCK
    qi = jnp.arange(Q_BLOCK)
    ki = jnp.arange(band)
    dist_w = qi[:, None] + WINDOW - ki[None, :]
    bias_w = rel_bias[t5_bucket(dist_w)].transpose(2, 0, 1)
    in_window = (dist_w >= 0) & (dist_w < WINDOW)
    bidx = jnp.arange(B)[:, None, None]

    def block(args):
        q_blk, sel_blk, t0 = args
        t_q = t0 + qi
        kg = ks_blocks[bidx, sel_blk]
        vg = vs_blocks[bidx, sel_blk]
        kpos = (sel_blk[..., None] * SLC_LEN + jnp.arange(SLC_LEN)).reshape(B, Q_BLOCK, -1)
        dist_s = t_q[None, :, None] - kpos
        bias_s = rel_bias[t5_bucket(dist_s)].transpose(0, 3, 1, 2)
        logits_s = jnp.einsum('bqhd,bqnkd->bhqnk', q_blk, kg).reshape(B, H, Q_BLOCK, -1).astype(f32) * scale + bias_s
        p_s = masked_softmax(logits_s, (dist_s >= 0)[:, None])
        o_s = jnp.einsum('bhqnk,bqnkd->bqhd', p_s.reshape(B, H, Q_BLOCK, n_sel, SLC_LEN).astype(vg.dtype), vg)
        kb = lax.dynamic_slice_in_dim(kw_pad, t0, band, axis=1)
        vb = lax.dynamic_slice_in_dim(vw_pad, t0, band, axis=1)
        mask_w = in_window & (t0 - WINDOW + ki >= 0)[None, :]
        logits_w = jnp.einsum('bqhd,bkd->bhqk', q_blk, kb).astype(f32) * scale + bias_w
        p_w = masked_softmax(logits_w, mask_w)
        o_w = jnp.einsum('bhqk,bkd->bqhd', p_w.astype(vb.dtype), vb)
        return o_s, o_w

    q_blocks = q.reshape(B, nq, Q_BLOCK, H, Dh).swapaxes(0, 1)
    sel_blocks = sel.reshape(B, nq, Q_BLOCK, n_sel).swapaxes(0, 1)
    o_slc, o_win = lax.map(block, (q_blocks, sel_blocks, jnp.arange(nq) * Q_BLOCK))
    o_slc = o_slc.swapaxes(0, 1).reshape(B, S, H, Dh)
    o_win = o_win.swapaxes(0, 1).reshape(B, S, H, Dh)
    g = jax.nn.sigmoid(gate_logits.astype(f32)).reshape(B, S, H, 3).astype(q.dtype)
    out = g[..., 0:1] * o_cmp + g[..., 1:2] * o_slc + g[..., 2:3] * o_win
    return out.reshape(B, S, H * Dh)

def causal_block_attention(q, k, v, scale):
    B, S, H, _ = q.shape
    nq = S // Q_BLOCK
    kpos = jnp.arange(S)

    def one(args):
        q_blk, t0 = args
        logits = jnp.einsum('bqhd,bkhd->bhqk', q_blk, k).astype(f32) * scale
        mask = kpos[None, :] <= (t0 + jnp.arange(Q_BLOCK))[:, None]
        p = masked_softmax(logits, mask)
        return jnp.einsum('bhqk,bkhd->bqhd', p.astype(v.dtype), v)

    qb = q.reshape(B, nq, Q_BLOCK, H, -1).swapaxes(0, 1)
    out = lax.map(one, (qb, jnp.arange(nq) * Q_BLOCK))
    return out.swapaxes(0, 1).reshape(B, S, H, -1)

def mla_mixer(c_q, c_kv, k_rope, qa_norm, kv_norm, wq_b, wkv_b, qn, kn, cos, sin):
    B, S, _ = c_q.shape
    q = (rms_norm(c_q, qa_norm) @ wq_b).reshape(B, S, MLA_HEADS, NOPE_DIM + ROPE_DIM)
    q = jnp.concatenate([q[..., :NOPE_DIM], apply_rope(q[..., NOPE_DIM:], cos, sin)], axis=-1)
    kv = (rms_norm(c_kv, kv_norm) @ wkv_b).reshape(B, S, MLA_HEADS, NOPE_DIM + V_DIM)
    k_nope, v = kv[..., :NOPE_DIM], kv[..., NOPE_DIM:]
    k_r = apply_rope(k_rope[:, :, None, :], cos, sin)
    k = jnp.concatenate([k_nope, jnp.broadcast_to(k_r, (B, S, MLA_HEADS, ROPE_DIM))], axis=-1)
    q = rms_norm(q, qn)
    k = rms_norm(k, kn)
    o = causal_block_attention(q, k, v, (NOPE_DIM + ROPE_DIM) ** -0.5)
    return o.reshape(B, S, MLA_HEADS * V_DIM)

def stick_breaking_mixer(q, k, v):
    B, S, H, Dh = q.shape
    scale = Dh ** -0.5
    nq = S // Q_BLOCK
    kpos = jnp.arange(S)

    def one(args):
        q_blk, t0 = args
        z = jnp.einsum('bqhd,bkhd->bhqk', q_blk, k).astype(f32) * scale
        strict = kpos[None, :] < (t0 + jnp.arange(Q_BLOCK))[:, None]
        log_1m = jnp.where(strict, jax.nn.log_sigmoid(-z), 0.0)
        rem = lax.cumsum(log_1m, axis=3, reverse=True) - log_1m
        a = jnp.where(strict, jnp.exp(jax.nn.log_sigmoid(z) + rem), 0.0)
        return jnp.einsum('bhqk,bkhd->bqhd', a.astype(v.dtype), v)

    qb = q.reshape(B, nq, Q_BLOCK, H, Dh).swapaxes(0, 1)
    out = lax.map(one, (qb, jnp.arange(nq) * Q_BLOCK))
    return out.swapaxes(0, 1).reshape(B, S, H * Dh)

def first_inputs(seed: int = 0) -> dict:
    key = jax.random.key(seed)
    ks = jax.random.split(key, 24)
    L = DEPTH
    nrm = lambda k, shape, s: jax.random.normal(k, shape, f32) * s
    gain = lambda k, shape: 1.0 + 0.02 * jax.random.normal(k, shape, f32)
    qk_dim = NOPE_DIM + ROPE_DIM
    return {
        "x": jax.random.normal(ks[0], (BATCH, SEQ, D_MODEL), f32),
        "rel_bias": nrm(ks[1], (N_BUCKETS, NSA_HEADS), 0.5),
        "norm1_w": gain(ks[2], (L, D_MODEL)),
        "w_in": nrm(ks[3], (L, D_MODEL, IN_COLS), D_MODEL ** -0.5),
        "conv_w": nrm(ks[4], (L, CONV_WIDTH, CONV_CH), CONV_WIDTH ** -0.5),
        "conv_b": nrm(ks[5], (L, CONV_CH), 0.02),
        "nsa_q_norm": gain(ks[6], (L, HEAD_DIM)),
        "nsa_k_norm": gain(ks[7], (L, 3, HEAD_DIM)),
        "cmp_pos": nrm(ks[8], (L, 2, CMP_LEN, HEAD_DIM), 0.1),
        "cmp_w1": nrm(ks[9], (L, 2, CMP_LEN * HEAD_DIM, CMP_HIDDEN), (CMP_LEN * HEAD_DIM) ** -0.5),
        "cmp_w2": nrm(ks[10], (L, 2, CMP_HIDDEN, HEAD_DIM), CMP_HIDDEN ** -0.5),
        "mla_q_a_norm": gain(ks[11], (L, Q_LORA)),
        "mla_kv_norm": gain(ks[12], (L, KV_LORA)),
        "mla_wq_b": nrm(ks[13], (L, Q_LORA, MLA_HEADS * qk_dim), Q_LORA ** -0.5),
        "mla_wkv_b": nrm(ks[14], (L, KV_LORA, MLA_HEADS * (NOPE_DIM + V_DIM)), KV_LORA ** -0.5),
        "mla_q_norm": gain(ks[15], (L, qk_dim)),
        "mla_k_norm": gain(ks[16], (L, qk_dim)),
        "out_norm_w": gain(ks[17], (L, D_MODEL)),
        "w_out": nrm(ks[18], (L, D_MODEL, D_MODEL), D_MODEL ** -0.5),
        "norm2_w": gain(ks[19], (L, D_MODEL)),
        "ffn_w1": nrm(ks[20], (L, D_MODEL, D_FF), D_MODEL ** -0.5),
        "ffn_w2": nrm(ks[21], (L, D_FF, D_MODEL), D_FF ** -0.5),
    }

def first_block(x, rel_bias, norm1_w, w_in, conv_w, conv_b, nsa_q_norm, nsa_k_norm, cmp_pos, cmp_w1, cmp_w2,
              mla_q_a_norm, mla_kv_norm, mla_wq_b, mla_wkv_b, mla_q_norm, mla_k_norm, out_norm_w, w_out,
              norm2_w, ffn_w1, ffn_w2):
    B, S, D = x.shape
    cos, sin = rope_tables(S)
    for l in range(DEPTH):
        h = rms_norm(x, norm1_w[l])
        cols = split_cols(h @ w_in[l], IN_SIZES)
        a_b, a_c, a_u = cols[0:3]
        n_q, n_kc, n_vc, n_ks, n_vs, n_kw, n_vw, n_g = cols[3:11]
        m_cq, m_ckv, m_kr = cols[11:14]
        s_q, s_k, s_v = cols[14:17]
        y_a = short_conv_mixer(a_b, a_c, a_u, conv_w[l], conv_b[l])
        y_b = nsa_mixer(n_q.reshape(B, S, NSA_HEADS, HEAD_DIM), n_kc, n_vc, n_ks, n_vs, n_kw, n_vw, n_g,
                        nsa_q_norm[l], nsa_k_norm[l], cmp_pos[l], cmp_w1[l], cmp_w2[l], rel_bias)
        y_c = mla_mixer(m_cq, m_ckv, m_kr, mla_q_a_norm[l], mla_kv_norm[l], mla_wq_b[l], mla_wkv_b[l],
                        mla_q_norm[l], mla_k_norm[l], cos, sin)
        y_d = stick_breaking_mixer(s_q.reshape(B, S, SB_HEADS, HEAD_DIM), s_k.reshape(B, S, SB_HEADS, HEAD_DIM),
                                   s_v.reshape(B, S, SB_HEADS, HEAD_DIM))
        y = jnp.concatenate([y_a, y_b, y_c, y_d], axis=-1).reshape(B, S, N_GROUPS, GROUP_WIDTH)
        y = rms_norm(y, out_norm_w[l].reshape(N_GROUPS, GROUP_WIDTH)).reshape(B, S, D)
        x = x + y @ w_out[l]
        h2 = rms_norm(x, norm2_w[l])
        x = x + jnp.square(jax.nn.relu(h2 @ ffn_w1[l])) @ ffn_w2[l]
    return x


RET_HEADS = 4
RET_DK = 128
RET_DV = 256
RET_CHUNK = 128
GLA_HEADS = 4
GLA_DK = 128
GLA_DV = 256
GLA_RANK = 16
GLA_TAU = 16.0
GLA_LOG_GATE_MIN = -1.0
GLA_CHUNK = 64
SWA_Q_HEADS = 16
SWA_KV_HEADS = 4
SWA_HEAD_DIM = 64
SWA_WINDOW = 128
N_BRANCH = 3
BRANCH_WIDTH = RET_HEADS * RET_DV
D_FF_2 = -(-8 * D_MODEL // (3 * 256)) * 256
NORM_EPS = 1e-6
GN_EPS = 1e-5

IN_SPLITS = (
    RET_HEADS * RET_DK, RET_HEADS * RET_DK, RET_HEADS * RET_DV, RET_HEADS * RET_DV,
    GLA_HEADS * GLA_DK, GLA_HEADS * GLA_DK, GLA_HEADS * GLA_DV, GLA_HEADS * GLA_DV, GLA_RANK,
    SWA_Q_HEADS * SWA_HEAD_DIM, SWA_KV_HEADS * SWA_HEAD_DIM, SWA_KV_HEADS * SWA_HEAD_DIM,
    N_BRANCH * D_MODEL,
)
D_IN = sum(IN_SPLITS)


def _split_points():
    return [int(o) for o in np.cumsum(IN_SPLITS)[:-1]]

def rmsnorm(x, w):
    xf = x.astype(jnp.float32)
    y = xf * lax.rsqrt(jnp.mean(xf * xf, axis=-1, keepdims=True) + NORM_EPS)
    return (y * w.astype(jnp.float32)).astype(x.dtype)

def head_groupnorm(o, w, b):
    B, S, H, dv = o.shape
    of = o.astype(jnp.float32)
    mu = jnp.mean(of, axis=-1, keepdims=True)
    var = jnp.mean(jnp.square(of - mu), axis=-1, keepdims=True)
    y = ((of - mu) * lax.rsqrt(var + GN_EPS)).reshape(B, S, H * dv)
    return y * w.astype(jnp.float32) + b.astype(jnp.float32)

def head_rmsnorm(o, w):
    B, S, H, dv = o.shape
    of = o.astype(jnp.float32)
    y = of * lax.rsqrt(jnp.mean(of * of, axis=-1, keepdims=True) + NORM_EPS)
    return y.reshape(B, S, H * dv) * w.astype(jnp.float32)

def retention(q, k, v):
    B, S, H, dk = q.shape
    dv = v.shape[-1]
    C = RET_CHUNK
    N = S // C
    log_g = jnp.log1p(-jnp.exp2(-5.0 - jnp.arange(H, dtype=jnp.float32)))
    q = (q * dk ** -0.5).reshape(B, N, C, H, dk)
    k = k.reshape(B, N, C, H, dk)
    v = v.reshape(B, N, C, H, dv)
    pos = jnp.arange(C, dtype=jnp.float32)
    rel = pos[:, None] - pos[None, :]
    decay = jnp.exp(jnp.where((rel >= 0)[None], rel[None] * log_g[:, None, None], -jnp.inf))
    scores = jnp.einsum('bnihd,bnjhd->bnhij', q, k) * decay
    intra = jnp.einsum('bnhij,bnjhe->bnihe', scores, v)
    zeta = jnp.exp((C - 1 - pos)[None, :] * log_g[:, None])
    kv = jnp.einsum('bnjhd,bnjhe,hj->nbhde', k, v, zeta)
    gamma_c = jnp.exp(C * log_g)[None, :, None, None]

    def step(R, kv_n):
        return gamma_c * R + kv_n, R

    _, states = lax.scan(step, jnp.zeros(kv.shape[1:], kv.dtype), kv)
    xi = jnp.exp((pos + 1.0)[:, None] * log_g[None, :])
    inter = jnp.einsum('bnihd,nbhde->bnihe', q * xi[:, :, None], states)
    return (intra + inter).reshape(B, S, H, dv)

def gla(q, k, v, log_a):
    B, S, H, dk = q.shape
    dv = v.shape[-1]
    C = GLA_CHUNK
    N = S // C
    q = (q * dk ** -0.5).reshape(B, N, C, H, dk)
    k = k.reshape(B, N, C, H, dk)
    v = v.reshape(B, N, C, H, dv)
    b = jnp.cumsum(log_a.reshape(B, N, C, H, dk), axis=2)
    b_last = b[:, :, -1:]
    q_dec = q * jnp.exp(b)
    k_inv = k * jnp.exp(-b)
    causal = jnp.tril(jnp.ones((C, C), dtype=bool))
    A = jnp.where(causal, jnp.einsum('bnihd,bnjhd->bnhij', q_dec, k_inv), 0.0)
    intra = jnp.einsum('bnhij,bnjhe->bnihe', A, v)
    kv = jnp.einsum('bnjhd,bnjhe->nbhde', k * jnp.exp(b_last - b), v)
    chunk_decay = jnp.moveaxis(jnp.exp(b_last[:, :, 0]), 1, 0)

    def step(St, inp):
        kv_n, a_n = inp
        return a_n[..., None] * St + kv_n, St

    _, states = lax.scan(step, jnp.zeros(kv.shape[1:], kv.dtype), (kv, chunk_decay))
    inter = jnp.einsum('bnihd,nbhde->bnihe', q_dec, states)
    return (intra + inter).reshape(B, S, H, dv)

def swa_sinks(q, k, v, sinks):
    B, S, Hq, dh = q.shape
    Hkv = k.shape[2]
    G = Hq // Hkv
    W = SWA_WINDOW
    N = S // W
    slopes = jnp.exp2(-8.0 * jnp.arange(1, Hq + 1, dtype=jnp.float32) / Hq).reshape(Hkv, G)
    qb = q.reshape(B, N, W, Hkv, G, dh)
    kb = k.reshape(B, N, W, Hkv, dh)
    vb = v.reshape(B, N, W, Hkv, dh)

    def with_prev(t):
        prev = jnp.pad(t[:, :-1], ((0, 0), (1, 0), (0, 0), (0, 0), (0, 0)))
        return jnp.concatenate([prev, t], axis=2)

    kk, vv = with_prev(kb), with_prev(vb)
    scores = jnp.einsum('bnqhgd,bnkhd->bnhgqk', qb, kk).astype(jnp.float32) * dh ** -0.5
    qpos = W + jnp.arange(W)
    kpos = jnp.arange(2 * W)
    dist = qpos[:, None] - kpos[None, :]
    blk = jnp.arange(N)
    valid = ((dist >= 0) & (dist < W))[None] & ((blk[:, None, None] > 0) | (kpos[None, None, :] >= W))
    logits = scores - slopes[:, :, None, None] * dist.astype(jnp.float32)
    logits = jnp.where(valid[None, :, None, None], logits, -jnp.inf)
    sink = sinks.astype(jnp.float32).reshape(Hkv, G)[:, :, None, None]
    m = jnp.maximum(jnp.max(logits, axis=-1, keepdims=True), sink)
    p = jnp.exp(logits - m)
    probs = p / (jnp.sum(p, axis=-1, keepdims=True) + jnp.exp(sink - m))
    out = jnp.einsum('bnhgqk,bnkhd->bnqhgd', probs.astype(v.dtype), vv)
    return out.reshape(B, S, Hq * dh)

def second_inputs(seed: int = 0) -> dict:
    key = jax.random.key(seed)
    ks = jax.random.split(key, 17)
    f32 = jnp.float32

    def nrm(k, shape, scale):
        return jax.random.normal(k, shape, f32) * scale

    def gain(k, n):
        return 1.0 + nrm(k, (DEPTH, n), 0.05)

    return {
        'x': nrm(ks[0], (BATCH, SEQ, D_MODEL), 1.0),
        'norm_mix_pre': gain(ks[1], D_MODEL),
        'norm_mix_post': gain(ks[2], D_MODEL),
        'w_in': nrm(ks[3], (DEPTH, D_MODEL, D_IN), D_MODEL ** -0.5),
        'ret_norm_w': gain(ks[4], RET_HEADS * RET_DV),
        'ret_norm_b': nrm(ks[5], (DEPTH, RET_HEADS * RET_DV), 0.02),
        'gla_w_alpha2': nrm(ks[6], (DEPTH, GLA_RANK, GLA_HEADS * GLA_DK), GLA_RANK ** -0.5),
        'gla_b_alpha': nrm(ks[7], (DEPTH, GLA_HEADS * GLA_DK), 0.1),
        'gla_norm_w': gain(ks[8], GLA_HEADS * GLA_DV),
        'attn_sinks': nrm(ks[9], (DEPTH, SWA_Q_HEADS), 0.5),
        'w_branch': nrm(ks[10], (DEPTH, N_BRANCH, BRANCH_WIDTH, D_MODEL), BRANCH_WIDTH ** -0.5),
        'w_out': nrm(ks[11], (DEPTH, D_MODEL, D_MODEL), D_MODEL ** -0.5),
        'norm_ffn_pre': gain(ks[12], D_MODEL),
        'norm_ffn_post': gain(ks[13], D_MODEL),
        'ffn_w_gate': nrm(ks[14], (DEPTH, D_MODEL, D_FF_2), D_MODEL ** -0.5),
        'ffn_w_up': nrm(ks[15], (DEPTH, D_MODEL, D_FF_2), D_MODEL ** -0.5),
        'ffn_w_down': nrm(ks[16], (DEPTH, D_FF_2, D_MODEL), D_FF_2 ** -0.5),
    }

def second_block(x, norm_mix_pre, norm_mix_post, w_in, ret_norm_w, ret_norm_b, gla_w_alpha2,
              gla_b_alpha, gla_norm_w, attn_sinks, w_branch, w_out, norm_ffn_pre, norm_ffn_post,
              ffn_w_gate, ffn_w_up, ffn_w_down):
    B, S, _ = x.shape
    split_points = _split_points()
    for l in range(DEPTH):
        h = rmsnorm(x, norm_mix_pre[l])
        proj = h @ w_in[l]
        (rq, rk, rv, rg, gq, gk, gv, gg, ga, sq, sk, sv, gate_logits) = jnp.split(proj, split_points, axis=-1)

        o_ret = retention(rq.reshape(B, S, RET_HEADS, RET_DK), rk.reshape(B, S, RET_HEADS, RET_DK),
                          rv.reshape(B, S, RET_HEADS, RET_DV))
        o_ret = (head_groupnorm(o_ret, ret_norm_w[l], ret_norm_b[l]) * jax.nn.silu(rg)).astype(x.dtype)

        z = (ga @ gla_w_alpha2[l] + gla_b_alpha[l]).astype(jnp.float32)
        log_a = jnp.maximum(jax.nn.log_sigmoid(z) / GLA_TAU, GLA_LOG_GATE_MIN)
        o_gla = gla(gq.reshape(B, S, GLA_HEADS, GLA_DK), gk.reshape(B, S, GLA_HEADS, GLA_DK),
                    gv.reshape(B, S, GLA_HEADS, GLA_DV), log_a.reshape(B, S, GLA_HEADS, GLA_DK))
        o_gla = (head_rmsnorm(o_gla, gla_norm_w[l]) * jax.nn.silu(gg)).astype(x.dtype)

        o_swa = swa_sinks(sq.reshape(B, S, SWA_Q_HEADS, SWA_HEAD_DIM),
                          sk.reshape(B, S, SWA_KV_HEADS, SWA_HEAD_DIM),
                          sv.reshape(B, S, SWA_KV_HEADS, SWA_HEAD_DIM), attn_sinks[l]).astype(x.dtype)

        branches = jnp.stack([o_ret, o_gla, o_swa], axis=2)
        projected = jnp.einsum('bsnc,ncd->bsnd', branches, w_branch[l])
        gates = jax.nn.sigmoid(gate_logits.reshape(B, S, N_BRANCH, D_MODEL))
        merged = jnp.sum(gates * projected, axis=2)
        x = x + rmsnorm(merged @ w_out[l], norm_mix_post[l])

        h = rmsnorm(x, norm_ffn_pre[l])
        f = (jax.nn.silu(h @ ffn_w_gate[l]) * (h @ ffn_w_up[l])) @ ffn_w_down[l]
        x = x + rmsnorm(f, norm_ffn_post[l])
    return x


def setup_inputs(seed=0):
    out = dict(first_inputs(seed))
    for name, value in second_inputs(seed + 1).items():
        if name != "x":
            out[name + "_2"] = value
    return out


def reference(
    x, rel_bias, norm1_w, w_in, conv_w, conv_b, nsa_q_norm, nsa_k_norm, cmp_pos, cmp_w1, cmp_w2,
    mla_q_a_norm, mla_kv_norm, mla_wq_b, mla_wkv_b, mla_q_norm, mla_k_norm, out_norm_w, w_out,
    norm2_w, ffn_w1, ffn_w2, norm_mix_pre_2, norm_mix_post_2, w_in_2, ret_norm_w_2,
    ret_norm_b_2, gla_w_alpha2_2, gla_b_alpha_2, gla_norm_w_2, attn_sinks_2, w_branch_2,
    w_out_2, norm_ffn_pre_2, norm_ffn_post_2, ffn_w_gate_2, ffn_w_up_2, ffn_w_down_2,
):
    x = first_block(
        x, rel_bias, norm1_w, w_in, conv_w, conv_b, nsa_q_norm, nsa_k_norm, cmp_pos, cmp_w1,
        cmp_w2, mla_q_a_norm, mla_kv_norm, mla_wq_b, mla_wkv_b, mla_q_norm, mla_k_norm,
        out_norm_w, w_out, norm2_w, ffn_w1, ffn_w2,
    )
    return second_block(
        x, norm_mix_pre_2, norm_mix_post_2, w_in_2, ret_norm_w_2, ret_norm_b_2, gla_w_alpha2_2,
        gla_b_alpha_2, gla_norm_w_2, attn_sinks_2, w_branch_2, w_out_2, norm_ffn_pre_2,
        norm_ffn_post_2, ffn_w_gate_2, ffn_w_up_2, ffn_w_down_2,
    )


_drawn_inputs = setup_inputs


def setup_inputs(seed=0):
    import zlib

    import numpy as np

    out = dict(_drawn_inputs(seed))
    spreads = {}
    factors = {'conv_b': 3.803,
     'nsa_q_norm': 7.627,
     'nsa_k_norm': 7.966,
     'mla_q_a_norm': 5.567,
     'mla_kv_norm': 3.912,
     'mla_q_norm': 6.123,
     'mla_k_norm': 5.59,
     'norm2_w': 2.71,
     'ret_norm_w_2': 28.0,
     'ret_norm_b_2': 64.0,
     'gla_b_alpha_2': 13.322,
     'gla_norm_w_2': 27.656,
     'attn_sinks_2': 45.512,
     'rel_bias': 3.444,
     'out_norm_w': 3.502,
     'norm_mix_pre_2': 4.314,
     'norm_mix_post_2': 8.0,
     'norm_ffn_pre_2': 7.184,
     'norm_ffn_post_2': 8.0}
    for name, (base, spread) in spreads.items():
        noise = np.random.default_rng([zlib.crc32(name.encode()), seed]).standard_normal(out[name].shape)
        drawn = base * np.exp(spread * noise) if base else spread * noise
        out[name] = __import__('jax').numpy.asarray(drawn.astype(out[name].dtype))
    for name, factor in factors.items():
        out[name] = (out[name] * factor).astype(out[name].dtype)
    return out
```

```python
from contextlib import ExitStack

import numpy as np

import concourse.bass as bass
from concourse import mybir

ALU = mybir.AluOpType
ACT = mybir.ActivationFunctionType
F32 = mybir.dt.float32
F32R = mybir.dt.float32r
AX = mybir.AxisListType.X

P = 128
T = 512
NT = T // P
D = 1024
KD = D // P
EPS = 1e-6
GN_EPS = 1e-5
NEG = -1.0e30
CMP_LEN, CMP_STRIDE = 32, 16
N_CMP = (T - CMP_LEN) // CMP_STRIDE + 1
NH = 4
HD = 64
N_BUCKETS = 32
QKD = 96
F1 = 4 * D // P
HALF1 = F1 // 2
F2 = 2816 // P
HALF2 = F2 // 2
GC = 64
NGC = T // GC
RAW = 3
SPL = 3

PCOL = {}


def _columns():
    at = 0
    for name, n in (("norm1", 8), ("conv_w", 6), ("conv_b", 2), ("nsa_q", 1), ("nsa_k", 3), ("mla_qa", 2),
                    ("mla_kv", 1), ("mla_q", 1), ("mla_k", 1), ("out_norm", 8), ("norm2", 8), ("pos", 32),
                    ("pre", 8), ("post", 8), ("ret_w", 8), ("ret_b", 8), ("b_alpha", 4), ("gla_w", 8),
                    ("fpre", 8), ("fpost", 8), ("sinks", 16)):
        PCOL[name] = at
        at += n
    return at


NPCOL = _columns()
SWA_HEAD = [[(2 * (c // 4) + hf) * 4 + c % 4 for hf in range(2)] for c in range(8)]


def plan():
    order, slots = [], {}

    def lin(name, kind, n_slots, *args):
        slots[name] = (sum(n for _, n in slots.values()), n_slots)
        order.append((kind, name) + args)

    def fm(name, src="h"):
        lin(name, "fm", 1, src)

    def attention(units):
        n = len(units)
        for i in range(n + 2):
            if i < n:
                order.append(("att_scores", units[i]))
            if 1 <= i <= n:
                order.append(("att_turn", units[i - 1]))
            if i >= 2:
                order.append(("att_pv", units[i - 2]))

    order.append(("bias_tables", 0))
    order.append(("norm", "n1"))
    order.append(("apply_h", "n1", "norm1"))
    for name in ("ks", "kw", "kc", "vc", "nq0", "nq1"):
        fm(name)
    lin("v1", "tm", 4, 396)
    for name in ("ks", "kw", "nq0", "nq1"):
        order.append(("norm", name))
        order.append(("nsa_apply", name))
    for kv in range(2):
        lin(("cmp", kv), "cmp_up", 4, kv)
    order.append(("cmp_down", 0))
    order.append(("norm", "kcmp"))
    order.append(("cmp_apply", 0))
    order.append(("cmp_softmax", 0))
    units = []
    for pair in range(2):
        for qt in range(NT):
            for hf in range(2):
                for kind in ("slc", "win"):
                    units.append((kind, 2 * pair + hf, qt))
    attention(units)
    for name in ("cq0", "cq1", "ckv", "kr", "krs"):
        fm(name)
    for name in ("cq", "ckv"):
        order.append(("norm", name))
    order.append(("mla_lora", 0))
    order.append(("mla_v", 0))
    order.append(("mla_rope_k", 0))
    for h in range(NH):
        order.append(("mla_qk", h))
    attention([("mla", h, qt) for pair in range(2) for qt in range(NT) for h in (2 * pair, 2 * pair + 1)])
    for name in ("sq0", "sq1", "sk0", "sk1"):
        fm(name)
    for h in range(NH):
        for kt in reversed(range(NT)):
            order.append(("sb_scores", h, kt))
            order.append(("sb_exp", h, kt))
        order.append(("sb_pv", h))
    for c in range(2):
        for name in ("ac", "au", "ab"):
            fm((name, c))
        order.append(("conv", c))
    for g in range(4):
        order.append(("norm", ("y", g)))
    order.append(("apply_y", "y"))
    for c in range(KD):
        fm(("wout", c))
    order.append(("norm", "n2"))
    order.append(("apply_h", "n2", "norm2"))
    for half in range(2):
        for c in range(HALF1):
            fm(("up1", half, c))
        lin(("down1", half), "down", KD * HALF1 // 8, HALF1)
    order.append(("norm", "pre"))
    order.append(("apply_h", "pre", "pre"))
    for h in range(4):
        if h % 2 == 0:
            lin(("rv", h // 2), "tm", 4, 512)
        fm(("rq", h))
        fm(("rk", h))
        for e in range(2):
            fm(("rg", h, e))
        for jt in range(NT):
            order.append(("ret_scores", h, jt))
        order.append(("ret_pv", h))
        order.append(("ret_mean", h))
        order.append(("norm", ("ret", h)))
        order.append(("ret_out", h))

    def branch(b):
        for m in range(KD):
            fm(("gate", b, m))
            fm(("br", b, m), "o")

    branch(0)
    fm("ga")
    for h in range(4):
        if h % 2 == 0:
            lin(("gv", h // 2), "tm", 4, 512)
        fm(("gq", h))
        fm(("gk", h))
        order.append(("gla_decay", h))
        for e in range(2):
            fm(("gg", h, e))
        order.append(("gla_chunks", h))
        order.append(("norm", ("gla", h)))
        order.append(("gla_out", h))
    branch(1)
    for c in range(8):
        fm(("wq", c))
    for c in range(2):
        fm(("wk", c))
    lin("wv", "tm", 2, 256)
    attention([("swa", c, hf, qt) for c in range(8) for qt in range(NT) for hf in range(2)])
    branch(2)
    order.append(("merge", "merge"))
    for c in range(KD):
        fm(("wout2", c))
    order.append(("norm", "post"))
    order.append(("residual", "post"))
    order.append(("norm", "fpre"))
    order.append(("apply_h", "fpre", "fpre"))
    for half in range(2):
        for c in range(HALF2):
            fm(("fg", half, c))
            fm(("fu", half, c))
        lin(("down2", half), "down", KD * HALF2 // 8, HALF2)
    order.append(("norm", "fpost"))
    order.append(("residual", "fpost"))
    order.append(("store", 0))
    return order, slots


ORDER, SLOTS = plan()
N_SLOTS = sum(n for _, n in SLOTS.values())

SEMAPHORES = """x_in const_in wqb_in misc_in late_in bias_out0 bias_out1 bias_in y_out
w_hi w_lo slot_used v_chain s_chain sq_s sq_v rstd rstd_used ms_lo
h_ready bias_v bcast_v gate_v nsa_v cmpx cmp_s cmp_v att_l att_n att_exp att_p att_tr att_done
lora mla_k mla_q mla_rot sb_sp sb_exp sb_a sb_pe conv_v y_ready hid_s hid x_ready ret_a ret_d ret_done sil
o_ready gla_v gla_s gla_kd gla_st gla_a gla_done prod gate_s merged merged_hl q_s swa_s ft lo_t table""".split()


class Counts:

    def __init__(self, known):
        self.known = known
        self.at = {}
        self.n = {}
        self.sem = {}

    def did(self, name, *key, by=1):
        self.n[name] = self.n.get(name, 0) + by
        assert (name, key) not in self.at, (name, key)
        self.at[(name, key)] = self.n[name]
        return self.sem[name], by

    def after(self, name, *key):
        v = self.at.get((name, key)) or self.known.get((name, key))
        assert v or not self.known, (name, key)
        return self.sem[name], v or 1


def build(nc, a, known):
    ctx = ExitStack()
    with ctx:
        return _program(ctx, nc, a, known)


def _program(ctx, nc, a, known):
    C = Counts(known)
    did, after = C.did, C.after
    for name in SEMAPHORES:
        C.sem[name] = ctx.enter_context(nc.semaphore(name))
    for s in range(RAW):
        C.sem[f"w_landed{s}"] = ctx.enter_context(nc.semaphore(f"w_landed{s}"))
    for b in range(8):
        for what in ("bank_full", "bank_free"):
            C.sem[f"{what}{b}"] = ctx.enter_context(nc.semaphore(f"{what}{b}"))

    def sb(name, shape, dt=F32):
        return ctx.enter_context(nc.sbuf_tensor(name, shape, dt))

    bank = [ctx.enter_context(nc.psum_tensor(f"bank{b}", [P, 512], F32)) for b in range(8)]

    x_sb = sb("x_sb", [P, KD, T])
    h_hi, h_lo = sb("h_hi", [P, KD, T], F32R), sb("h_lo", [P, KD, T], F32R)
    w_raw = sb("w_raw", [P, RAW, 1024])
    w_hi, w_lo = sb("w_hi_t", [P, SPL, 1024], F32R), sb("w_lo_t", [P, SPL, 1024], F32R)
    par = sb("par", [P, NPCOL])
    ones = sb("ones", [P, P])
    ones64 = sb("ones64", [P, P])
    ident = sb("ident", [P, P])
    causal = sb("causal", [P, T])
    sq = sb("sq", [P, 2, T])
    sq_sum = sb("sq_sum", [P, T])
    rstd_t = sb("rstd_t", [P, 3, T])
    tmp = sb("tmp", [P, 2, T])
    att_l = sb("att_l_t", [P, 3, T])
    att_pt = sb("att_pt", [P, 2, T])
    small = sb("small", [P, 4, 8])
    epst = sb("epst", [P, 8])

    area = ExitStack()

    def sa(name, shape, dt=F32):
        return area.enter_context(nc.sbuf_tensor(name, shape, dt))

    y = sa("y", [P, KD, T])
    v1 = sa("v1", [P, NT, 396])
    gates = sa("gates", [P, NT, 12])
    rb = sa("rb", [N_BUCKETS + 1, NH])
    rb_b = sa("rb_b", [N_BUCKETS + 1, NH, P])
    w2k, w2v = sa("w2k", [P, 2, P]), sa("w2v", [P, 2, HD])
    wqb = sa("wqb", [P, 2, 2, NH, QKD])
    wkb = sa("wkb", [P, NH, QKD])
    wvb = sa("wvb", [P, NH * HD])
    rope_c, rope_s = sa("rope_c", [QKD, T]), sa("rope_s", [QKD, T])
    sbm = sa("sbm", [P, 4, P])
    part = ExitStack()

    def sp_(name, shape, dt=F32):
        return part.enter_context(nc.sbuf_tensor(name, shape, dt))

    tab = sp_("tab", [P, 2, 1024])
    part.close()
    cmp_x = [sp_("cmp_xh", [P, 2, 16, 32], F32R), sp_("cmp_xl", [P, 2, 16, 32], F32R)]
    part.close()
    cmp_pt = sp_("cmp_pt_t", [32, NT, NH, P])
    onehot = sp_("onehot", [N_BUCKETS + 1, 640 + 1024])
    cb_t = sp_("cb_t", [N_CMP, NH, T])
    kv_raw = sp_("kv_raw", [P, 2, T])
    part.close()
    sb_a = sp_("sb_a_t", [P, 2, 1280])
    conv_t = sp_("conv_t", [P, 2, 2 + T])
    part.close()
    mk, mq = sp_("mk", [QKD, NH, T]), sp_("mq", [QKD, NH, T])
    mv = sp_("mv", [P, NT, NH * HD])
    cq = sp_("cq", [P, 2, T])
    ckv = sp_("ckv", [P, T])
    kr = sp_("kr", [QKD, 2, T])
    nsa = ExitStack()

    def sn(name, shape, dt=F32):
        return nsa.enter_context(nc.sbuf_tensor(name, shape, dt))

    toep = sn("toep", [P, NH, T])
    cmp_bias = sn("cmp_bias_t", [P, NT, NH, N_CMP])
    ks_d, kw_d = sn("ks_d", [P, T]), sn("kw_d", [P, T])
    nq = sn("nq", [P, 2, T])
    cmp_h = sn("cmp_h", [P, 4, 32])
    cmp_k = sn("cmp_k_t", [P, 2, 32])
    cmp_vt = sn("cmp_vt_t", [32, HD])
    cmp_p = sn("cmp_p", [P, NT, NH, N_CMP])
    cmp_s = sn("cmp_s_t", [P, 4, NT, NH])
    nsa.close()
    s_qk = sn("s_qk", [P, 4, T])
    sb_e = sn("sb_e", [P, 2, T])
    sb_sp = sn("sb_sp_t", [P, 2, 1280])
    nsa.close()
    part.close()
    area.close()

    hid1 = [area.enter_context(nc.sbuf_tensor(n, [P, HALF1, T], F32R)) for n in ("hid1_hi", "hid1_lo")]
    r1 = sa("r1", [P, 2, T])
    area.close()

    merged = sa("merged_t", [P, KD, T])
    sig = sa("sig", [P, 2, T])
    mixers = ExitStack()
    o_hl = [mixers.enter_context(nc.sbuf_tensor(n, [P, KD, T], F32R)) for n in ("o_hi", "o_lo")]
    inner = ExitStack()

    def si(name, shape, dt=F32):
        return inner.enter_context(nc.sbuf_tensor(name, shape, dt))

    qf, kf = si("qf", [P, 2, T]), si("kf", [P, 2, T])
    vt = si("vt", [P, NT, 512])
    silu = si("silu", [P, 2, T])
    mix_o = si("mix_o", [P, 2, T])
    fp = ExitStack()

    def sg(name, shape, dt=F32):
        return fp.enter_context(nc.sbuf_tensor(name, shape, dt))

    decay = sg("decay", [P, 4, T])
    ret_a = sg("ret_a_t", [P, 1280])
    ret_d = sg("ret_d_t", [P, 2, T])
    fp.close()
    ga_t = sg("ga_t", [16, T])
    wa2 = sg("wa2", [16, T])
    gscan = sg("gscan", [P, T])
    gmask = sg("gmask", [P, P])
    gk_i = sg("gk_i", [P, T])
    g_ed = sg("g_ed", [P, T])
    g_st = sg("g_st", [P, NGC - 1, 256])
    fp.close()
    g_ln, g_b, g_eb = att_l[:, 0], att_l[:, 1], att_l[:, 2]
    gk_t = att_pt[:, 0].rearrange("p (m k) -> p m k", m=NT)
    ga_m = att_pt[:, 1].rearrange("p (m i) -> p m i", m=NT)
    inner.close()
    wq = si("wq", [P, 8, T])
    wk = si("wk", [P, 2, T])
    wv = si("wv", [P, NT, 256])
    alibi = si("alibi", [P, 16, 256])
    swa_o = sq_sum
    inner.close()
    mixers.close()
    f_acc = merged
    hid2 = [si("hid2_hi", [P, HALF2, T], F32R), si("hid2_lo", [P, HALF2, T], F32R)]
    sig2 = si("sig2", [P, 2, T])
    inner.close()
    area.close()

    lin_src = {"h": (h_hi, h_lo), "o": o_hl}

    def col(name, c=0, n=1, parts=P):
        return par[0:parts, PCOL[name] + c:PCOL[name] + c + n]

    tenants = {}
    n_tenants = [0] * 8
    turn = {"lin": 0, "att": 0}
    pools = {"lin": [0, 1, 2, 3], "att": [5, 6, 7], "out": [4]}

    def full(name):
        b, k = tenants[name]
        return C.sem[f"bank_full{b}"], k + 1

    def evacuated(name):
        b, k = tenants[name]
        return C.sem[f"bank_free{b}"], k + 1

    def release(name):
        return C.sem[f"bank_free{tenants[name][0]}"], 1

    def ps(name):
        return bank[tenants[name][0]]

    slot_done = {}

    def ev(name):
        return ("bank", name)

    norms = {
        "n1": ([x_sb[:, c] for c in range(KD)], P, T, ones, 1 / D, "eps", [("x", "in")] * KD),
        "n2": ([x_sb[:, c] for c in range(KD)], P, T, ones, 1 / D, "eps", [ev(("wout", c)) for c in range(KD)]),
        "pre": ([x_sb[:, c] for c in range(KD)], P, T, ones, 1 / D, "eps",
                [ev(("down1", 1, c)) for c in range(KD)]),
        "post": ([merged[:, c] for c in range(KD)], P, T, ones, 1 / D, "eps",
                 [ev(("wout2", c)) for c in range(KD)]),
        "fpre": ([x_sb[:, c] for c in range(KD)], P, T, ones, 1 / D, "eps",
                 [("ev", "x_ready", "post", c) for c in range(KD)]),
        "fpost": ([f_acc[:, c] for c in range(KD)], P, T, ones, 1 / D, "eps",
                  [ev(("down2", 1, c)) for c in range(KD)]),
        "ks": ([ks_d[:]], P, T, ones64, 1 / HD, "eps", [ev("ks")]),
        "kw": ([kw_d[:]], P, T, ones64, 1 / HD, "eps", [ev("kw")]),
        "nq0": ([nq[:, 0]], P, T, ones64, 1.0, "eps*64", [ev("nq0")]),
        "nq1": ([nq[:, 1]], P, T, ones64, 1.0, "eps*64", [ev("nq1")]),
        "kcmp": ([cmp_k[:, 0, 0:N_CMP]], P, N_CMP, ones64, 1 / HD, "eps", [ev("cmp_k")]),
        "cq": ([cq[:, c] for c in range(2)], P, T, ones, 1 / 192, "eps", [ev("cq0"), ev("cq1")]),
        "ckv": ([ckv[:]], P, T, ones, 1 / P, "eps", [ev("ckv")]),
    }
    for h in range(NH):
        norms[("mk", h)] = ([mk[:, h]], QKD, T, ones, 1 / QKD, "eps", [ev(("mk", h))])
        norms[("mq", h)] = ([mq[:, h]], QKD, T, ones, 1.0, "eps*96", [("ev", "mla_q", h)])
        norms[("ret", h)] = ([ret_d[:, e] for e in range(2)], P, T, ones, 1 / 256, "gn_eps",
                             [("ev", "ret_d", h, e) for e in range(2)])
        norms[("gla", h)] = ([mix_o[:, e] for e in range(2)], P, T, ones, 1 / 256, "eps",
                             [ev(("gla_o", h, e)) for e in range(2)])
    for g in range(4):
        srcs = ([("ev", "conv_v", c) for c in range(2)] if g == 0 else
                [ev(({1: "nsa_o", 2: "mla_o", 3: "sb_o"}[g], c)) for c in range(2)])
        norms[("y", g)] = ([y[:, 2 * g + c] for c in range(2)], P, T, ones, 1 / 256, "eps", srcs)
    EPS_COL = {"eps": 0, "eps*64": 1, "eps*96": 2, "gn_eps": 3}
    EPS_VAL = [EPS, EPS * HD, EPS * QKD, GN_EPS]

    norm_order = []
    for step in ORDER:
        if step[0] == "norm":
            norm_order.append(step[1])
        elif step[0] == "mla_qk":
            norm_order += [("mk", step[1]), ("mq", step[1])]
    norm_at = {k: i for i, k in enumerate(norm_order)}
    sq_use = {}
    for k in norm_order:
        for c in range(len(norms[k][0])):
            sq_use[(k, c)] = len(sq_use)
    sq_uses = list(sq_use)

    def rstd(key):
        _, parts, cols, *_ = norms[key]
        return rstd_t[0:parts, norm_at[key] % 3, 0:cols]

    def wait_src(eng, w):
        if w[0] == "bank":
            eng.wait_ge(*evacuated(w[1]))
        elif w[0] == "ev":
            eng.wait_ge(*after(w[1], *w[2:]))
        else:
            eng.wait_ge(C.sem["x_in"], 16)

    def att(u):
        kind = u[0]
        if kind in ("slc", "win"):
            _, h, qt = u
            pb = HD * (h % 2)
            k = ks_d if kind == "slc" else kw_d
            v0 = 0 if kind == "slc" else HD
            g = 3 * h + (1 if kind == "slc" else 2)
            return dict(q=nq[pb:pb + HD, h // 2, qt * P:(qt + 1) * P], k=k[pb:pb + HD, 0:(qt + 1) * P],
                        w=(qt + 1) * P, bias=toep[:, h, (NT - 1 - qt) * P:T],
                        v=[v1[:, kt, v0:v0 + HD] for kt in range(qt + 1)],
                        out=("nsa_o", h // 2), pb=pb, qt=qt, first=False, last=kind == "win",
                        bank_first=(kind == "slc" and h % 2 == 0 and qt == 0),
                        bank_last=(kind == "win" and h % 2 == 1 and qt == NT - 1),
                        gate=gates[:, qt, g:g + 1])
        if kind == "mla":
            _, h, qt = u
            return dict(q=mq[:, h, qt * P:(qt + 1) * P], k=mk[:, h, 0:(qt + 1) * P], w=(qt + 1) * P,
                        bias=causal[:, (NT - 1 - qt) * P:T],
                        v=[mv[:, kt, h * HD:(h + 1) * HD] for kt in range(qt + 1)],
                        out=("mla_o", h // 2), pb=HD * (h % 2), qt=qt, first=True, last=True,
                        bank_first=(h % 2 == 0 and qt == 0), bank_last=(h % 2 == 1 and qt == NT - 1), gate=None)
        _, c, hf, qt = u
        pb, lo = HD * hf, max(0, qt - 1)
        kv = 2 * (c // 4) + hf
        return dict(q=wq[pb:pb + HD, c, qt * P:(qt + 1) * P], k=wk[pb:pb + HD, c // 4, lo * P:(qt + 1) * P],
                    w=(qt + 1 - lo) * P, bias=alibi[:, 2 * c + hf, (0 if qt else P):2 * P],
                    v=[wv[:, kt, kv * HD:(kv + 1) * HD] for kt in range(lo, qt + 1)],
                    out=("swa_o", c), pb=pb, qt=qt, first=True, last=True,
                    bank_first=(hf == 0 and qt == 0), bank_last=(hf == 1 and qt == NT - 1), gate=None,
                    sink=col("sinks", 2 * c + hf))

    att_order = [s[1] for s in ORDER if s[0] == "att_scores"]
    att_at = {u: i for i, u in enumerate(att_order)}

    sig_names = [s[1] for s in ORDER if s[0] == "fm" and isinstance(s[1], tuple) and s[1][0] in ("rg", "gg", "gate")]
    sig_at = {name: i for i, name in enumerate(sig_names)}

    def sig_user(n):
        name = sig_names[n]
        return ("br",) + name[1:] if name[0] == "gate" else name

    SB_OFF = [0, 512, 896, 1152]
    sb_order = [(s[1], s[2]) for s in ORDER if s[0] == "sb_scores"]

    block = ctx.enter_context(nc.Block())

    @block.tensor
    def _(pe):
        def take(name, pool="lin"):
            banks = pools[pool]
            b = banks[turn[pool] % len(banks)] if pool in turn else banks[0]
            if pool in turn:
                turn[pool] += 1
            if n_tenants[b]:
                pe.wait_ge(C.sem[f"bank_free{b}"], n_tenants[b])
            tenants[name] = (b, n_tenants[b])
            n_tenants[b] += 1
            return bank[b]

        def fill(name, ins):
            ins.then_inc(C.sem[f"bank_full{tenants[name][0]}"], 1)

        def mm(out, lhs, rhs, start, stop, **kw):
            return pe.matmul(out, lhs, rhs, start=start, stop=stop, **kw)

        def mm3(out, wh, wl, xh, xl, start, stop):
            mm(out, wh, xh, start, False)
            mm(out, wh, xl, False, False)
            return mm(out, wl, xh, False, stop)

        def slot_ready(i):
            pe.wait_ge(*after("w_lo", i))

        def slot_free(i, ins=None, name=None):
            if name is not None:
                slot_done[i] = full(name)
            else:
                ins.then_inc(*did("slot_used", i))
                slot_done[i] = after("slot_used", i)

        def ms(key, n_src):
            srcs, parts, cols, one, *_ = norms[key]
            out = take(("ms", key))
            if n_src == 1:
                pe.wait_ge(*after("sq_s", key, 0))
                rhs = sq[0:parts, sq_use[(key, 0)] % 2, 0:cols]
            else:
                pe.wait_ge(*after("sq_v", key, n_src - 1))
                rhs = sq_sum[0:parts, 0:cols]
            fill(("ms", key), mm(out[0:parts, 0:cols], one[0:parts, 0:parts], rhs, True, True))

        pe.wait_ge(C.sem["const_in"], 16 * N_CONST)
        seen_h = None
        for step in ORDER:
            stage = step[0]
            if stage == "bias_tables":
                pe.wait_ge(C.sem["misc_in"], 16 * N_MISC)
                pe.wait_ge(*after("bcast_v"))
                for h in range(NH):
                    for n, (c0, w) in enumerate(((0, 512), (512, 128), (640, 512), (1152, 512))):
                        out = take(("tab", h, n))
                        fill(("tab", h, n), mm(out[:, 0:w], rb_b[:, h], onehot[:, c0:c0 + w], True, True))
            elif stage == "norm":
                ms(step[1], len(norms[step[1]][0]))
            elif stage in ("apply_h", "apply_y", "merge"):
                seen_h = step[1]
            elif stage == "fm":
                _, name, src = step
                i = SLOTS[name][0]
                xh, xl = lin_src[src]
                slot_ready(i)
                out = take(name)
                for k in range(KD):
                    if src == "h":
                        pe.wait_ge(*after("h_ready", seen_h, k))
                    else:
                        pe.wait_ge(*after("o_ready", name[1], k))
                    wsl = slice(k * P, (k + 1) * P)
                    last = mm3(out[:], w_hi[:, i % SPL, wsl], w_lo[:, i % SPL, wsl], xh[:, k], xl[:, k],
                               k == 0, k == KD - 1)
                fill(name, last)
                slot_free(i, name=name)
            elif stage == "tm":
                _, name, cols = step
                i0, ns = SLOTS[name]
                outs = [take((name, t)) for t in range(NT)]
                per = KD // ns
                for s in range(ns):
                    slot_ready(i0 + s)
                    for t in range(NT):
                        for kk in range(per):
                            k = s * per + kk
                            if t == 0:
                                pe.wait_ge(*after("h_ready", seen_h, k))
                            wsl = slice(kk * (1024 // per), kk * (1024 // per) + cols)
                            ts = slice(t * P, (t + 1) * P)
                            wh, wl = w_hi[:, (i0 + s) % SPL, wsl], w_lo[:, (i0 + s) % SPL, wsl]
                            o = outs[t][:, 0:cols]
                            mm(o, h_hi[:, k, ts], wh, k == 0, False)
                            mm(o, h_hi[:, k, ts], wl, False, False)
                            last = mm(o, h_lo[:, k, ts], wh, False, k == KD - 1)
                        if s == ns - 1:
                            fill((name, t), last)
                    if s == ns - 1:
                        slot_free(i0 + s, name=(name, NT - 1))
                    else:
                        slot_free(i0 + s, last)
            elif stage == "down":
                _, name, nk = step
                i0 = SLOTS[name][0]
                hh, hl = hid1 if name[0] == "down1" else hid2
                for o in range(KD):
                    nm = (name[0], name[1], o)
                    out = take(nm)
                    for k in range(nk):
                        g = o * nk + k
                        i = i0 + g // 8
                        if g % 8 == 0:
                            slot_ready(i)
                        if o == 0:
                            pe.wait_ge(*after("hid", name[0], name[1], k))
                        wsl = slice(g % 8 * P, g % 8 * P + P)
                        last = mm3(out[:], w_hi[:, i % SPL, wsl], w_lo[:, i % SPL, wsl], hh[:, k], hl[:, k],
                                   k == 0, k == nk - 1)
                        if k == nk - 1:
                            fill(nm, last)
                            if g % 8 == 7:
                                slot_free(i, name=nm)
                        elif g % 8 == 7:
                            slot_free(i, last)
            elif stage == "cmp_up":
                _, name, kv = step
                i0 = SLOTS[name][0]
                pe.wait_ge(*after("cmpx", kv))
                outs = [take(("cmp_h", kv, c)) for c in range(2)]
                for j in range(16):
                    i = i0 + j // 4
                    if j % 4 == 0:
                        slot_ready(i)
                    for c in range(2):
                        wsl = slice((j % 4) * 256 + c * P, (j % 4) * 256 + (c + 1) * P)
                        last = mm3(outs[c][:, 0:32], w_hi[:, i % SPL, wsl], w_lo[:, i % SPL, wsl],
                                   cmp_x[0][:, kv, j], cmp_x[1][:, kv, j], j == 0, j == 15)
                        if j == 15:
                            fill(("cmp_h", kv, c), last)
                    if j % 4 == 3:
                        if j == 15:
                            slot_free(i, name=("cmp_h", kv, 1))
                        else:
                            slot_free(i, last)
            elif stage == "cmp_down":
                pe.wait_ge(*evacuated(("cmp_h", 1, 1)))
                out = take("cmp_k")
                for c in range(2):
                    last = mm(out[:, 0:N_CMP], w2k[:, c], cmp_h[:, c, 0:N_CMP], c == 0, c == 1)
                fill("cmp_k", last)
                out = take("cmp_vt")
                for c in range(2):
                    last = mm(out[0:N_CMP, 0:HD], cmp_h[:, 2 + c, 0:N_CMP], w2v[:, c], c == 0, c == 1)
                fill("cmp_vt", last)
            elif stage == "cmp_softmax":
                pe.wait_ge(C.sem["bias_in"], 16 * 2 * NH)
                out = take("cmp_bias")
                for qt in range(NT):
                    for h in range(NH):
                        last = pe.transpose(out[:, (qt * NH + h) * N_CMP:(qt * NH + h + 1) * N_CMP],
                                            cb_t[:, h, qt * P:(qt + 1) * P], ident[0:N_CMP, 0:N_CMP])
                fill("cmp_bias", last)
                pe.wait_ge(*after("rstd_used", "kcmp"))
                pe.wait_ge(*after("rstd_used", "nq1"))
                for hf in range(2):
                    out = take(("cmp_sc", hf))
                    pb = HD * hf
                    for qt in range(NT):
                        for j in range(2):
                            last = mm(out[:, (qt * 2 + j) * N_CMP:(qt * 2 + j + 1) * N_CMP],
                                      nq[pb:pb + HD, j, qt * P:(qt + 1) * P], cmp_k[pb:pb + HD, 1, 0:N_CMP],
                                      True, True, skip_group_check=True)
                    fill(("cmp_sc", hf), last)
                pe.wait_ge(*after("cmp_v", "p"))
                for qt in range(NT):
                    out = take(("cmp_pt", qt))
                    for h in range(NH):
                        last = pe.transpose(out[0:N_CMP, h * P:(h + 1) * P], cmp_p[:, qt, h], ident[:])
                    fill(("cmp_pt", qt), last)
            elif stage == "att_scores":
                u = step[1]
                A = att(u)
                if u[0] in ("slc", "win"):
                    pe.wait_ge(*after("rstd_used", "nq1"))
                elif u[0] == "mla":
                    pe.wait_ge(*after("rstd_used", ("mq", u[1])))
                else:
                    pe.wait_ge(*evacuated(("wk", 1)))
                out = take(("sc", u), "att")
                fill(("sc", u), mm(out[:, 0:A["w"]], A["q"], A["k"], True, True))
            elif stage == "att_turn":
                u = step[1]
                A = att(u)
                pe.wait_ge(*after("att_p", u))
                out = take(("pt", u), "att")
                for b in range(A["w"] // P):
                    last = pe.transpose(out[:, b * P:(b + 1) * P], att_l[:, att_at[u] % 3, b * P:(b + 1) * P],
                                        ident[:])
                fill(("pt", u), last)
            elif stage == "att_pv":
                u = step[1]
                A = att(u)
                if A["bank_first"]:
                    take(A["out"], "out")
                out = ps(A["out"])[A["pb"]:A["pb"] + HD, A["qt"] * P:(A["qt"] + 1) * P]
                if u[0] == "slc":
                    h, qt = u[1], u[2]
                    pe.wait_ge(*evacuated(("cmp_pt", qt)))
                    pe.wait_ge(*evacuated("cmp_vt"))
                    mm(out, cmp_vt[0:N_CMP, :], cmp_pt[0:N_CMP, qt, h], True, False)
                if u[0] in ("slc", "win"):
                    pe.wait_ge(*evacuated(("v1", NT - 1)))
                elif u[0] == "mla":
                    pe.wait_ge(*evacuated(("mv", 1)))
                else:
                    pe.wait_ge(*evacuated(("wv", NT - 1)))
                pe.wait_ge(*evacuated(("pt", u)))
                n = len(A["v"])
                for b in range(n):
                    last = mm(out, A["v"][b], att_pt[:, att_at[u] % 2, b * P:(b + 1) * P],
                              A["first"] and b == 0, A["last"] and b == n - 1)
                if A["bank_last"]:
                    fill(A["out"], last)
                else:
                    last.then_inc(*did("att_done", u))
            elif stage == "mla_v":
                pe.wait_ge(*after("rstd_used", "ckv"))
                for n in range(2):
                    out = take(("mv", n))
                    for t in range(2):
                        tt = 2 * n + t
                        last = mm(out[:, t * 256:(t + 1) * 256], ckv[:, tt * P:(tt + 1) * P], wvb[:], True, True,
                                  skip_group_check=True)
                    fill(("mv", n), last)
            elif stage == "mla_qk":
                h = step[1]
                out = take(("mk", h))
                fill(("mk", h), mm(out[0:QKD, :], wkb[:, h], ckv[:], True, True))
                pe.wait_ge(*after("rstd_used", "cq"))
                for v in range(2):
                    out = take(("mq", h, v))
                    mm(out[0:QKD, :], wqb[:, 0, v, h], cq[:, 0], True, False)
                    fill(("mq", h, v), mm(out[0:QKD, :], wqb[0:HD, 1, v, h], cq[0:HD, 1], False, True))
                ms(("mk", h), 1)
                ms(("mq", h), 1)
            elif stage == "sb_scores":
                _, h, kt = step
                pb = HD * (h % 2)
                pe.wait_ge(*evacuated("sk1"))
                out = take(("z", h, kt))
                fill(("z", h, kt), mm(out[:, 0:T - kt * P], s_qk[pb:pb + HD, 2 + h // 2, kt * P:(kt + 1) * P],
                                      s_qk[pb:pb + HD, h // 2, kt * P:T], True, True))
            elif stage == "sb_exp":
                _, h, kt = step
                pb = HD * (h % 2)
                w = T - kt * P
                out = take(("r", h, kt), "att")
                mm(out[:, 0:w], s_qk[pb:pb + HD, 2 + h // 2, kt * P:(kt + 1) * P],
                   s_qk[pb:pb + HD, h // 2, kt * P:T], True, False, skip_group_check=True)
                mm(out[:, 0:P], ident[:], sbm[:, 3], False, False, skip_group_check=True)
                pe.wait_ge(*after("sb_sp", h, kt))
                for j in range(NT - 1, kt, -1):
                    mm(out[:, (j - kt) * P:w], sbm[:, 1], sb_sp[:, h % 2, SB_OFF[j]:SB_OFF[j] + T - j * P],
                       False, False, skip_group_check=True)
                last = mm(out[:, 0:w], sbm[:, 0], sb_sp[:, h % 2, SB_OFF[kt]:SB_OFF[kt] + w], False, True,
                          skip_group_check=True)
                fill(("r", h, kt), last)
            elif stage == "sb_pv":
                h = step[1]
                pb = HD * (h % 2)
                if h % 2 == 0:
                    take(("sb_o", h // 2), "out")
                out = ps(("sb_o", h // 2))
                pe.wait_ge(*evacuated(("r", h, 0)))
                for kt in range(NT):
                    w = T - kt * P
                    last = mm(out[pb:pb + HD, kt * P:T], v1[:, kt, 2 * HD + h * HD:2 * HD + (h + 1) * HD],
                              sb_a[:, h % 2, SB_OFF[kt]:SB_OFF[kt] + w], kt == 0, kt == NT - 1)
                if h % 2 == 0:
                    last.then_inc(*did("sb_pe", h))
                else:
                    fill(("sb_o", h // 2), last)
            elif stage == "ret_scores":
                _, h, jt = step
                pe.wait_ge(*evacuated(("rk", h)))
                out = take(("rs", h, jt), "att")
                fill(("rs", h, jt), mm(out[:, 0:T - jt * P], kf[:, h % 2, jt * P:(jt + 1) * P], qf[:, h % 2, jt * P:T],
                                       True, True))
            elif stage == "ret_pv":
                h = step[1]
                pe.wait_ge(*evacuated((("rv", h // 2), NT - 1)))
                pe.wait_ge(*evacuated(("rs", h, NT - 1)))
                for e in range(2):
                    out = take(("ret_o", h, e))
                    for jt in range(NT):
                        w = T - jt * P
                        last = mm(out[:, jt * P:T], vt[:, jt, h % 2 * 256 + e * P:h % 2 * 256 + (e + 1) * P],
                                  ret_a[:, SB_OFF[jt]:SB_OFF[jt] + w], jt == 0, jt == NT - 1)
                    fill(("ret_o", h, e), last)
            elif stage == "ret_mean":
                h = step[1]
                out = take(("mean", h))
                for e in range(2):
                    pe.wait_ge(*evacuated(("ret_o", h, e)))
                    last = mm(out[:], ones[:], mix_o[:, e], e == 0, e == 1)
                fill(("mean", h), last)
            elif stage == "gla_decay":
                h = step[1]
                pe.wait_ge(*evacuated("ga"))
                pe.wait_ge(C.sem["late_in"], 16 * 4)
                out = take(("gz", h), "att")
                fill(("gz", h), mm(out[:], wa2[:, h * P:(h + 1) * P], ga_t[:], True, True))
            elif stage == "gla_chunks":
                h = step[1]
                pe.wait_ge(*after("gla_v", "kd", h))
                out = take(("kdt", h), "att")
                for m in range(NT):
                    last = pe.transpose(out[:, m * P:(m + 1) * P], kf[:, h % 2, m * P:(m + 1) * P], ident[:])
                fill(("kdt", h), last)
                out = take(("ga_s", h), "att")
                for m in range(NT):
                    ms_ = slice(m * P, (m + 1) * P)
                    last = mm(out[:, ms_], gk_i[:, ms_], qf[:, h % 2, ms_], True, True, skip_group_check=True)
                fill(("ga_s", h), last)
                pe.wait_ge(*evacuated(("kdt", h)))
                pe.wait_ge(*evacuated((("gv", h // 2), NT - 1)))
                for n in range(NGC - 1):
                    out = take(("kv", h, n), "att")
                    r = slice(GC * (n % 2), GC * (n % 2) + GC)
                    fill(("kv", h, n), mm(out[:, 0:256], gk_t[r, n // 2], vt[r, n // 2, h % 2 * 256:(h % 2 + 1) * 256],
                                          True, True))
                pe.wait_ge(*evacuated(("ga_s", h)))
                for e in range(2):
                    out = take(("gla_o", h, e))
                    for m in range(NT):
                        mm(out[:, m * P:(m + 1) * P], vt[:, m, h % 2 * 256 + e * P:h % 2 * 256 + (e + 1) * P], ga_m[:, m],
                           True, False, skip_group_check=True)
                        for n in (2 * m, 2 * m + 1):
                            if n == 0:
                                continue
                            pe.wait_ge(*evacuated(("kv", h, n - 1)))
                            last = mm(out[:, n * GC:(n + 1) * GC], g_st[:, n - 1, e * P:(e + 1) * P],
                                      qf[:, h % 2, n * GC:(n + 1) * GC], False, n % 2 == 1, skip_group_check=True)
                    fill(("gla_o", h, e), last)

    @block.scalar
    def _(act):
        act.preload_act_table_set("natural_log_exp_and_others")
        act.dma_start(par[:], a["par"]).then_inc(C.sem["const_in"], 16)
        for t, src in ((ones, "ones"), (ones64, "ones64"), (ident, "ident"), (causal, "causal")):
            act.dma_start(t[:], a[src]).then_inc(C.sem["const_in"], 16)
        act.dma_start(onehot[:], a["onehot"]).then_inc(C.sem["misc_in"], 16)
        act.dma_start(rb[0:N_BUCKETS, :], a["rel_bias"]).then_inc(C.sem["misc_in"], 16)
        for t, src in ((w2k, "w2k"), (w2v, "w2v"), (wqb, "wqb"), (wkb, "wkb"), (wvb, "wvb"),
                       (rope_c, "rope_c"), (rope_s, "rope_s"), (sbm, "sbm")):
            act.dma_start(t[:], a[src]).then_inc(C.sem["misc_in"], 16)

        def chain(ins):
            ins.then_inc(C.sem["s_chain"], 1)
            C.n["s_chain"] = C.n.get("s_chain", 0) + 1
            act.wait_ge(C.sem["s_chain"], C.n["s_chain"])

        def copy_out(name, dst, src_ap, scale=1.0):
            act.wait_ge(*full(name))
            act.activation(dst, src_ap, ACT.Copy, scale=scale).then_inc(*release(name))

        def sq_free(key, c):
            u = sq_use[(key, c)]
            if u >= 2:
                k2, c2 = sq_uses[u - 2]
                if len(norms[k2][0]) == 1:
                    act.wait_ge(*full(("ms", k2)))
                else:
                    act.wait_ge(*after("sq_v", k2, max(c2, 1)))

        def norm(key):
            srcs, parts, cols, one, scale, eps, waits = norms[key]
            for c, s in enumerate(srcs):
                wait_src(act, waits[c])
                sq_free(key, c)
                act.activation(sq[0:parts, sq_use[(key, c)] % 2, 0:cols], s, ACT.Square)\
                   .then_inc(*did("sq_s", key, c))
            act.wait_ge(*full(("ms", key)))
            r = norm_at[key]
            if r >= 3:
                act.wait_ge(*after("rstd_used", norm_order[r - 3]))
            if r == 0:
                act.wait_ge(*after("table", "eps"))
            e = EPS_COL[eps]
            act.activation(rstd(key), ps(("ms", key))[0:parts, 0:cols], ACT.Ln, scale=scale,
                           bias=epst[0:parts, e:e + 1]).then_inc(*release(("ms", key)))
            act.wait_ge(*evacuated(("ms", key)))
            act.activation(rstd(key), rstd(key), ACT.Exp, scale=-0.5).then_inc(*did("rstd", key))

        def ready(name, c=None):
            act.wait_ge(*after(name, c))

        act.wait_ge(C.sem["const_in"], 16 * N_CONST)
        for step in ORDER:
            stage = step[0]
            if stage == "norm":
                norm(step[1])
            elif stage == "fm":
                name = step[1]
                key = name[0] if isinstance(name, tuple) else name
                if name == "ks" or name == "kw":
                    copy_out(name, (ks_d if name == "ks" else kw_d)[:], ps(name)[:])
                elif name == "nq0" or name == "nq1":
                    copy_out(name, nq[:, int(name[2])], ps(name)[:])
                elif name == "cq0" or name == "cq1":
                    copy_out(name, cq[:, int(name[2])], ps(name)[:])
                elif name == "ckv":
                    copy_out(name, ckv[:], ps(name)[:])
                elif name == "kr" or name == "krs":
                    copy_out(name, kr[:, 0 if name == "kr" else 1], ps(name)[0:QKD, :])
                elif name in ("sq0", "sq1", "sk0", "sk1"):
                    if name == "sq0":
                        act.wait_ge(*full(("mla_o", 1)))
                    c = int(name[2]) + (2 if name[1] == "k" else 0)
                    copy_out(name, s_qk[:, c], ps(name)[:], scale=HD ** -0.5 if name[1] == "q" else 1.0)
                elif key == "up1":
                    _, half, c = name
                    n = half * HALF1 + c
                    act.wait_ge(*full(name))
                    if n == 0:
                        act.wait_ge(*after("h_ready", "n2", KD - 1))
                    if n >= 2:
                        act.wait_ge(*after("hid", "down1", (n - 2) // HALF1, (n - 2) % HALF1))
                    act.activation(r1[:, n % 2], ps(name)[:], ACT.Relu).then_inc(*release(name))
                    act.wait_ge(*evacuated(name))
                    act.activation(r1[:, n % 2], r1[:, n % 2], ACT.Square).then_inc(*did("hid_s", name))
                elif key in ("rq", "gq"):
                    h = name[1]
                    if key == "rq" and h >= 2:
                        act.wait_ge(*full(("rs", h - 2, NT - 1)))
                    if key == "gq" and h >= 2:
                        act.wait_ge(*full(("gla_o", h - 2, 1)))
                    copy_out(name, qf[:, h % 2], ps(name)[:], scale=P ** -0.5 if key == "gq" else 1.0)
                elif key in ("rk", "gk"):
                    copy_out(name, kf[:, name[1] % 2], ps(name)[:])
                elif key in ("rg", "gg"):
                    _, h, e = name
                    n = sig_at[name]
                    act.wait_ge(*full(name))
                    if n >= 2:
                        act.wait_ge(*evacuated(sig_user(n - 2)))
                    act.activation(sig[:, n % 2], ps(name)[:], ACT.Sigmoid).then_inc(*did("gate_s", name))
                elif key == "ga":
                    act.wait_ge(*after("o_ready", 0, KD - 1))
                    copy_out(name, ga_t[:], ps(name)[0:16, :])
                elif key == "gate":
                    _, b, m = name
                    n = sig_at[name]
                    act.wait_ge(*full(name))
                    act.wait_ge(*evacuated(sig_user(n - 2)))
                    act.activation(sig[:, n % 2], ps(name)[:], ACT.Sigmoid).then_inc(*release(name))
                elif key == "wq":
                    if name[1] == 0:
                        act.wait_ge(*full(("gla_o", 3, 1)))
                        act.wait_ge(*after("o_ready", 1, KD - 1))
                    copy_out(name, wq[:, name[1]], ps(name)[:], scale=HD ** -0.5)
                elif key == "wk":
                    copy_out(name, wk[:, name[1]], ps(name)[:])
                elif key == "fg":
                    _, half, c = name
                    n = half * HALF2 + c
                    act.wait_ge(*full(name))
                    if n == 0:
                        act.wait_ge(*full(("swa_o", 7)))
                        act.wait_ge(*after("h_ready", "fpre", KD - 1))
                    if n >= 2:
                        act.wait_ge(*evacuated(("fu", (n - 2) // HALF2, (n - 2) % HALF2)))
                    act.activation(sig2[:, n % 2], ps(name)[:], ACT.Sigmoid).then_inc(*did("gate_s", name))
            elif stage == "tm":
                name = step[1]
                if name == ("rv", 0):
                    act.wait_ge(*full(("down1", 1, KD - 1)))
                elif name in (("rv", 1), ("gv", 0), ("gv", 1)):
                    act.wait_ge(*full({"rv1": ("ret_o", 1, 1), "gv0": ("ret_o", 3, 1),
                                       "gv1": ("gla_o", 1, 1)}[name[0] + str(name[1])]))
                for t in range(NT):
                    if name == "v1":
                        copy_out((name, t), v1[:, t], ps((name, t))[:, 0:396])
                    elif name == "wv":
                        copy_out((name, t), wv[:, t], ps((name, t))[:, 0:256])
                    else:
                        copy_out((name, t), vt[:, t], ps((name, t))[:])
                if name == "v1":
                    act.wait_ge(*evacuated(("v1", NT - 1)))
                    act.activation(gates[:], v1[:, :, 384:396], ACT.Exp, scale=-1.0).then_inc(*did("cmp_s", "g"))
            elif stage == "cmp_down":
                copy_out("cmp_k", cmp_k[:, 0, 0:N_CMP], ps("cmp_k")[:, 0:N_CMP])
                copy_out("cmp_vt", cmp_vt[0:N_CMP, :], ps("cmp_vt")[0:N_CMP, 0:HD])
            elif stage == "cmp_up":
                kv = step[2]
                for c in range(2):
                    act.wait_ge(*full(("cmp_h", kv, c)))
                    act.activation(cmp_h[:, 2 * kv + c, 0:N_CMP], ps(("cmp_h", kv, c))[:, 0:N_CMP], ACT.Exp,
                                   scale=-1.0).then_inc(*did("cmp_s", kv, c))
            elif stage == "cmp_softmax":
                act.wait_ge(*after("cmp_v", "l"))
                act.activation(cmp_p[:], cmp_p[:], ACT.Exp).then_inc(*did("cmp_s", "exp"))
                for qt in range(NT):
                    copy_out(("cmp_pt", qt), cmp_pt[0:N_CMP, qt], ps(("cmp_pt", qt))[0:N_CMP, :]
                             .rearrange("p (h q) -> p h q", h=NH))
            elif stage == "att_scores":
                u = step[1]
                A = att(u)
                n = att_at[u]
                act.wait_ge(*after("att_n", u))
                L, sm = att_l[:, n % 3, 0:A["w"]], small[:, n % 4]
                act.activation(L, L, ACT.Exp, bias=sm[:, 1:2], accum_out=sm[:, 2:3]).then_inc(*did("att_exp", u))
                if "sink" in A:
                    act.activation(sm[:, 5:6], A["sink"], ACT.Exp, bias=sm[:, 1:2]).then_inc(*did("swa_s", u))
            elif stage == "att_turn":
                u = step[1]
                A = att(u)
                n = att_at[u]
                act.wait_ge(*full(("pt", u)))
                if n >= 2:
                    v = att_order[n - 2]
                    act.wait_ge(*(full(att(v)["out"]) if att(v)["bank_last"] else after("att_done", v)))
                act.activation(att_pt[:, n % 2, 0:A["w"]], ps(("pt", u))[:, 0:A["w"]], ACT.Copy)\
                   .then_inc(*release(("pt", u)))
            elif stage == "att_pv":
                u = step[1]
                A = att(u)
                if A["bank_last"]:
                    if u[0] == "swa":
                        if u[1] >= 1:
                            act.wait_ge(*after("o_ready", 2, u[1] - 1))
                        copy_out(A["out"], swa_o[:], ps(A["out"])[:])
                    else:
                        g = 1 if u[0] == "win" else 2
                        copy_out(A["out"], y[:, 2 * g + A["out"][1]], ps(A["out"])[:])
            elif stage == "mla_v":
                for n in range(2):
                    copy_out(("mv", n), mv[:, 2 * n:2 * n + 2], ps(("mv", n))[:].rearrange("p (t c) -> p t c", t=2))
            elif stage == "mla_qk":
                norm(("mk", step[1]))
                norm(("mq", step[1]))
            elif stage == "sb_scores":
                _, h, kt = step
                w = T - kt * P
                n = sb_order.index((h, kt))
                act.wait_ge(*full(("z", h, kt)))
                if n >= 2:
                    act.wait_ge(*after("sb_sp", *sb_order[n - 2]))
                e = sb_e[:, n % 2, 0:w]
                chain(act.activation(e, ps(("z", h, kt))[:, 0:w], ACT.Abs))
                chain(act.activation(e, e, ACT.Exp, scale=-1.0))
                act.activation(e, e, ACT.Ln, bias=1.0).then_inc(*did("sb_exp", h, kt))
            elif stage == "sb_exp":
                _, h, kt = step
                w = T - kt * P
                act.wait_ge(*full(("r", h, kt)))
                if h >= 2:
                    act.wait_ge(*(after("sb_pe", h - 2) if h % 2 == 0 else full(("sb_o", 0))))
                act.activation(sb_a[:, h % 2, SB_OFF[kt]:SB_OFF[kt] + w], ps(("r", h, kt))[:, 0:w], ACT.Exp)\
                   .then_inc(*release(("r", h, kt)))
            elif stage == "sb_pv":
                if step[1] % 2 == 1:
                    nm = ("sb_o", step[1] // 2)
                    copy_out(nm, y[:, 6 + step[1] // 2], ps(nm)[:])
            elif stage == "ret_pv":
                h = step[1]
                for e in range(2):
                    if h >= 1:
                        act.wait_ge(*after("ret_d", h - 1, e))
                    copy_out(("ret_o", h, e), mix_o[:, e], ps(("ret_o", h, e))[:])
            elif stage == "gla_decay":
                h = step[1]
                if h >= 1:
                    act.wait_ge(*evacuated(("kv", h - 1, NGC - 2)))
                g0 = g_ln
                act.wait_ge(*full(("gz", h)))
                chain(act.activation(g0, ps(("gz", h))[:], ACT.Abs, bias=col("b_alpha", h)))
                chain(act.activation(g0, g0, ACT.Exp, scale=-1.0))
                act.activation(g0, g0, ACT.Ln, bias=1.0).then_inc(*did("gla_s", "ln", h))
                act.wait_ge(*after("gla_v", "d", h))
                act.activation(g_eb, g_b, ACT.Exp).then_inc(*did("gla_s", "eb", h))
                act.activation(gk_i[:], g_b, ACT.Exp, scale=-1.0).then_inc(*did("gla_s", "enb", h))
                act.activation(g_ed[:], g_ed[:], ACT.Exp).then_inc(*did("gla_s", "ed", h))
            elif stage == "gla_chunks":
                h = step[1]
                if h >= 1:
                    act.wait_ge(*full(("kv", h - 1, NGC - 2)))
                copy_out(("kdt", h), gk_t, ps(("kdt", h))[:].rearrange("p (m k) -> p m k", m=NT))
                for e in range(2):
                    if h >= 1:
                        act.wait_ge(*after("gla_done", h - 1, e))
                    copy_out(("gla_o", h, e), mix_o[:, e], ps(("gla_o", h, e))[:])

    @block.vector
    def _(dve):
        def chain(ins):
            ins.then_inc(C.sem["v_chain"], 1)
            C.n["v_chain"] = C.n.get("v_chain", 0) + 1
            dve.wait_ge(C.sem["v_chain"], C.n["v_chain"])

        def own(name, *key):
            dve.wait_ge(*after(name, *key))

        def split(t, hi, lo, *event):
            chain(dve.tensor_copy(hi, t))
            dve.tensor_tensor(lo, t, hi.bitcast(F32), ALU.subtract).then_inc(*did(*event))
            own(*event)

        def squares(key):
            srcs, parts, cols, *_ = norms[key]
            if len(srcs) == 1:
                return
            for c in range(1, len(srcs)):
                own("sq_s", key, c)
                b = [sq[0:parts, sq_use[(key, x)] % 2, 0:cols] for x in (c - 1, c)]
                if c == 1:
                    for k2 in reversed(norm_order[:norm_at[key]]):
                        if len(norms[k2][0]) > 1:
                            dve.wait_ge(*full(("ms", k2)))
                            break
                else:
                    own("sq_v", key, c - 1)
                dve.tensor_tensor(sq_sum[0:parts, 0:cols], b[0] if c == 1 else sq_sum[0:parts, 0:cols], b[1],
                                  ALU.add).then_inc(*did("sq_v", key, c))

        def scaled(key, dst, src, w, parts=P):
            return dve.scalar_tensor_tensor(out=dst, in0=src, scalar=w, in1=rstd(key), op0=ALU.mult, op1=ALU.mult)

        for i, v in enumerate(EPS_VAL):
            ins = dve.memset(epst[:, i:i + 1], v)
        ins.then_inc(*did("table", "eps"))
        dve.wait_ge(C.sem["const_in"], 16 * N_CONST)
        last_h = None
        for step in ORDER:
            stage = step[0]
            if stage == "bias_tables":
                dve.wait_ge(C.sem["misc_in"], 16 * N_MISC)
                chain(dve.memset(rb[N_BUCKETS:N_BUCKETS + 1, :], NEG))
                dve.tensor_copy(rb_b[:], rb[:, :, None].to_broadcast([33, NH, P])).then_inc(*did("bcast_v"))
                for h in range(NH):
                    for n, (c0, w) in enumerate(((0, 512), (512, 128), (0, 512), (512, 512))):
                        if h and n in (0, 2):
                            dve.wait_ge(C.sem[f"bias_out{n // 2}"], 16 * h)
                        dve.wait_ge(*full(("tab", h, n)))
                        dve.tensor_copy(tab[:, n // 2, c0:c0 + w], ps(("tab", h, n))[:, 0:w])\
                           .then_inc(*release(("tab", h, n)))
            elif stage == "norm":
                squares(step[1])
            elif stage in ("apply_h", "apply_y"):
                key = step[1]
                if last_h is not None:
                    dve.wait_ge(*full(last_h))
                for c in range(KD):
                    if stage == "apply_y":
                        nk, src, w = ("y", c // 2), y[:, c], col("out_norm", c)
                    else:
                        nk, src, w = key, x_sb[:, c], col(step[2], c)
                    if stage == "apply_y" or c == 0:
                        own("rstd", nk)
                    t = tmp[:, c % 2]
                    ins = scaled(nk, t, src, w)
                    if (stage == "apply_y" and c % 2 == 1) or (stage == "apply_h" and c == KD - 1):
                        ins.then_inc(*did("rstd_used", nk))
                        own("rstd_used", nk)
                    else:
                        chain(ins)
                    split(t, h_hi[:, c], h_lo[:, c], "h_ready", key, c)
            elif stage == "fm":
                name, src = step[1], step[2]
                if src == "h":
                    last_h = name
                key = name[0] if isinstance(name, tuple) else name
                if name in ("kc", "vc"):
                    kv = 0 if name == "kc" else 1
                    dve.wait_ge(*full(name))
                    dve.tensor_copy(kv_raw[0:HD, kv], ps(name)[0:HD, :])
                    dve.tensor_copy(kv_raw[HD:P, kv, 0:T - 1], ps(name)[HD:P, 1:T]).then_inc(*release(name))
                    dve.wait_ge(*evacuated(name))
                    v4 = kv_raw[:, kv].rearrange("p (n j two) -> p j two n", j=8, two=2)
                    pos = par[:, PCOL["pos"] + 16 * kv:PCOL["pos"] + 16 * (kv + 1)]
                    t = tmp[:, 0].rearrange("p (j n) -> p j n", n=32)
                    chain(dve.memset(tmp[:, 0], 0.0))
                    for k in range(2):
                        dve.wait_ge(C.sem[f"bias_out{k}"], 16 * NH)
                    for half in range(2):
                        ins = dve.tensor_tensor(t[:, 8 * half:8 * half + 8, 0:N_CMP],
                                                v4[:, :, 0, half:half + N_CMP],
                                                pos[:, 8 * half:8 * half + 8, None].to_broadcast([P, 8, N_CMP]), ALU.add)
                    chain(ins)
                    split(tmp[:, 0], cmp_x[0][:, kv].rearrange("p j n -> p (j n)"),
                          cmp_x[1][:, kv].rearrange("p j n -> p (j n)"), "cmpx", kv)
                elif key in ("ac", "au", "ab"):
                    c = name[1]
                    dve.wait_ge(*full(name))
                    v = conv_t[:, 0, 2:2 + T]
                    if key == "ac":
                        if c == 0:
                            dve.wait_ge(*full(("mla_o", 1)))
                            chain(dve.memset(conv_t[:], 0.0))
                        ins = dve.tensor_copy(conv_t[:, 1, 2:2 + T], ps(name)[:])
                    elif key == "au":
                        ins = dve.tensor_tensor(v, ps(name)[:], conv_t[:, 1, 2:2 + T], ALU.mult)
                    else:
                        yc = y[:, c]
                        w = [col("conv_w", 2 * k + c) for k in range(3)]
                        chain(dve.tensor_scalar(yc, conv_t[:, 0, 2:2 + T], w[2], col("conv_b", c), ALU.mult, ALU.add))
                        for k in (1, 0):
                            chain(dve.scalar_tensor_tensor(out=yc, in0=conv_t[:, 0, k:k + T], scalar=w[k], in1=yc,
                                                           op0=ALU.mult, op1=ALU.add))
                        ins = dve.tensor_tensor(conv_t[:, 1, 2:2 + T], ps(name)[:], yc, ALU.mult)
                    ins.then_inc(*release(name))
                    dve.wait_ge(*evacuated(name))
                    if key == "ab":
                        dve.tensor_copy(y[:, c], conv_t[:, 1, 2:2 + T]).then_inc(*did("conv_v", c))
                        own("conv_v", c)
                elif key == "wout":
                    c = name[1]
                    dve.wait_ge(*full(name))
                    dve.tensor_tensor(x_sb[:, c], ps(name)[:], x_sb[:, c], ALU.add).then_inc(*release(name))
                elif key == "wout2":
                    c = name[1]
                    dve.wait_ge(*full(name))
                    dve.tensor_copy(merged[:, c], ps(name)[:]).then_inc(*release(name))
                elif key == "up1":
                    _, half, c = name
                    own("hid_s", name)
                    if half == 1 and c == 0:
                        dve.wait_ge(*full(("down1", 0, KD - 1)))
                    if half == 0 and c == 0:
                        dve.wait_ge(*full(("wout", KD - 1)))
                    split(r1[:, (half * HALF1 + c) % 2], hid1[0][:, c], hid1[1][:, c], "hid", "down1", half, c)
                elif key in ("rg", "gg"):
                    _, h, e = name
                    n = sig_at[name]
                    own("gate_s", name)
                    dve.tensor_tensor(silu[:, e], ps(name)[:], sig[:, n % 2], ALU.mult).then_inc(*release(name))
                    dve.wait_ge(*evacuated(name))
                elif key == "br":
                    _, b, m = name
                    n = sig_at[("gate", b, m)]
                    dve.wait_ge(*full(name))
                    dve.wait_ge(*evacuated(("gate", b, m)))
                    t = merged[:, m] if b == 0 else tmp[:, n % 2]
                    ins = dve.tensor_tensor(t, ps(name)[:], sig[:, n % 2], ALU.mult)
                    ins.then_inc(*release(name))
                    dve.wait_ge(*evacuated(name))
                    if b:
                        chain(dve.tensor_tensor(merged[:, m], merged[:, m], t, ALU.add))
                elif key == "fu":
                    _, half, c = name
                    n = half * HALF2 + c
                    own("gate_s", ("fg", half, c))
                    if half == 1 and c == 0:
                        dve.wait_ge(*full(("down2", 0, KD - 1)))
                    s = sig2[:, n % 2]
                    dve.tensor_tensor(s, ps(("fg", half, c))[:], s, ALU.mult).then_inc(*release(("fg", half, c)))
                    dve.wait_ge(*evacuated(("fg", half, c)))
                    dve.wait_ge(*full(name))
                    t = tmp[:, n % 2]
                    dve.tensor_tensor(t, ps(name)[:], s, ALU.mult).then_inc(*release(name))
                    dve.wait_ge(*evacuated(name))
                    split(t, hid2[0][:, c], hid2[1][:, c], "hid", "down2", half, c)
            elif stage == "tm" and step[1] == "v1":
                last_h = ("v1", NT - 1)
                own("cmp_s", "g")
                chain(dve.tensor_scalar(gates[:], gates[:], 1.0, None, ALU.add))
                dve.reciprocal(gates[:], gates[:]).then_inc(*did("gate_v"))
                own("gate_v")
            elif stage == "tm":
                last_h = (step[1], NT - 1)
            elif stage == "down":
                _, name, nk = step
                for o in range(KD):
                    nm = (name[0], name[1], o)
                    dve.wait_ge(*full(nm))
                    if name[0] == "down1" or name[1] == 1:
                        dst = x_sb[:, o] if name[0] == "down1" else f_acc[:, o]
                        if nm[0] == "down2":
                            dve.wait_ge(*evacuated(("down2", 0, o)))
                        dve.tensor_tensor(dst, ps(nm)[:], dst, ALU.add).then_inc(*release(nm))
                    else:
                        dve.tensor_copy(f_acc[:, o], ps(nm)[:]).then_inc(*release(nm))
            elif stage == "nsa_apply":
                name = step[1]
                own("rstd", name)
                dst = {"ks": ks_d[:], "kw": kw_d[:], "nq0": nq[:, 0], "nq1": nq[:, 1]}[name]
                w = {"ks": col("nsa_k", 1), "kw": col("nsa_k", 2)}.get(name, col("nsa_q"))
                scaled(name, dst, dst, w).then_inc(*did("rstd_used", name))
                own("rstd_used", name)
            elif stage == "cmp_up":
                kv = step[2]
                for c in range(2):
                    own("cmp_s", kv, c)
                    hcol = cmp_h[:, 2 * kv + c, 0:N_CMP]
                    chain(dve.tensor_scalar(hcol, hcol, 1.0, None, ALU.add))
                    chain(dve.reciprocal(hcol, hcol))
                    dve.tensor_tensor(hcol, ps(("cmp_h", kv, c))[:, 0:N_CMP], hcol, ALU.mult)\
                       .then_inc(*release(("cmp_h", kv, c)))
                    dve.wait_ge(*evacuated(("cmp_h", kv, c)))
            elif stage == "cmp_apply":
                own("rstd", "kcmp")
                scaled("kcmp", cmp_k[:, 1, 0:N_CMP], cmp_k[:, 0, 0:N_CMP], col("nsa_k", 0))\
                    .then_inc(*did("rstd_used", "kcmp"))
                own("rstd_used", "kcmp")
            elif stage == "cmp_softmax":
                dve.wait_ge(*full("cmp_bias"))
                dve.tensor_copy(cmp_bias[:].rearrange("p a b c -> p (a b c)"),
                                ps("cmp_bias")[:, 0:NT * NH * N_CMP]).then_inc(*release("cmp_bias"))
                dve.wait_ge(*evacuated("cmp_bias"))
                p3 = cmp_p[:].rearrange("p a b c -> p (a b) c")
                bc = lambda i: cmp_s[:, i].rearrange("p a b -> p (a b)")[:, :, None].to_broadcast([P, NT * NH, N_CMP])
                dve.wait_ge(*evacuated("cmp_bias"))
                for hf in range(2):
                    n = ("cmp_sc", hf)
                    dve.wait_ge(*full(n))
                    dve.tensor_tensor(cmp_p[:, :, hf:NH:2], ps(n)[:, 0:NT * 2 * N_CMP]
                                      .rearrange("p (a b c) -> p a b c", a=NT, b=2), cmp_bias[:, :, hf:NH:2],
                                      ALU.add).then_inc(*release(n))
                dve.wait_ge(*evacuated(n))
                chain(dve.tensor_reduce(cmp_s[:, 0].rearrange("p a b -> p (a b)"), p3, AX, ALU.max))
                chain(dve.tensor_scalar(cmp_s[:, 0], cmp_s[:, 0], NEG / 10, None, ALU.max))
                dve.tensor_tensor(p3, p3, bc(0), ALU.subtract).then_inc(*did("cmp_v", "l"))
                own("cmp_s", "exp")
                chain(dve.tensor_reduce(cmp_s[:, 1].rearrange("p a b -> p (a b)"), p3, AX, ALU.add))
                chain(dve.tensor_scalar(cmp_s[:, 1], cmp_s[:, 1], 1e-30, None, ALU.max))
                chain(dve.reciprocal(cmp_s[:, 2], cmp_s[:, 1]))
                chain(dve.tensor_tensor(cmp_s[:, 3], cmp_s[:, 2],
                                        gates[:].rearrange("p t (h c) -> p t h c", c=3)[:, :, :, 0], ALU.mult))
                dve.tensor_tensor(p3, p3, bc(3), ALU.mult).then_inc(*did("cmp_v", "p"))
                own("cmp_v", "p")
            elif stage == "att_scores":
                u = step[1]
                A = att(u)
                n = att_at[u]
                L, sm = att_l[:, n % 3, 0:A["w"]], small[:, n % 4]
                dve.wait_ge(*full(("sc", u)))
                if n >= 3:
                    dve.wait_ge(*full(("pt", att_order[n - 3])))
                if n >= 4:
                    own("att_p", att_order[n - 4])
                if n == 0:
                    dve.wait_ge(C.sem["bias_in"], 16 * 2 * NH)
                if u[0] == "swa" and u == ("swa", 0, 0, 0):
                    dve.wait_ge(C.sem["late_in"], 16 * 5)
                dve.tensor_tensor_reduce(L, ps(("sc", u))[:, 0:A["w"]], A["bias"], 1.0, -3.0e38, ALU.add, ALU.max,
                                         sm[:, 0:1]).then_inc(*release(("sc", u)))
                dve.wait_ge(*evacuated(("sc", u)))
                if "sink" in A:
                    dve.tensor_scalar(sm[:, 1:2], sm[:, 0:1], A["sink"], -1.0, ALU.max, ALU.mult)\
                       .then_inc(*did("att_n", u))
                else:
                    dve.tensor_scalar(sm[:, 1:2], sm[:, 0:1], -1.0, None, ALU.mult).then_inc(*did("att_n", u))
            elif stage == "att_turn":
                u = step[1]
                A = att(u)
                n = att_at[u]
                L, sm = att_l[:, n % 3, 0:A["w"]], small[:, n % 4]
                if "sink" in A:
                    own("swa_s", u)
                    chain(dve.tensor_tensor(sm[:, 2:3], sm[:, 2:3], sm[:, 5:6], ALU.add))
                else:
                    own("att_exp", u)
                chain(dve.reciprocal(sm[:, 3:4], sm[:, 2:3]))
                if A["gate"] is not None:
                    dve.tensor_scalar(L, L, sm[:, 3:4], A["gate"], ALU.mult, ALU.mult).then_inc(*did("att_p", u))
                else:
                    dve.tensor_scalar(L, L, sm[:, 3:4], None, ALU.mult).then_inc(*did("att_p", u))
            elif stage == "att_pv":
                u = step[1]
                if u[0] == "swa" and att(u)["bank_last"]:
                    c = u[1]
                    dve.wait_ge(*evacuated(("swa_o", c)))
                    if c == 0:
                        dve.wait_ge(*full(("br", 1, KD - 1)))
                    split(swa_o[:], o_hl[0][:, c], o_hl[1][:, c], "o_ready", 2, c)
            elif stage == "mla_lora":
                own("rstd", "cq")
                for c in range(2):
                    ins = scaled("cq", cq[:, c], cq[:, c], col("mla_qa", c))
                ins.then_inc(*did("rstd_used", "cq"))
                own("rstd_used", "cq")
                own("rstd", "ckv")
                scaled("ckv", ckv[:], ckv[:], col("mla_kv")).then_inc(*did("rstd_used", "ckv"))
                own("rstd_used", "ckv")
            elif stage == "mla_rope_k":
                dve.wait_ge(*evacuated("krs"))
                dve.tensor_tensor(kr[:, 0], kr[:, 0], rope_c[:], ALU.mult)
                chain(dve.tensor_tensor(kr[:, 1], kr[:, 1], rope_s[:], ALU.mult))
                chain(dve.tensor_tensor(kr[:, 0], kr[:, 0], kr[:, 1], ALU.add))
            elif stage == "mla_qk":
                h = step[1]
                dve.wait_ge(*full(("mk", h)))
                dve.tensor_tensor(mk[:, h], ps(("mk", h))[0:QKD, :], kr[:, 0], ALU.add).then_inc(*release(("mk", h)))
                dve.wait_ge(*evacuated(("mk", h)))
                dve.wait_ge(*full(("mq", h, 1)))
                dve.tensor_tensor(mq[:, h], ps(("mq", h, 0))[0:QKD, :], rope_c[:], ALU.mult)\
                   .then_inc(*release(("mq", h, 0)))
                dve.tensor_tensor(tmp[0:QKD, 0], ps(("mq", h, 1))[0:QKD, :], rope_s[:], ALU.mult)\
                   .then_inc(*release(("mq", h, 1)))
                dve.wait_ge(*evacuated(("mq", h, 0)))
                dve.wait_ge(*evacuated(("mq", h, 1)))
                dve.tensor_tensor(mq[:, h], mq[:, h], tmp[0:QKD, 0], ALU.add).then_inc(*did("mla_q", h))
                own("mla_q", h)
                own("rstd", ("mk", h))
                scaled(("mk", h), mk[:, h], mk[:, h], col("mla_k", parts=QKD)).then_inc(*did("rstd_used", ("mk", h)))
                own("rstd", ("mq", h))
                scaled(("mq", h), mq[:, h], mq[:, h], col("mla_q", parts=QKD)).then_inc(*did("rstd_used", ("mq", h)))
                own("rstd_used", ("mq", h))
            elif stage == "sb_scores":
                _, h, kt = step
                w = T - kt * P
                n = sb_order.index((h, kt))
                own("sb_exp", h, kt)
                if h >= 2 and kt == NT - 1:
                    dve.wait_ge(*full(("r", h - 2, 0)))
                sp = sb_sp[:, h % 2, SB_OFF[kt]:SB_OFF[kt] + w]
                dve.scalar_tensor_tensor(out=sp, in0=ps(("z", h, kt))[:, 0:w], scalar=0.0,
                                         in1=sb_e[:, n % 2, 0:w], op0=ALU.max, op1=ALU.add)\
                   .then_inc(*release(("z", h, kt)))
                dve.wait_ge(*evacuated(("z", h, kt)))
                dve.tensor_tensor(sp[:, 0:P], sp[:, 0:P], sbm[:, 2], ALU.mult).then_inc(*did("sb_sp", h, kt))
            elif stage == "ret_scores":
                _, h, jt = step
                w = T - jt * P
                dve.wait_ge(*full(("rs", h, jt)))
                if h >= 1:
                    dve.wait_ge(*full(("ret_o", h - 1, 1)))
                if h == 0 and jt == 0:
                    dve.wait_ge(C.sem["late_in"], 16)
                dve.tensor_tensor(ret_a[:, SB_OFF[jt]:SB_OFF[jt] + w], ps(("rs", h, jt))[:, 0:w], decay[:, h, 0:w],
                                  ALU.mult).then_inc(*release(("rs", h, jt)))
            elif stage == "ret_mean":
                h = step[1]
                dve.wait_ge(*full(("mean", h)))
                dve.tensor_scalar(tmp[:, 0], ps(("mean", h))[:], -1 / 256, None, ALU.mult).then_inc(*release(("mean", h)))
                dve.wait_ge(*evacuated(("mean", h)))
                for e in range(2):
                    if h >= 1:
                        own("ret_done", h - 1, e)
                    dve.tensor_tensor(ret_d[:, e], mix_o[:, e], tmp[:, 0], ALU.add).then_inc(*did("ret_d", h, e))
                own("ret_d", h, 1)
            elif stage in ("ret_out", "gla_out"):
                h = step[1]
                ret = stage == "ret_out"
                key = ("ret" if ret else "gla", h)
                own("rstd", key)
                if not ret and h == 0:
                    dve.wait_ge(*full(("br", 0, KD - 1)))
                for e in range(2):
                    c = 2 * h + e
                    src = ret_d[:, e] if ret else mix_o[:, e]
                    t = tmp[:, e]
                    ins = scaled(key, t, src, col("ret_w" if ret else "gla_w", c))
                    ins.then_inc(*did("ret_done" if ret else "gla_done", h, e))
                    own("ret_done" if ret else "gla_done", h, e)
                    if ret:
                        ins = dve.scalar_tensor_tensor(out=t, in0=t, scalar=col("ret_b", c), in1=silu[:, e],
                                                       op0=ALU.add, op1=ALU.mult)
                    else:
                        ins = dve.tensor_tensor(t, t, silu[:, e], ALU.mult)
                    if e == 1:
                        ins.then_inc(*did("rstd_used", key))
                        own("rstd_used", key)
                    else:
                        chain(ins)
                    split(t, o_hl[0][:, c], o_hl[1][:, c], "o_ready", 0 if ret else 1, c)
            elif stage == "gla_decay":
                h = step[1]
                own("gla_s", "ln", h)
                dve.wait_ge(C.sem["late_in"], 16 * 4)
                g0, g1 = g_ln, g_b
                dve.tensor_scalar(g_eb, ps(("gz", h))[:], col("b_alpha", h), 0.0, ALU.add, ALU.min)\
                   .then_inc(*release(("gz", h)))
                dve.wait_ge(*evacuated(("gz", h)))
                chain(dve.tensor_tensor(g0, g_eb, g0, ALU.subtract))
                chain(dve.tensor_scalar(g0, g0, 1 / 16.0, -1.0, ALU.mult, ALU.max))
                chain(dve.tensor_tensor_scan(g1, gscan[:], g0, 0.0, ALU.mult, ALU.add))
                b4 = g1.rearrange("p (n c) -> p n c", c=GC)
                dve.tensor_tensor(g_ed[:].rearrange("p (n c) -> p n c", c=GC),
                                  b4[:, :, GC - 1:GC].to_broadcast([P, NGC, GC]), b4, ALU.subtract)\
                   .then_inc(*did("gla_v", "d", h))
                if h >= 1:
                    dve.wait_ge(*full(("gla_o", h - 1, 1)))
                own("gla_s", "eb", h)
                dve.tensor_tensor(qf[:, h % 2], qf[:, h % 2], g_eb, ALU.mult)
                own("gla_s", "enb", h)
                dve.tensor_tensor(gk_i[:], kf[:, h % 2], gk_i[:], ALU.mult)
                own("gla_s", "ed", h)
                dve.tensor_tensor(kf[:, h % 2], kf[:, h % 2], g_ed[:], ALU.mult).then_inc(*did("gla_v", "kd", h))
                own("gla_v", "kd", h)
            elif stage == "gla_chunks":
                h = step[1]
                dve.wait_ge(*full(("ga_s", h)))
                dve.tensor_tensor(ga_m, ps(("ga_s", h))[:].rearrange("p (m i) -> p m i", m=NT),
                                  gmask[:, None, :].to_broadcast([P, NT, P]), ALU.mult).then_inc(*release(("ga_s", h)))
                for n in range(NGC - 1):
                    dve.wait_ge(*full(("kv", h, n)))
                    src = ps(("kv", h, n))[:, 0:256]
                    if n == 0:
                        ins = dve.tensor_copy(g_st[:, 0], src)
                    else:
                        dve.wait_ge(*evacuated(("kv", h, n - 1)))
                        a_n = g_eb[:, (n + 1) * GC - 1:(n + 1) * GC]
                        ins = dve.scalar_tensor_tensor(out=g_st[:, n], in0=g_st[:, n - 1], scalar=a_n, in1=src,
                                                       op0=ALU.mult, op1=ALU.add)
                    ins.then_inc(*release(("kv", h, n)))
            elif stage == "merge":
                dve.wait_ge(*full(("br", 2, KD - 1)))
                for c in range(KD):
                    split(merged[:, c], h_hi[:, c], h_lo[:, c], "h_ready", "merge", c)
            elif stage == "residual":
                key = step[1]
                own("rstd", key)
                src = merged
                for c in range(KD):
                    if c >= 2:
                        own("x_ready", key, c - 2)
                    t = tmp[:, c % 2]
                    ins = scaled(key, t, src[:, c], col(key, c))
                    if c == KD - 1:
                        ins.then_inc(*did("rstd_used", key))
                        own("rstd_used", key)
                    else:
                        chain(ins)
                    dve.tensor_tensor(x_sb[:, c], x_sb[:, c], t, ALU.add).then_inc(*did("x_ready", key, c))
                own("x_ready", key, KD - 1)

    @block.gpsimd
    def _(pool):
        for i in range(N_SLOTS):
            pool.wait_ge(C.sem[f"w_landed{i % RAW}"], 16 * (i // RAW + 1))
            if i >= SPL:
                pool.wait_ge(*slot_done[i - SPL])
            hi, lo, raw = w_hi[:, i % SPL], w_lo[:, i % SPL], w_raw[:, i % RAW]
            pool.tensor_scalar(hi, raw, 1.0, 0.0, ALU.mult, ALU.add).then_inc(*did("w_hi", i))
            pool.wait_ge(*after("w_hi", i))
            pool.tensor_tensor(lo, raw, hi.bitcast(F32), ALU.subtract).then_inc(*did("w_lo", i))

    @block.sync
    def _(sp):
        sp.dma_start(x_sb[:], a["x"]).then_inc(C.sem["x_in"], 16)
        n = 0

        def bias_tables():
            for h in range(NH):
                for k, (w, last) in enumerate(((640, ("tab", h, 1)), (1024, ("tab", h, 3)))):
                    for nn in (2 * k, 2 * k + 1):
                        sp.wait_ge(*evacuated(("tab", h, nn)))
                    rows = P if k == 0 else N_CMP
                    dst = a["scratch"][h, k, 0:rows * w].rearrange("(p w) -> p w", w=w)
                    sp.dma_start(dst, tab[0:rows, k, 0:w]).then_inc(C.sem[f"bias_out{k}"], 16)
            for k in range(2):
                sp.wait_ge(C.sem[f"bias_out{k}"], 16 * NH)
            t = a["scratch"].tensor
            for h in range(NH):
                sp.dma_start(toep[:, h], bass.AP(tensor=t, offset=(2 * h) * P * 1024 + P - 1,
                                                 ap=[[640 - 1, P], [1, T]])).then_inc(C.sem["bias_in"], 16)
                sp.dma_start(cb_t[:, h], bass.AP(tensor=t, offset=(2 * h + 1) * P * 1024 + T - CMP_LEN + 1,
                                                 ap=[[1024 - CMP_STRIDE, N_CMP], [1, T]]))\
                  .then_inc(C.sem["bias_in"], 16)

        for step in ORDER:
            stage = step[0]
            name = step[1]
            if stage in ("fm", "tm", "down", "cmp_up"):
                for _ in range(SLOTS[name][1]):
                    if n >= RAW:
                        sp.wait_ge(*after("w_lo", n - RAW))
                    sp.dma_start(w_raw[:, n % RAW], a["w"][n]).then_inc(C.sem[f"w_landed{n % RAW}"], 16)
                    n += 1
                    if n == RAW:
                        bias_tables()
            if name == ("rv", 0):
                sp.wait_ge(*full(("down1", 1, KD - 1)))
                sp.dma_start(decay[:], a["decay"]).then_inc(C.sem["late_in"], 16)
            if name == "ga":
                sp.wait_ge(*after("o_ready", 0, KD - 1))
                sp.wait_ge(C.sem["late_in"], 16)
                for t, src in ((wa2, "wa2"), (gscan, "gscan"), (gmask, "gmask")):
                    sp.dma_start(t[:], a[src]).then_inc(C.sem["late_in"], 16)
                sp.wait_ge(C.sem["late_in"], 16 * 4)
            if name == ("wq", 0):
                sp.wait_ge(*full(("gla_o", 3, 1)))
                sp.wait_ge(*after("o_ready", 1, KD - 1))
                sp.dma_start(alibi[:], a["alibi"]).then_inc(C.sem["late_in"], 16)
        sp.wait_ge(*after("x_ready", "fpost", KD - 1))
        sp.dma_start(a["y"], x_sb[:]).then_inc(C.sem["y_out"], 16)
        sp.wait_ge(C.sem["y_out"], 16)

    return C.at


N_CONST = 5
N_MISC = 10


def _constants():
    f = np.float32
    i = np.arange(P)
    c = {}
    c["ones"] = np.ones((P, P), f)
    c["ones64"] = (i[:, None] // HD == i[None] // HD).astype(f)
    c["ident"] = np.eye(P, dtype=f)
    x = np.arange(T)
    c["causal"] = np.where(x[None] - (T - P) <= i[:, None], 0.0, NEG).astype(f)
    c["sbm"] = np.stack([-(i[:, None] >= i[None]).astype(f), -np.ones((P, P), f), (i[None] > i[:, None]).astype(f),
                         np.where(i[None] > i[:, None], 0.0, NEG).astype(f)], axis=1)
    exact = N_BUCKETS // 2
    dist = np.concatenate([T - 1 - np.arange(640), np.arange(1024) - T])
    d = np.maximum(dist, 1).astype(f)
    large = exact + (np.log(d / f(exact)) / f(np.log(128 / exact)) * f(N_BUCKETS - exact)).astype(np.int32)
    bucket = np.where(dist < exact, dist, np.minimum(large, N_BUCKETS - 1))
    bucket = np.where(dist < 0, N_BUCKETS, bucket)
    c["onehot"] = (np.arange(N_BUCKETS + 1)[:, None] == bucket[None]).astype(f)
    inv = (1.0 / (f(10000.0) ** (np.arange(0, 32, 2, dtype=f) / f(32)))).astype(f)
    ang = np.arange(T, dtype=f)[None] * inv[:, None]
    cos, sin = np.cos(ang), np.sin(ang)
    c["rope_c"] = np.concatenate([np.ones((HD, T), f), cos, cos]).astype(f)
    c["rope_s"] = np.concatenate([np.zeros((HD, T), f), -sin, sin]).astype(f)
    log_g = np.log1p(-np.exp2(-5.0 - np.arange(4)))
    rel = (x[None] - i[:, None])
    c["decay"] = np.stack([np.where(rel >= 0, np.exp(rel * g), 0.0) * P ** -0.5 for g in log_g], axis=1).astype(f)
    c["gscan"] = np.broadcast_to((x % GC != 0).astype(f), (P, T))
    c["gmask"] = ((i[:, None] // GC == i[None] // GC) & (i[:, None] <= i[None])).astype(f)
    slope = np.exp2(-8.0 * np.arange(1, 17) / 16)
    dd = P + i[:, None] - np.arange(2 * P)[None]
    c["alibi"] = np.stack([np.where((dd >= 0) & (dd < P), -slope[SWA_HEAD[k // 2][k % 2]] * dd, NEG)
                           for k in range(16)], axis=1).astype(f)
    return c


def _fm(w):
    n = w.shape[1] // P
    return w.reshape(KD, P, n, P).transpose(2, 1, 0, 3).reshape(n, P, 1024)


def _tm(w, per):
    w = np.pad(w, ((0, 0), (0, 1024 // per - w.shape[1])))
    return w.reshape(KD // per, per, P, 1024 // per).transpose(0, 2, 1, 3).reshape(KD // per, P, 1024)


def _down(w):
    nk = w.shape[0] // P
    blocks = w.reshape(nk, P, KD, P).transpose(2, 0, 1, 3).reshape(KD * nk, P, P)
    return blocks.reshape(-1, 8, P, P).transpose(0, 2, 1, 3).reshape(-1, P, 1024)


def _weights(v):
    w1 = v["w_in"][0]
    sizes = [256] * 3 + [256] + [64] * 6 + [12] + [192, 128, 32] + [256] * 3
    at = np.concatenate([[0], np.cumsum(sizes)])
    ab, ac, au, nq, kc, vc, ks, vs, kw, vw, ng, cq, ckv, kr, sq, sk, sv = [
        w1[:, at[i]:at[i + 1]] for i in range(len(sizes))]
    zeros = lambda n: np.zeros((D, n), w1.dtype)
    one = lambda w: _fm(w)[0]
    slot = {"ks": one(np.concatenate([ks, ks], 1)), "kw": one(np.concatenate([kw, kw], 1)),
            "kc": one(np.concatenate([kc, kc], 1)), "vc": one(np.concatenate([vc, vc], 1)),
            "cq0": one(cq[:, :P]), "cq1": one(np.concatenate([cq[:, P:], zeros(64)], 1)), "ckv": one(ckv),
            "kr": one(np.concatenate([zeros(HD), kr, zeros(32)], 1)),
            "krs": one(np.concatenate([zeros(HD), kr[:, 16:], kr[:, :16], zeros(32)], 1))}
    for c in range(2):
        cc = slice(c * P, (c + 1) * P)
        slot.update({f"nq{c}": one(nq[:, cc]), f"sq{c}": one(sq[:, cc]), f"sk{c}": one(sk[:, cc]),
                     ("ab", c): one(ab[:, cc]), ("ac", c): one(ac[:, cc]), ("au", c): one(au[:, cc])})
    slot["v1"] = _tm(np.concatenate([vs, vw, sv, ng], 1), 2)
    for kv in range(2):
        slot[("cmp", kv)] = v["cmp_w1"][0, kv].reshape(4, 4, P, 256).transpose(0, 2, 1, 3).reshape(4, P, 1024)
    for c, s in enumerate(_fm(v["w_out"][0])):
        slot[("wout", c)] = s
    for half in range(2):
        for c in range(HALF1):
            g = half * HALF1 + c
            slot[("up1", half, c)] = one(v["ffn_w1"][0][:, g * P:(g + 1) * P])
        slot[("down1", half)] = _down(v["ffn_w2"][0][half * HALF1 * P:(half + 1) * HALF1 * P])
    w2 = v["w_in_2"][0]
    sizes = [512, 512, 1024, 1024, 512, 512, 1024, 1024, 16, 1024, 256, 256, 3072]
    at = np.concatenate([[0], np.cumsum(sizes)])
    rq, rk, rv, rg, gq, gk, gv, gg, ga, sq, sk, sv, gate = [w2[:, at[i]:at[i + 1]] for i in range(len(sizes))]
    for h in range(4):
        for name, w in (("rq", rq), ("rk", rk), ("gq", gq), ("gk", gk)):
            slot[(name, h)] = one(w[:, h * P:(h + 1) * P])
        for name, w in (("rg", rg), ("gg", gg)):
            for e in range(2):
                slot[(name, h, e)] = one(w[:, (2 * h + e) * P:(2 * h + e + 1) * P])
    for g in range(2):
        slot[("rv", g)] = _tm(rv[:, g * 512:(g + 1) * 512], 2)
        slot[("gv", g)] = _tm(gv[:, g * 512:(g + 1) * 512], 2)
    slot["ga"] = one(np.concatenate([ga, zeros(P - 16)], 1))
    pairs = [h for c in SWA_HEAD for h in c]
    sq = sq.reshape(D, 16, HD)[:, pairs].reshape(D, 1024)
    for c in range(8):
        slot[("wq", c)] = one(sq[:, c * P:(c + 1) * P])
    for c in range(2):
        slot[("wk", c)] = one(sk[:, c * P:(c + 1) * P])
    slot["wv"] = _tm(sv, 4)
    for b in range(3):
        wb = v["w_branch_2"][0, b]
        if b == 2:
            wb = wb.reshape(16, HD, D)[pairs].reshape(1024, D)
        for m in range(KD):
            mm = slice(m * P, (m + 1) * P)
            slot[("gate", b, m)] = one(gate[:, b * D:(b + 1) * D][:, mm])
            slot[("br", b, m)] = one(wb[:, mm])
    for c, s in enumerate(_fm(v["w_out_2"][0])):
        slot[("wout2", c)] = s
    for half in range(2):
        for c in range(HALF2):
            g = slice((half * HALF2 + c) * P, (half * HALF2 + c + 1) * P)
            slot[("fg", half, c)] = one(v["ffn_w_gate_2"][0][:, g])
            slot[("fu", half, c)] = one(v["ffn_w_up_2"][0][:, g])
        slot[("down2", half)] = _down(v["ffn_w_down_2"][0][half * HALF2 * P:(half + 1) * HALF2 * P])
    return np.concatenate([slot[name].reshape(n, P, 1024) for name, (_, n) in SLOTS.items()])


def _params(v):
    f = v["x"].dtype
    cols = lambda w: np.pad(w, (0, -len(w) % P)).reshape(-1, P).T
    twice = lambda w: np.concatenate([w, w])[:, None]
    pos = v["cmp_pos"][0].reshape(2, 16, P)
    parts = [cols(v["norm1_w"][0]),
             np.concatenate([cols(v["conv_w"][0, k]) for k in range(3)], 1), cols(v["conv_b"][0]),
             twice(v["nsa_q_norm"][0]), np.concatenate([twice(v["nsa_k_norm"][0, k]) for k in range(3)], 1),
             cols(v["mla_q_a_norm"][0]), cols(v["mla_kv_norm"][0]), cols(v["mla_q_norm"][0]),
             cols(v["mla_k_norm"][0]), cols(v["out_norm_w"][0]), cols(v["norm2_w"][0]),
             pos.reshape(32, P).T, cols(v["norm_mix_pre_2"][0]), cols(v["norm_mix_post_2"][0]),
             cols(v["ret_norm_w_2"][0]), cols(v["ret_norm_b_2"][0]), cols(v["gla_b_alpha_2"][0]),
             cols(v["gla_norm_w_2"][0]), cols(v["norm_ffn_pre_2"][0]), cols(v["norm_ffn_post_2"][0]),
             np.broadcast_to(v["attn_sinks_2"][0][[h for c in SWA_HEAD for h in c]][None], (P, 16))]
    return np.ascontiguousarray(np.concatenate(parts, axis=1).astype(f))


def _arrays(v):
    f = np.float32
    out = dict(_constants())
    out["x"] = v["x"][0].reshape(T, KD, P).transpose(2, 1, 0)
    out["w"] = _weights(v)
    out["par"] = _params(v)
    out["rel_bias"] = v["rel_bias"]
    w2 = v["cmp_w2"][0]
    out["w2k"] = np.concatenate([w2[0], w2[0]], 1).reshape(2, P, P).transpose(1, 0, 2)
    out["w2v"] = w2[1].reshape(2, P, HD).transpose(1, 0, 2)
    wqb = v["mla_wq_b"][0].reshape(192, NH, QKD)
    turned = np.concatenate([wqb[:, :, :HD], wqb[:, :, HD + 16:], wqb[:, :, HD:HD + 16]], axis=2)
    both = np.pad(np.stack([wqb, turned], 1), ((0, 64), (0, 0), (0, 0), (0, 0)))
    out["wqb"] = both.reshape(2, P, 2, NH, QKD).transpose(1, 0, 2, 3, 4)
    wkv = v["mla_wkv_b"][0].reshape(P, NH, 2 * HD)
    out["wkb"] = np.pad(wkv[:, :, :HD], ((0, 0), (0, 0), (0, 32)))
    out["wvb"] = wkv[:, :, HD:].reshape(P, NH * HD)
    out["wa2"] = v["gla_w_alpha2_2"][0]
    return {k: np.ascontiguousarray(t) for k, t in out.items()}


def _program_in(nc, arrays, known):
    a = {k: nc.dram_tensor(f"in_{k}", t.shape, mybir.dt.from_np(t.dtype), kind="ExternalInput").ap()
         for k, t in arrays.items()}
    a["scratch"] = nc.dram_tensor("scratch", (NH, 2, P * 1024), F32, kind="Internal").ap()
    a["y"] = nc.dram_tensor("out_y", (P, KD, T), F32, kind="ExternalOutput").ap()
    return build(nc, a, known)


def kernel(**inputs):
    import concourse.bacc as _bacc
    from concourse.bass_utils import run_bass_kernel_spmd as _run

    arrays = _arrays({k: np.asarray(t) for k, t in inputs.items()})
    counting = _bacc.Bacc("TRN2", target_bir_lowering=False, num_devices=1)
    counts = _program_in(counting, arrays, {})
    nc = _bacc.Bacc("TRN2", target_bir_lowering=False, num_devices=1)
    _program_in(nc, arrays, counts)
    r = _run(nc, [{f"in_{k}": t for k, t in arrays.items()}], core_ids=[0])
    y = r.results[0]["out_y"]
    return np.ascontiguousarray(y.transpose(2, 1, 0).reshape(1, T, D))
```

```python
from contextlib import ExitStack

import numpy as np

import concourse.bass as bass
from concourse import mybir

ALU = mybir.AluOpType
ACT = mybir.ActivationFunctionType
F32 = mybir.dt.float32
F32R = mybir.dt.float32r
AX = mybir.AxisListType.X

P = 128
T = 512
NT = T // P
D = 1024
KD = D // P
EPS = 1e-6
GN_EPS = 1e-5
NEG = -1.0e30
CMP_LEN, CMP_STRIDE = 32, 16
N_CMP = (T - CMP_LEN) // CMP_STRIDE + 1
NH = 4
HD = 64
N_BUCKETS = 32
QKD = 96
F1 = 4 * D // P
HALF1 = F1 // 2
F2 = 2816 // P
HALF2 = F2 // 2
GC = 64
NGC = T // GC
RAW = 3
SPL = 3

PCOL = {}


def _columns():
    at = 0
    for name, n in (("norm1", 8), ("conv_w", 6), ("conv_b", 2), ("nsa_q", 1), ("nsa_k", 2), ("mla_qa", 2),
                    ("mla_kv", 1), ("mla_q", 1), ("mla_k", 1), ("out_norm", 8), ("norm2", 8), ("pos", 32),
                    ("pre", 8), ("post", 8), ("ret_w", 8), ("ret_b", 8), ("b_alpha", 4), ("gla_w", 8),
                    ("fpre", 8), ("fpost", 8), ("sinks", 16), ("head_of", 4)):
        PCOL[name] = at
        at += n
    return at


NPCOL = _columns()
SWA_HEAD = [[(2 * (c // 4) + hf) * 4 + c % 4 for hf in range(2)] for c in range(8)]


def plan():
    order, slots = [], {}

    def lin(name, kind, n_slots, *args):
        slots[name] = (sum(n for _, n in slots.values()), n_slots)
        order.append((kind, name) + args)

    def fm(name, src="h"):
        lin(name, "fm", 1, src)

    def together(names, src="h"):
        first = len(order)
        for name in names:
            fm(name, src)
        ends = order[first:]
        del order[first:]
        return (lambda k0, k1: ("fmk", tuple(names), src, k0, k1)), ends

    def quarters(name, src="h"):
        def quarter(k):
            if k == 0:
                held.extend(together([name], src))
            order.append(held[0](k, k + 2))
            if k + 2 == KD:
                order.extend(held[1])
        held = []
        return [lambda k=k: quarter(k) for k in range(0, KD, 2)]

    def tm(name, ns, cols):
        return [lambda s=s: lin((name, "s", s), "tm", 1, name, cols, s, ns) for s in range(ns)]

    def sqs(key, n):
        return [("sq", key, c) for c in range(n)]

    def attention(units):
        n, steps = len(units), []
        for i in range(n + 3):
            for lag, stage in enumerate(("att_scores", "att_norm", "att_turn", "att_pv")):
                if 0 <= i - lag < n:
                    steps.append((stage, units[i - lag]))
        return steps

    def weave(main, filler):
        n = 0
        for i, step in enumerate(main):
            put(step)
            while n < len(filler) and n * len(main) < (i + 1) * len(filler):
                put(filler[n])
                n += 1
        for step in filler[n:]:
            put(step)

    def put(step):
        if callable(step):
            step()
        else:
            order.append(step)

    def F(name, src="h"):
        return lambda: fm(name, src)

    def run(steps):
        for step in steps:
            put(step)

    def down(name, nk, key):
        slots[name] = (sum(n for _, n in slots.values()), KD * nk // 8)
        for o in range(KD):
            order.append(("down", name, nk, o))
            if name[1] == 1:
                order.append(("sq", key, o))

    run(sqs("n1", KD) + [("norm", "n1"), ("bias_tables", 0), ("apply_h", "n1", "norm1")])
    part, ends = together(("kvc", "ksw", "nq0"))
    run([part(0, KD)] + ends)

    def U(kv, s):
        return lambda: lin(("cmp", kv, s), "cmp_up", 1, kv, s)

    v1 = tm("v1", 4, 396)
    run([("sq", "ksw", 0), F("nq1"), ("sq", "nq0", 0), ("norm", "ksw"), ("cmp_x", 0), ("nsa_apply", "ksw"),
         F("cq0"), ("sq", "nq1", 0), ("norm", "nq0"), ("cmp_x", 1), ("nsa_apply", "nq0"),
         U(0, 0), F("cqr"), ("norm", "nq1"), ("nsa_apply", "nq1"), ("sq", "cq", 0), ("sq", "cq", 1),
         U(0, 1), F("ckv"), ("norm", "cq"), ("sq", "ckv", 0),
         U(0, 2), F("sq0"), ("norm", "ckv"), ("mla_lora", 0), U(0, 3), F("sq1"), ("mla_rope_k", 0),
         U(1, 0), F("sk0"), U(1, 1), F("sk1"), U(1, 2), v1[0], U(1, 3), v1[1], v1[2], v1[3]])
    filler = []
    for h in range(NH):
        lin4 = quarters((("ac", 0), ("au", 0), ("ab", 0), ("ac", 1))[h])
        filler += [("mla_qk", h), ("sq", ("mk", h), 0), ("sq", ("mq", h), 0)] + lin4[:2] + [("norm", ("mk", h))] +\
            lin4[2:] + [("norm", ("mq", h)), ("mla_scale", h)]
    filler += quarters(("au", 1)) + quarters(("ab", 1))
    run([("cmp_bias", 0), ("cmp_down", 0), ("sq", "kcmp", 0), ("mla_v", 0)] + filler[:5] + [("norm", "kcmp"), ("cmp_apply", 0)] +
        filler[5:10] + [("cmp_scores", 0)] + filler[10:16] + [("cmp_turn", 0)])
    filler = filler[16:]
    pairs = [(pair, qt, hf) for pair in range(2) for qt in range(NT) for hf in range(2)]
    weave(attention([(kind, 2 * pair + hf, qt) for pair, qt, hf in pairs for kind in ("slc", "win")]), filler)
    order.append(("x_again", 0))
    tiles = [(h, kt) for h in range(NH) for kt in reversed(range(NT))]
    sbs = []
    for n in range(len(tiles) + 2):
        if n < len(tiles):
            sbs.append(("sb_scores",) + tiles[n])
        if n >= 2 and (n - 2) % NT == NT - 1:
            sbs.append(("sb_pv", tiles[n - 2][0]))
        if 1 <= n <= len(tiles):
            sbs.append(("sb_exp",) + tiles[n - 1])
    cut = 3 * len(sbs) // 4
    outs = [sqs(("y", 0), 2), [("norm", ("y", 0))] + sqs(("y", 1), 2), [("y_out", 0), ("norm", ("y", 1))],
            [("y_out", 1)]]
    weave(attention([("mla", 2 * pair + hf, qt) for pair, qt, hf in pairs]),
          sbs[:2] + outs[0] + sbs[2:4] + outs[1] + sbs[4:6] + outs[2] + sbs[6:8] + outs[3] + sbs[8:cut])
    run(sbs[cut:cut + 1] + sqs(("y", 2), 2) + sbs[cut + 1:cut + 3] + [("norm", ("y", 2))] + sbs[cut + 3:cut + 4] +
        [("y_out", 2)] + sbs[cut + 4:-2])
    part, ends = together([("wout", c) for c in range(3)])
    run([part(0, 3), sbs[-2], part(3, 4), sbs[-1], ("x_again", 1)] + sqs(("y", 3), 2) +
        [part(4, 6), ("norm", ("y", 3)), ("y_out", 3), part(6, KD)])
    for c in range(KD):
        run(ends[c:c + 1] or [F(("wout", c))])
        order.append(("sq", "n2", c))
    order.append(("norm", "n2"))
    order.append(("apply_h", "n2", "norm2"))
    part, ends = together([("up1", 0, c) for c in range(3)])
    run([part(0, KD)] + ends)
    for half in range(2):
        for c in range(3 * (half == 0), HALF1):
            fm(("up1", half, c))
        down(("down1", half), HALF1, "pre")

    def branch(b, after_gates=(), whole=lambda name, src="h": [F(name, src)]):
        steps = whole(("gate", b, 0)) + whole(("gate", b, 1)) + list(after_gates)
        for m in range(KD):
            steps += whole(("br", b, m), "o")
            if m + 2 < KD:
                steps += whole(("gate", b, m + 2))
        return steps

    order.append(("norm", "pre"))
    order.append(("apply_h", "pre", "pre"))
    part, ends = together([("rq", 0), ("rk", 0), ("rq", 1)])
    run([part(0, KD)] + ends + tm(("rv", 0), 4, 512))
    for h in range(4):
        run([("ret_scores", h, jt) for jt in range(NT)])
        if h:
            put(("ret_out", h - 1))
        run([F(("rg", h, 0)), ("ret_pv", h), F(("rg", h, 1)), ("ret_mean", h)])
        if h < 3:
            run(([F(("rq", h + 1))] if h else []) + sqs(("ret", h), 2) + [F(("rk", h + 1)), ("norm", ("ret", h))])
        if h == 1:
            run(tm(("rv", 1), 4, 512))
    steps = branch(0)
    run(steps[:1] + sqs(("ret", 3), 2) + steps[1:2] + [("norm", ("ret", 3)), ("ret_out", 3), F("ga"), F(("gq", 0))] +
        steps[2:] + tm(("gv", 0), 4, 512) + [F(("gk", 0)), ("gla_decay", 0), ("gla_scale", 0)])
    for h in range(4):
        nxt = (("gq", h + 1), ("gk", h + 1)) if h < 3 else (("wq", 0), ("wq", 1))
        run([F(("gg", h, 0)), F(("gg", h, 1)), ("gla_turn", h), F(nxt[0]), ("gla_chunks", h)])
        if h == 1:
            run(tm(("gv", 1), 4, 512))
        run(sqs(("gla", h), 2) + [F(nxt[1]), ("norm", ("gla", h))])
        if h < 3:
            put(("gla_decay", h + 1))
        put(("gla_out", h))
        if h < 3:
            put(("gla_scale", h + 1))
    run([F(("wk", c)) for c in range(2)] + tm("wv", 2, 256))
    filler = branch(1, whole=quarters)
    for c, at in ((2, 3), (3, 6), (4, 8), (5, 11), (6, 14), (7, 16)):
        filler[4 * at:4 * at] = quarters(("wq", c))
    weave(attention([("swa", c, hf, qt) for c in range(8) for qt in range(NT) for hf in range(2)]), filler)
    run(branch(2, [("swa_split", 0)]))
    for c in range(KD):
        run([F(("wout2", c), "m"), ("sq", "post", c)])
    order.append(("norm", "post"))
    for c in range(KD):
        run([("residual", "post", c), ("sq", "fpre", c)])
    order.append(("norm", "fpre"))
    order.append(("apply_h", "fpre", "fpre"))
    part, ends = together([("fg", 0, 0), ("fu", 0, 0), ("fg", 0, 1)])
    run([part(0, KD)] + ends + [F(("fu", 0, 1))])
    for half in range(2):
        for c in range(2 * (half == 0), HALF2):
            fm(("fg", half, c))
            fm(("fu", half, c))
        down(("down2", half), HALF2, "fpost")
    order.append(("norm", "fpost"))
    for c in range(KD):
        order.append(("residual", "fpost", c))
    return order, slots


ORDER, SLOTS = plan()
N_SLOTS = sum(n for _, n in SLOTS.values())
TOGETHER = {name for step in ORDER if step[0] == "fmk" for name in step[1]}
PE_SUM = ("fpre",)

SEMAPHORES = """x_in0 x_in1 x_in2 x_in3 x_back mixer_in kv_in ksw_in kr_in zeros table_out sq_pe const_in wqb_in misc_in late_in bias_out0 bias_out1 bias_in y_out
w_hi w_lo slot_used v_chain s_chain sq_s sq_v rstd rstd_used ms_lo
h_ready bias_v bcast_v gate_v nsa_v cmpx cmp_s cmp_v att_l att_n att_exp att_p att_tr att_done
lora mla_k mla_q mla_rot sb_sp sb_exp sb_a sb_pe conv_v y_ready hid_s hid x_ready ret_a ret_d ret_done sil
o_ready m_ready gla_v gla_s gla_kd gla_st gla_a gla_done prod gate_s merged merged_hl q_s swa_s ft lo_t table""".split()


class Counts:

    def __init__(self, known):
        self.known = known
        self.at = {}
        self.n = {}
        self.sem = {}

    def did(self, name, *key, by=1):
        self.n[name] = self.n.get(name, 0) + by
        assert (name, key) not in self.at, (name, key)
        self.at[(name, key)] = self.n[name]
        return self.sem[name], by

    def after(self, name, *key):
        v = self.at.get((name, key)) or self.known.get((name, key))
        assert v or not self.known, (name, key)
        return self.sem[name], v or 1


def build(nc, a, known):
    ctx = ExitStack()
    with ctx:
        return _program(ctx, nc, a, known)


def _program(ctx, nc, a, known):
    C = Counts(known)
    did, after = C.did, C.after
    for name in SEMAPHORES:
        C.sem[name] = ctx.enter_context(nc.semaphore(name))
    for s in range(RAW):
        C.sem[f"w_landed{s}"] = ctx.enter_context(nc.semaphore(f"w_landed{s}"))
    for c in range(8):
        C.sem[f"alibi_in{c}"] = ctx.enter_context(nc.semaphore(f"alibi_in{c}"))
    for b in range(8):
        for what in ("bank_full", "bank_free"):
            C.sem[f"{what}{b}"] = ctx.enter_context(nc.semaphore(f"{what}{b}"))

    def sb(name, shape, dt=F32):
        return ctx.enter_context(nc.sbuf_tensor(name, shape, dt))

    bank = [ctx.enter_context(nc.psum_tensor(f"bank{b}", [P, 512], F32)) for b in range(8)]

    x_sb = sb("x_sb", [P, KD, T])
    h_hi, h_lo = sb("h_hi", [P, KD, T], F32R), sb("h_lo", [P, KD, T], F32R)
    w_raw = sb("w_raw", [P, RAW, 1024])
    w_hi, w_lo = sb("w_hi_t", [P, SPL, 1024], F32R), sb("w_lo_t", [P, SPL, 1024], F32R)
    par = sb("par", [P, NPCOL])
    ones = sb("ones", [P, P])
    ones64 = sb("ones64", [P, P])
    ident = sb("ident", [P, P])
    causal = sb("causal", [P, T])
    sq = sb("sq", [P, 2, T])
    sq_sum = sb("sq_sum", [P, T])
    rstd_t = sb("rstd_t", [P, 3, T])
    tmp = sb("tmp", [P, 2, T])
    att_l = sb("att_l_t", [P, 3, T])
    att_pt = sb("att_pt", [P, 2, T])
    small = sb("small", [P, 4, 8])
    epst = sb("epst", [P, 8])

    area = ExitStack()

    def sa(name, shape, dt=F32):
        return area.enter_context(nc.sbuf_tensor(name, shape, dt))

    y = sa("y", [P, KD, T])
    v1 = sa("v1", [P, NT, 396])
    gates = sa("gates", [P, NT, 12])
    rb = sa("rb", [N_BUCKETS + 1, NH])
    w2k, w2v = sa("w2k", [P, 2, P]), sa("w2v", [P, 2, HD])
    wqb = sa("wqb", [P, 2, 2, NH, QKD])
    wkb = sa("wkb", [P, NH, QKD])
    wvb = sa("wvb", [P, NH * HD])
    rope_c, rope_s = sa("rope_c", [QKD, T]), sa("rope_s", [QKD, T])
    sbm = sa("sbm", [P, 4, P])
    part = ExitStack()

    def sp_(name, shape, dt=F32):
        return part.enter_context(nc.sbuf_tensor(name, shape, dt))

    nq, ks_d, kw_d, s_qk = x_sb[:, 0:2], x_sb[:, 2], x_sb[:, 3], x_sb[:, 4:8]
    cq, kr = y[:, 4:6], y[0:QKD, 6:8]
    conv_t = sa("conv_t", [P, 2, 2 + T])
    cmp_pt = sa("cmp_pt_t", [P, NT, P])
    tab = sp_("tab", [NH, 640 + 1024])
    part.close()
    cmp_x = [sp_("cmp_xh", [P, 2, 16, 32], F32R), sp_("cmp_xl", [P, 2, 16, 32], F32R)]
    mla_first = ExitStack()

    def sm_(name, shape, dt=F32):
        return mla_first.enter_context(nc.sbuf_tensor(name, shape, dt))

    onehot = sm_("onehot", [N_BUCKETS + 1, 640 + 1024])
    cb_t = sm_("cb_t", [N_CMP, NH, T])
    mla_first.close()
    kv_raw = sm_("kv_raw", [P, 2, T])
    mla_first.close()
    part.close()
    mk = sp_("mk", [P, NH, T])
    mv = sp_("mv", [P, NT, NH * HD])
    ckv = sp_("ckv", [P, T])
    sp_("rest of onehot", [P, 640 + 1024 - 1536])
    mq = sp_("mq", [P, NH, T])
    nsa = ExitStack()

    def sn(name, shape, dt=F32):
        return nsa.enter_context(nc.sbuf_tensor(name, shape, dt))

    toep = sn("toep", [P, NH, T])
    cmp_bias = sn("cmp_bias_t", [P, NT, NH, N_CMP])
    cmp_h = sn("cmp_h", [P, 4, 32])
    cmp_k = sn("cmp_k_t", [P, 2, 32])
    cmp_hv = sn("cmp_hv", [P, 2, NH, 32])
    cmp_vt = sn("cmp_vt_t", [P, NH, HD])
    cmp_p = sn("cmp_p", [P, NT, NH, 32])
    cmp_s = sn("cmp_s_t", [P, 4, NT, NH])
    nsa.close()
    sb_e = sn("sb_e", [P, 2, T])
    sb_sp = sn("sb_sp_t", [P, 2, 1280])
    sb_a = sn("sb_a_t", [P, 2, 1280])
    nsa.close()
    part.close()
    area.close()

    hid1 = [area.enter_context(nc.sbuf_tensor(n, [P, HALF1, T], F32R)) for n in ("hid1_hi", "hid1_lo")]
    r1 = sa("r1", [P, 2, T])
    area.close()

    merged = sa("merged_t", [P, KD, T])
    sig = sa("sig", [P, 2, T])
    mixers = ExitStack()
    o_hl = [mixers.enter_context(nc.sbuf_tensor(n, [P, KD, T], F32R)) for n in ("o_hi", "o_lo")]
    inner = ExitStack()

    def si(name, shape, dt=F32):
        return inner.enter_context(nc.sbuf_tensor(name, shape, dt))

    qf, kf = si("qf", [P, 2, T]), si("kf", [P, 2, T])
    vt = si("vt", [P, NT, 512])
    silu = si("silu", [P, 2, T])
    mix_o = si("mix_o", [P, 2, T])
    fp = ExitStack()

    def sg(name, shape, dt=F32):
        return fp.enter_context(nc.sbuf_tensor(name, shape, dt))

    decay = sg("decay", [P, 4, T])
    ret_a = sg("ret_a_t", [P, 1280])
    ret_d = sg("ret_d_t", [P, 2, T])
    fp.close()
    ga_t = sg("ga_t", [16, T])
    wa2 = sg("wa2", [16, T])
    gscan = sg("gscan", [P, T])
    gmask = sg("gmask", [P, P])
    gk_i = sg("gk_i", [P, T])
    g_ed = sg("g_ed", [P, T])
    g_st = sg("g_st", [P, NGC - 1, 256])
    fp.close()
    g_ln, g_b, g_eb = att_l[:, 0], att_l[:, 1], att_l[:, 2]
    gk_t = att_pt[:, 0].rearrange("p (m k) -> p m k", m=NT)
    ga_m = att_pt[:, 1].rearrange("p (m i) -> p m i", m=NT)
    inner.close()
    wq = si("wq", [P, 8, T])
    wk = si("wk", [P, 2, T])
    wv = si("wv", [P, NT, 256])
    alibi = si("alibi", [P, 16, 256])
    swa_o = wq
    inner.close()
    m_hl = [si("m_hi", [P, KD, T], F32R), si("m_lo", [P, KD, T], F32R)]
    inner.close()
    mixers.close()
    f_acc = merged
    hid2 = [si("hid2_hi", [P, HALF2, T], F32R), si("hid2_lo", [P, HALF2, T], F32R)]
    sig2 = si("sig2", [P, 2, T])
    inner.close()
    area.close()

    lin_src = {"h": (h_hi, h_lo), "o": o_hl, "m": m_hl}

    def col(name, c=0, n=1, parts=P):
        return par[0:parts, PCOL[name] + c:PCOL[name] + c + n]

    tenants = {}
    n_tenants = [0] * 8
    turn = {"lin": 0, "att": 0}
    pools = {"lin": [0, 1, 2, 3], "att": [5, 6, 7], "out": [4]}

    def full(name):
        b, k = tenants[name]
        return C.sem[f"bank_full{b}"], k + 1

    def evacuated(name):
        b, k = tenants[name]
        return C.sem[f"bank_free{b}"], k + 1

    def release(name):
        return C.sem[f"bank_free{tenants[name][0]}"], 1

    def ps(name):
        return bank[tenants[name][0]]

    slot_done = {}

    def ev(name):
        return ("bank", name)

    norms = {
        "n1": ([x_sb[:, c] for c in range(KD)], P, T, ones, 1 / D, "eps", [("x", c // 2) for c in range(KD)]),
        "n2": ([x_sb[:, c] for c in range(KD)], P, T, ones, 1 / D, "eps", [ev(("wout", c)) for c in range(KD)]),
        "pre": ([x_sb[:, c] for c in range(KD)], P, T, ones, 1 / D, "eps",
                [ev(("down1", 1, c)) for c in range(KD)]),
        "post": ([merged[:, c] for c in range(KD)], P, T, ones, 1 / D, "eps",
                 [ev(("wout2", c)) for c in range(KD)]),
        "fpre": ([x_sb[:, c] for c in range(KD)], P, T, ones, 1 / D, "eps",
                 [("ev", "x_ready", "post", c) for c in range(KD)]),
        "fpost": ([f_acc[:, c] for c in range(KD)], P, T, ones, 1 / D, "eps",
                  [ev(("down2", 1, c)) for c in range(KD)]),
        "ksw": ([ks_d], P, T, ones64, 1 / HD, "eps", [ev("ksw")]),
        "nq0": ([nq[:, 0]], P, T, ones64, 1.0, "eps*64", [ev("nq0")]),
        "nq1": ([nq[:, 1]], P, T, ones64, 1.0, "eps*64", [ev("nq1")]),
        "kcmp": ([cmp_k[:, 0, 0:N_CMP]], P, N_CMP, ones64, 1 / HD, "eps", [ev("cmp_k")]),
        "cq": ([cq[:, c] for c in range(2)], P, T, ones, 1 / 192, "eps", [ev("cq0"), ev("cqr")]),
        "ckv": ([ckv[:]], P, T, ones, 1 / P, "eps", [ev("ckv")]),
    }
    for h in range(NH):
        norms[("mk", h)] = ([mk[0:QKD, h]], QKD, T, ones, 1 / QKD, "eps", [ev(("mk", h))])
        norms[("mq", h)] = ([mq[0:QKD, h]], QKD, T, ones, 1.0, "eps*96", [("ev", "mla_q", h)])
        norms[("ret", h)] = ([ret_d[:, e] for e in range(2)], P, T, ones, 1 / 256, "gn_eps",
                             [("ev", "ret_d", h, e) for e in range(2)])
        norms[("gla", h)] = ([mix_o[:, e] for e in range(2)], P, T, ones, 1 / 256, "eps",
                             [ev(("gla_o", h, e)) for e in range(2)])
    for g in range(4):
        srcs = ([("ev", "conv_v", c) for c in range(2)] if g == 0 else
                [ev(({1: "nsa_o", 2: "mla_o"}[g], c) if g < 3 else ("sb_o", 2 * c + 1)) for c in range(2)])
        norms[("y", g)] = ([y[:, 2 * g + c] for c in range(2)], P, T, ones, 1 / 256, "eps", srcs)
    EPS_COL = {"eps": 0, "eps*64": 1, "eps*96": 2, "gn_eps": 3}
    EPS_VAL = [EPS, EPS * HD, EPS * QKD, GN_EPS]

    norm_order = []
    for step in ORDER:
        if step[0] == "norm":
            norm_order.append(step[1])
    norm_at = {k: i for i, k in enumerate(norm_order)}
    sq_use = {}
    for step in ORDER:
        if step[0] == "sq":
            sq_use[step[1:]] = len(sq_use)
    sq_uses = list(sq_use)

    def rstd(key):
        _, parts, cols, *_ = norms[key]
        return rstd_t[0:parts, norm_at[key] % 3, 0:cols]

    def wait_src(eng, w):
        if w[0] == "bank":
            eng.wait_ge(*evacuated(w[1]))
        elif w[0] == "ev":
            eng.wait_ge(*after(w[1], *w[2:]))
        else:
            eng.wait_ge(C.sem[f"x_in{w[1]}"], 16)

    def att(u):
        kind = u[0]
        if kind in ("slc", "win"):
            _, h, qt = u
            pb = HD * (h % 2)
            k = ks_d if kind == "slc" else kw_d
            v0 = 0 if kind == "slc" else HD
            g = 3 * h + (1 if kind == "slc" else 2)
            return dict(q=nq[pb:pb + HD, h // 2, qt * P:(qt + 1) * P], k=k[pb:pb + HD, 0:(qt + 1) * P],
                        w=(qt + 1) * P, bias=toep[:, h, (NT - 1 - qt) * P:T],
                        v=[v1[:, kt, v0:v0 + HD] for kt in range(qt + 1)],
                        out=("nsa_o", h // 2), pb=pb, qt=qt, first=False, last=kind == "win",
                        bank_first=(kind == "slc" and h % 2 == 0 and qt == 0),
                        bank_last=(kind == "win" and h % 2 == 1 and qt == NT - 1),
                        gate=gates[:, qt, g:g + 1])
        if kind == "mla":
            _, h, qt = u
            return dict(q=mq[0:QKD, h, qt * P:(qt + 1) * P], k=mk[0:QKD, h, 0:(qt + 1) * P], w=(qt + 1) * P,
                        bias=causal[:, (NT - 1 - qt) * P:T],
                        v=[mv[:, kt, h * HD:(h + 1) * HD] for kt in range(qt + 1)],
                        out=("mla_o", h // 2), pb=HD * (h % 2), qt=qt, first=True, last=True,
                        bank_first=(h % 2 == 0 and qt == 0), bank_last=(h % 2 == 1 and qt == NT - 1), gate=None)
        _, c, hf, qt = u
        pb, lo = HD * hf, max(0, qt - 1)
        kv = 2 * (c // 4) + hf
        return dict(q=wq[pb:pb + HD, c, qt * P:(qt + 1) * P], k=wk[pb:pb + HD, c // 4, lo * P:(qt + 1) * P],
                    w=(qt + 1 - lo) * P, bias=alibi[:, 2 * c + hf, (0 if qt else P):2 * P],
                    v=[wv[:, kt, kv * HD:(kv + 1) * HD] for kt in range(lo, qt + 1)],
                    out=("swa_o", c), pb=pb, qt=qt, first=True, last=True,
                    bank_first=(hf == 0 and qt == 0), bank_last=(hf == 1 and qt == NT - 1), gate=None,
                    sink=col("sinks", 2 * c + hf))

    att_order = [s[1] for s in ORDER if s[0] == "att_scores"]
    att_at = {u: i for i, u in enumerate(att_order)}

    sig_names = [s[1] for s in ORDER if s[0] == "fm" and isinstance(s[1], tuple) and s[1][0] in ("rg", "gg", "gate")]
    sig_at = {name: i for i, name in enumerate(sig_names)}

    def sig_user(n):
        name = sig_names[n]
        return ("br",) + name[1:] if name[0] == "gate" else name

    TAB = ((0, 512), (512, 128), (640, 512), (1152, 512))
    SB_OFF = [0, 512, 896, 1152]
    sb_order = [(s[1], s[2]) for s in ORDER if s[0] == "sb_scores"]

    block = ctx.enter_context(nc.Block())

    @block.tensor
    def _(pe):
        def take(name, pool="lin"):
            banks = pools[pool]
            b = banks[turn[pool] % len(banks)] if pool in turn else banks[0]
            if pool in turn:
                turn[pool] += 1
            if n_tenants[b]:
                pe.wait_ge(C.sem[f"bank_free{b}"], n_tenants[b])
            tenants[name] = (b, n_tenants[b])
            n_tenants[b] += 1
            return bank[b]

        def fill(name, ins):
            ins.then_inc(C.sem[f"bank_full{tenants[name][0]}"], 1)

        def mm(out, lhs, rhs, start, stop, **kw):
            return pe.matmul(out, lhs, rhs, start=start, stop=stop, **kw)

        def mm3(out, wh, wl, xh, xl, start, stop):
            mm(out, wh, xh, start, False)
            mm(out, wh, xl, False, False)
            return mm(out, wl, xh, False, stop)

        def slot_ready(i):
            pe.wait_ge(*after("w_lo", i))

        def slot_free(i, ins=None, name=None):
            if name is not None:
                slot_done[i] = full(name)
            else:
                ins.then_inc(*did("slot_used", i))
                slot_done[i] = after("slot_used", i)

        def ms(key, n_src):
            srcs, parts, cols, one, *_ = norms[key]
            if key in PE_SUM:
                return
            out = take(("ms", key))
            if n_src == 1:
                pe.wait_ge(*after("sq_s", key, 0))
                rhs = sq[0:parts, sq_use[(key, 0)] % 2, 0:cols]
            else:
                pe.wait_ge(*after("sq_v", key, n_src - 1))
                rhs = sq_sum[0:parts, 0:cols]
            fill(("ms", key), mm(out[0:parts, 0:cols], one[0:parts, 0:parts], rhs, True, True))

        def x_chunk_ready(src, name, k):
            if src == "h":
                pe.wait_ge(*after("h_ready", seen_h, k))
            elif src == "o":
                pe.wait_ge(*after("o_ready", name[1], k))
            else:
                pe.wait_ge(*after("m_ready", k))

        pe.wait_ge(C.sem["const_in"], 16 * N_CONST)
        seen_h = None
        for step in ORDER:
            stage = step[0]
            if stage == "bias_tables":
                pe.wait_ge(C.sem["misc_in"], 16 * N_MISC)
                pe.wait_ge(*after("bcast_v"))
                for n, (c0, w) in enumerate(TAB):
                    out = take(("tab", n))
                    fill(("tab", n), mm(out[0:NH, 0:w], rb[:], onehot[:, c0:c0 + w], True, True))
            elif stage == "norm":
                ms(step[1], len(norms[step[1]][0]))
            elif stage == "sq" and step[1] in PE_SUM:
                _, key, c = step
                out = take(("ms", key)) if c == 0 else ps(("ms", key))
                pe.wait_ge(*after("sq_s", key, c))
                ins = mm(out[:], ones[:], sq[:, sq_use[(key, c)] % 2], c == 0, c == KD - 1)
                if c == KD - 1:
                    fill(("ms", key), ins)
                else:
                    ins.then_inc(*did("sq_pe", key, c))
            elif stage == "apply_h":
                seen_h = step[1]
            elif stage == "y_out":
                seen_h = "y"
            elif stage == "fmk":
                _, names, src, k0, k1 = step
                for name in names:
                    if k0 == 0:
                        slot_ready(SLOTS[name][0])
                        take(name)
                xh, xl = lin_src[src]
                blocks = [(k, name) for k in range(k0, min(k1, KD - 2)) for name in names]
                blocks += [(k, name) for name in names for k in range(max(k0, KD - 2), k1)]
                for k, name in blocks:
                    x_chunk_ready(src, name, k)
                    i = SLOTS[name][0]
                    wsl = slice(k * P, (k + 1) * P)
                    last = mm3(ps(name)[:], w_hi[:, i % SPL, wsl], w_lo[:, i % SPL, wsl], xh[:, k], xl[:, k],
                               k == 0, k == KD - 1)
                    if k == KD - 1:
                        fill(name, last)
                        slot_free(i, name=name)
            elif stage == "fm" and step[1] not in TOGETHER:
                _, name, src = step
                i = SLOTS[name][0]
                xh, xl = lin_src[src]
                slot_ready(i)
                out = take(name)
                for k in range(KD):
                    x_chunk_ready(src, name, k)
                    wsl = slice(k * P, (k + 1) * P)
                    last = mm3(out[:], w_hi[:, i % SPL, wsl], w_lo[:, i % SPL, wsl], xh[:, k], xl[:, k],
                               k == 0, k == KD - 1)
                fill(name, last)
                slot_free(i, name=name)
            elif stage == "tm":
                _, slot, name, cols, s, ns = step
                i = SLOTS[slot][0]
                if s == 0:
                    for t in range(NT):
                        take((name, t))
                per = KD // ns
                slot_ready(i)
                for t in range(NT):
                    for kk in range(per):
                        k = s * per + kk
                        if t == 0:
                            pe.wait_ge(*after("h_ready", seen_h, k))
                        wsl = slice(kk * (1024 // per), kk * (1024 // per) + cols)
                        ts = slice(t * P, (t + 1) * P)
                        wh, wl = w_hi[:, i % SPL, wsl], w_lo[:, i % SPL, wsl]
                        o = ps((name, t))[:, 0:cols]
                        mm(o, h_hi[:, k, ts], wh, k == 0, False)
                        mm(o, h_hi[:, k, ts], wl, False, False)
                        last = mm(o, h_lo[:, k, ts], wh, False, k == KD - 1)
                    if s == ns - 1:
                        fill((name, t), last)
                if s == ns - 1:
                    slot_free(i, name=(name, NT - 1))
                else:
                    slot_free(i, last)
            elif stage == "down":
                _, name, nk, o = step
                i0 = SLOTS[name][0]
                hh, hl = hid1 if name[0] == "down1" else hid2
                nm = (name[0], name[1], o)
                out = take(nm)
                for k in range(nk):
                    g = o * nk + k
                    i = i0 + g // 8
                    if g % 8 == 0:
                        slot_ready(i)
                    if o == 0:
                        pe.wait_ge(*after("hid", name[0], name[1], k))
                    wsl = slice(g % 8 * P, g % 8 * P + P)
                    last = mm3(out[:], w_hi[:, i % SPL, wsl], w_lo[:, i % SPL, wsl], hh[:, k], hl[:, k],
                               k == 0, k == nk - 1)
                    if k == nk - 1:
                        fill(nm, last)
                        if g % 8 == 7:
                            slot_free(i, name=nm)
                    elif g % 8 == 7:
                        slot_free(i, last)
            elif stage == "cmp_up":
                _, name, kv, s = step
                i = SLOTS[name][0]
                if s == 0:
                    pe.wait_ge(*after("cmpx", kv))
                    for c in range(2):
                        take(("cmp_h", kv, c), "att")
                slot_ready(i)
                for j in range(4 * s, 4 * s + 4):
                    for c in range(2):
                        wsl = slice((j % 4) * 256 + c * P, (j % 4) * 256 + (c + 1) * P)
                        last = mm3(ps(("cmp_h", kv, c))[:, 0:32], w_hi[:, i % SPL, wsl], w_lo[:, i % SPL, wsl],
                                   cmp_x[0][:, kv, j], cmp_x[1][:, kv, j], j == 0, j == 15)
                        if j == 15:
                            fill(("cmp_h", kv, c), last)
                if s == 3:
                    slot_free(i, name=("cmp_h", kv, 1))
                else:
                    slot_free(i, last)
            elif stage == "cmp_down":
                pe.wait_ge(C.sem["mixer_in"], 16 * N_MIXER)
                pe.wait_ge(*evacuated(("cmp_h", 1, 1)))
                pe.wait_ge(*after("cmp_v", "hv"))
                out = take("cmp_k")
                for c in range(2):
                    last = mm(out[:, 0:N_CMP], w2k[:, c], cmp_h[:, c, 0:N_CMP], c == 0, c == 1)
                fill("cmp_k", last)
                out = take("cmp_vt")
                for c in range(2):
                    last = mm(out[:, 0:HD], cmp_hv[:, c].rearrange("p h n -> p (h n)"), w2v[:, c], c == 0, c == 1)
                fill("cmp_vt", last)
            elif stage == "cmp_bias":
                pe.wait_ge(C.sem["bias_in"], 16 * 2 * NH)
                pe.wait_ge(C.sem["mixer_in"], 16 * N_MIXER)
                out = take("cmp_bias")
                for qt in range(NT):
                    for h in range(NH):
                        last = pe.transpose(out[:, (qt * NH + h) * N_CMP:(qt * NH + h + 1) * N_CMP],
                                            cb_t[:, h, qt * P:(qt + 1) * P], ident[0:N_CMP, 0:N_CMP])
                fill("cmp_bias", last)
            elif stage == "cmp_scores":
                pe.wait_ge(*after("rstd_used", "kcmp"))
                pe.wait_ge(*after("rstd_used", "nq1"))
                for hf in range(2):
                    out = take(("cmp_sc", hf))
                    pb = HD * hf
                    for qt in range(NT):
                        for j in range(2):
                            last = mm(out[:, (qt * 2 + j) * N_CMP:(qt * 2 + j + 1) * N_CMP],
                                      nq[pb:pb + HD, j, qt * P:(qt + 1) * P], cmp_k[pb:pb + HD, 1, 0:N_CMP],
                                      True, True, skip_group_check=True)
                    fill(("cmp_sc", hf), last)
            elif stage == "cmp_turn":
                pe.wait_ge(*after("cmp_v", "p"))
                out = take("cmp_pt")
                for qt in range(NT):
                    last = pe.transpose(out[:, qt * P:(qt + 1) * P], cmp_p[:, qt].rearrange("p h n -> p (h n)"), ident[:])
                fill("cmp_pt", last)
            elif stage == "att_scores":
                u = step[1]
                A = att(u)
                if u[0] in ("slc", "win"):
                    pe.wait_ge(*after("rstd_used", "nq1"))
                    pe.wait_ge(C.sem["ksw_in"], 16 * 2)
                elif u[0] == "mla":
                    pe.wait_ge(*after("rstd_used", ("mq", u[1])))
                else:
                    pe.wait_ge(*evacuated(("wk", 1)))
                    pe.wait_ge(*evacuated(("wq", u[1])))
                out = take(("sc", u), "att")
                fill(("sc", u), mm(out[:, 0:A["w"]], A["q"], A["k"], True, True))
            elif stage == "att_turn":
                u = step[1]
                A = att(u)
                pe.wait_ge(*after("att_p", u))
                out = take(("pt", u), "att")
                for b in range(A["w"] // P):
                    last = pe.transpose(out[:, b * P:(b + 1) * P], att_l[:, att_at[u] % 3, b * P:(b + 1) * P],
                                        ident[:])
                fill(("pt", u), last)
            elif stage == "att_pv":
                u = step[1]
                A = att(u)
                if A["bank_first"]:
                    take(A["out"], "out")
                out = ps(A["out"])[A["pb"]:A["pb"] + HD, A["qt"] * P:(A["qt"] + 1) * P]
                if u[0] == "slc":
                    h, qt = u[1], u[2]
                    pe.wait_ge(*evacuated("cmp_pt"))
                    pe.wait_ge(*evacuated("cmp_vt"))
                    mm(out, cmp_vt[:, h], cmp_pt[:, qt], True, False)
                if u[0] in ("slc", "win"):
                    pe.wait_ge(*evacuated(("v1", NT - 1)))
                elif u[0] == "mla":
                    pe.wait_ge(*evacuated(("mv", 1)))
                else:
                    pe.wait_ge(*evacuated(("wv", NT - 1)))
                pe.wait_ge(*evacuated(("pt", u)))
                n = len(A["v"])
                for b in range(n):
                    last = mm(out, A["v"][b], att_pt[:, att_at[u] % 2, b * P:(b + 1) * P],
                              A["first"] and b == 0, A["last"] and b == n - 1)
                if A["bank_last"]:
                    fill(A["out"], last)
                else:
                    last.then_inc(*did("att_done", u))
            elif stage == "mla_v":
                pe.wait_ge(*after("rstd_used", "ckv"))
                for n in range(2):
                    out = take(("mv", n))
                    for t in range(2):
                        tt = 2 * n + t
                        last = mm(out[:, t * 256:(t + 1) * 256], ckv[:, tt * P:(tt + 1) * P], wvb[:], True, True,
                                  skip_group_check=True)
                    fill(("mv", n), last)
            elif stage == "mla_qk":
                h = step[1]
                out = take(("mk", h))
                fill(("mk", h), mm(out[0:QKD, :], wkb[:, h], ckv[:], True, True))
                pe.wait_ge(*after("rstd_used", "cq"))
                for v in range(2):
                    out = take(("mq", h, v))
                    mm(out[0:QKD, :], wqb[:, 0, v, h], cq[:, 0], True, False)
                    fill(("mq", h, v), mm(out[0:QKD, :], wqb[0:HD, 1, v, h], cq[0:HD, 1], False, True))
            elif stage == "sb_scores":
                _, h, kt = step
                pb = HD * (h % 2)
                pe.wait_ge(*evacuated("sk1"))
                out = take(("z", h, kt))
                fill(("z", h, kt), mm(out[:, 0:T - kt * P], s_qk[pb:pb + HD, 2 + h // 2, kt * P:(kt + 1) * P],
                                      s_qk[pb:pb + HD, h // 2, kt * P:T], True, True))
            elif stage == "sb_exp":
                _, h, kt = step
                pb = HD * (h % 2)
                w = T - kt * P
                out = take(("r", h, kt), "att")
                mm(out[:, 0:w], s_qk[pb:pb + HD, 2 + h // 2, kt * P:(kt + 1) * P],
                   s_qk[pb:pb + HD, h // 2, kt * P:T], True, False, skip_group_check=True)
                mm(out[:, 0:P], ident[:], sbm[:, 3], False, False, skip_group_check=True)
                pe.wait_ge(*after("sb_sp", h, kt))
                for j in range(NT - 1, kt, -1):
                    mm(out[:, (j - kt) * P:w], sbm[:, 1], sb_sp[:, h % 2, SB_OFF[j]:SB_OFF[j] + T - j * P],
                       False, False, skip_group_check=True)
                last = mm(out[:, 0:w], sbm[:, 0], sb_sp[:, h % 2, SB_OFF[kt]:SB_OFF[kt] + w], False, True,
                          skip_group_check=True)
                fill(("r", h, kt), last)
            elif stage == "sb_pv":
                h = step[1]
                pb = HD * (h % 2)
                out = take(("sb_o", h), "out" if h == NH - 1 else "lin")
                pe.wait_ge(*evacuated(("r", h, 0)))
                for kt in range(NT):
                    w = T - kt * P
                    last = mm(out[pb:pb + HD, kt * P:T], v1[:, kt, 2 * HD + h * HD:2 * HD + (h + 1) * HD],
                              sb_a[:, h % 2, SB_OFF[kt]:SB_OFF[kt] + w], kt == 0, kt == NT - 1)
                fill(("sb_o", h), last)
            elif stage == "ret_scores":
                _, h, jt = step
                pe.wait_ge(*evacuated(("rk", h)))
                out = take(("rs", h, jt), "att")
                fill(("rs", h, jt), mm(out[:, 0:T - jt * P], kf[:, h % 2, jt * P:(jt + 1) * P], qf[:, h % 2, jt * P:T],
                                       True, True))
            elif stage == "ret_pv":
                h = step[1]
                pe.wait_ge(*evacuated((("rv", h // 2), NT - 1)))
                pe.wait_ge(*evacuated(("rs", h, NT - 1)))
                for e in range(2):
                    out = take(("ret_o", h, e))
                    for jt in range(NT):
                        w = T - jt * P
                        last = mm(out[:, jt * P:T], vt[:, jt, h % 2 * 256 + e * P:h % 2 * 256 + (e + 1) * P],
                                  ret_a[:, SB_OFF[jt]:SB_OFF[jt] + w], jt == 0, jt == NT - 1)
                    fill(("ret_o", h, e), last)
            elif stage == "ret_mean":
                h = step[1]
                out = take(("mean", h))
                for e in range(2):
                    pe.wait_ge(*evacuated(("ret_o", h, e)))
                    last = mm(out[:], ones[:], mix_o[:, e], e == 0, e == 1)
                fill(("mean", h), last)
            elif stage == "gla_decay":
                h = step[1]
                pe.wait_ge(*evacuated("ga"))
                pe.wait_ge(C.sem["late_in"], 16 * 4)
                out = take(("gz", h), "att")
                fill(("gz", h), mm(out[:], wa2[:, h * P:(h + 1) * P], ga_t[:], True, True))
            elif stage == "gla_turn":
                h = step[1]
                pe.wait_ge(*after("gla_v", "kd", h))
                out = take(("kdt", h), "att")
                for m in range(NT):
                    last = pe.transpose(out[:, m * P:(m + 1) * P], kf[:, h % 2, m * P:(m + 1) * P], ident[:])
                fill(("kdt", h), last)
                out = take(("ga_s", h), "att")
                for m in range(NT):
                    ms_ = slice(m * P, (m + 1) * P)
                    last = mm(out[:, ms_], gk_i[:, ms_], qf[:, h % 2, ms_], True, True, skip_group_check=True)
                fill(("ga_s", h), last)
            elif stage == "gla_chunks":
                h = step[1]
                pe.wait_ge(*evacuated(("kdt", h)))
                pe.wait_ge(*evacuated((("gv", h // 2), NT - 1)))
                for n in range(NGC - 1):
                    out = take(("kv", h, n), "att")
                    r = slice(GC * (n % 2), GC * (n % 2) + GC)
                    fill(("kv", h, n), mm(out[:, 0:256], gk_t[r, n // 2], vt[r, n // 2, h % 2 * 256:(h % 2 + 1) * 256],
                                          True, True))
                pe.wait_ge(*evacuated(("ga_s", h)))
                for e in range(2):
                    out = take(("gla_o", h, e))
                    for m in range(NT):
                        mm(out[:, m * P:(m + 1) * P], vt[:, m, h % 2 * 256 + e * P:h % 2 * 256 + (e + 1) * P], ga_m[:, m],
                           True, False, skip_group_check=True)
                        for n in (2 * m, 2 * m + 1):
                            if n == 0:
                                continue
                            pe.wait_ge(*evacuated(("kv", h, n - 1)))
                            last = mm(out[:, n * GC:(n + 1) * GC], g_st[:, n - 1, e * P:(e + 1) * P],
                                      qf[:, h % 2, n * GC:(n + 1) * GC], False, n % 2 == 1, skip_group_check=True)
                    fill(("gla_o", h, e), last)

    @block.scalar
    def _(act):
        act.preload_act_table_set("natural_log_exp_and_others")
        act.dma_start(par[:], a["par"]).then_inc(C.sem["const_in"], 16)
        for t, src in ((ones, "ones"), (ones64, "ones64")):
            act.dma_start(t[:], a[src]).then_inc(C.sem["const_in"], 16)
        act.dma_start(onehot[:], a["onehot"]).then_inc(C.sem["misc_in"], 16)
        act.dma_start(rb[0:N_BUCKETS, :], a["rel_bias"]).then_inc(C.sem["misc_in"], 16)

        def chain(ins):
            ins.then_inc(C.sem["s_chain"], 1)
            C.n["s_chain"] = C.n.get("s_chain", 0) + 1
            act.wait_ge(C.sem["s_chain"], C.n["s_chain"])

        def copy_out(name, dst, src_ap, scale=1.0):
            act.wait_ge(*full(name))
            act.activation(dst, src_ap, ACT.Copy, scale=scale).then_inc(*release(name))

        def sq_free(key, c):
            u = sq_use[(key, c)]
            if u >= 2:
                k2, c2 = sq_uses[u - 2]
                if len(norms[k2][0]) == 1 or (k2 in PE_SUM and c2 == KD - 1):
                    act.wait_ge(*full(("ms", k2)))
                elif k2 in PE_SUM:
                    act.wait_ge(*after("sq_pe", k2, c2))
                else:
                    act.wait_ge(*after("sq_v", k2, max(c2, 1)))

        def square(key, c):
            srcs, parts, cols, one, scale, eps, waits = norms[key]
            wait_src(act, waits[c])
            sq_free(key, c)
            act.activation(sq[0:parts, sq_use[(key, c)] % 2, 0:cols], srcs[c], ACT.Square)\
               .then_inc(*did("sq_s", key, c))

        def norm(key):
            srcs, parts, cols, one, scale, eps, waits = norms[key]
            act.wait_ge(*full(("ms", key)))
            r = norm_at[key]
            if r >= 3:
                act.wait_ge(*after("rstd_used", norm_order[r - 3]))
            if r == 0:
                act.wait_ge(*after("table", "eps"))
            e = EPS_COL[eps]
            act.activation(rstd(key), ps(("ms", key))[0:parts, 0:cols], ACT.Ln, scale=scale,
                           bias=epst[0:parts, e:e + 1]).then_inc(*release(("ms", key)))
            act.wait_ge(*evacuated(("ms", key)))
            act.activation(rstd(key), rstd(key), ACT.Exp, scale=-0.5).then_inc(*did("rstd", key))

        def ready(name, c=None):
            act.wait_ge(*after(name, c))

        act.wait_ge(C.sem["const_in"], 16 * N_CONST)
        for step in ORDER:
            stage = step[0]
            if stage == "norm":
                norm(step[1])
                if step[1] == "n1":
                    for t, src in ((w2k, "w2k"), (w2v, "w2v"), (ident, "ident"), (rope_c, "rope_c"), (rope_s, "rope_s"),
                                   (wqb, "wqb"), (wkb, "wkb"), (wvb, "wvb"), (causal, "causal"), (sbm, "sbm")):
                        act.dma_start(t[:], a[src]).then_inc(C.sem["mixer_in"], 16)
            elif stage == "sq":
                square(*step[1:])
            elif stage == "fm":
                name = step[1]
                key = name[0] if isinstance(name, tuple) else name
                if name == "ksw":
                    copy_out(name, ks_d, ps(name)[:])
                elif name == "nq0" or name == "nq1":
                    copy_out(name, nq[:, int(name[2])], ps(name)[:])
                elif name == "cq0":
                    copy_out(name, cq[:, 0], ps(name)[:])
                elif name == "cqr":
                    act.wait_ge(*full(name))
                    act.wait_ge(*after("zeros"))
                    chain(act.activation(cq[0:HD, 1], ps(name)[0:HD, :], ACT.Copy))
                    act.activation(kr[HD:QKD, 0], ps(name)[HD:QKD, :], ACT.Copy).then_inc(*release(name))
                    act.wait_ge(*evacuated(name))
                    for dst, src in ((HD, HD + 16), (HD + 16, HD)):
                        act.dma_start(kr[dst:dst + 16, 1], kr[src:src + 16, 0]).then_inc(C.sem["kr_in"], 16)
                elif name == "ckv":
                    copy_out(name, ckv[:], ps(name)[:])
                elif name in ("sq0", "sq1", "sk0", "sk1"):
                    c = int(name[2]) + (2 if name[1] == "k" else 0)
                    copy_out(name, s_qk[:, c], ps(name)[:], scale=HD ** -0.5 if name[1] == "q" else 1.0)
                elif key == "up1":
                    _, half, c = name
                    n = half * HALF1 + c
                    act.wait_ge(*full(name))
                    if n == 0:
                        act.wait_ge(*after("h_ready", "n2", KD - 1))
                    if n >= 2:
                        act.wait_ge(*after("hid", "down1", (n - 2) // HALF1, (n - 2) % HALF1))
                    act.activation(r1[:, n % 2], ps(name)[:], ACT.Relu).then_inc(*release(name))
                    act.wait_ge(*evacuated(name))
                    act.activation(r1[:, n % 2], r1[:, n % 2], ACT.Square).then_inc(*did("hid_s", name))
                elif key in ("rq", "gq"):
                    h = name[1]
                    if key == "rq" and h >= 2:
                        act.wait_ge(*full(("rs", h - 2, NT - 1)))
                    if key == "gq" and h >= 2:
                        act.wait_ge(*full(("gla_o", h - 2, 1)))
                    copy_out(name, qf[:, h % 2], ps(name)[:], scale=P ** -0.5 if key == "gq" else 1.0)
                elif key in ("rk", "gk"):
                    copy_out(name, kf[:, name[1] % 2], ps(name)[:])
                elif key in ("rg", "gg"):
                    _, h, e = name
                    n = sig_at[name]
                    act.wait_ge(*full(name))
                    if n >= 2:
                        act.wait_ge(*evacuated(sig_user(n - 2)))
                    act.activation(sig[:, n % 2], ps(name)[:], ACT.Sigmoid).then_inc(*did("gate_s", name))
                elif key == "ga":
                    act.wait_ge(*after("o_ready", 0, KD - 1))
                    copy_out(name, ga_t[:], ps(name)[0:16, :])
                elif key == "gate":
                    _, b, m = name
                    n = sig_at[name]
                    act.wait_ge(*full(name))
                    act.wait_ge(*evacuated(sig_user(n - 2)))
                    act.activation(sig[:, n % 2], ps(name)[:], ACT.Sigmoid).then_inc(*release(name))
                elif key == "wq":
                    if name[1] == 0:
                        act.wait_ge(*full(("gla_o", 3, 1)))
                    copy_out(name, wq[:, name[1]], ps(name)[:], scale=HD ** -0.5)
                elif name == "kvc":
                    act.wait_ge(*evacuated(name))
                    act.dma_start(kv_raw[HD:P, 0, 0:T - 1], kv_raw[0:HD, 0, 1:T]).then_inc(C.sem["kv_in"], 16)
                    act.dma_start(kv_raw[0:HD, 1], att_l[HD:P, 0]).then_inc(C.sem["kv_in"], 16)
                elif key == "wk":
                    if name[1] == 0:
                        act.wait_ge(*after("o_ready", 1, KD - 1))
                    copy_out(name, wk[:, name[1]], ps(name)[:])
                elif key == "fg":
                    _, half, c = name
                    n = half * HALF2 + c
                    act.wait_ge(*full(name))
                    if n == 0:
                        act.wait_ge(*full(("swa_o", 7)))
                        act.wait_ge(*after("h_ready", "fpre", KD - 1))
                    if n >= 2:
                        act.wait_ge(*evacuated(("fu", (n - 2) // HALF2, (n - 2) % HALF2)))
                    act.activation(sig2[:, n % 2], ps(name)[:], ACT.Sigmoid).then_inc(*did("gate_s", name))
            elif stage == "tm":
                _, _, name, _, s, ns = step
                if s < ns - 1:
                    continue
                if name == ("rv", 0):
                    act.wait_ge(*full(("down1", 1, KD - 1)))
                elif name in (("rv", 1), ("gv", 0), ("gv", 1)):
                    act.wait_ge(*full({"rv1": ("ret_o", 1, 1), "gv0": ("ret_o", 3, 1),
                                       "gv1": ("gla_o", 1, 1)}[name[0] + str(name[1])]))
                for t in range(NT):
                    if name == "v1":
                        copy_out((name, t), v1[:, t], ps((name, t))[:, 0:396])
                    elif name == "wv":
                        copy_out((name, t), wv[:, t], ps((name, t))[:, 0:256])
                    else:
                        copy_out((name, t), vt[:, t], ps((name, t))[:])
                if name == "v1":
                    act.wait_ge(*evacuated(("v1", NT - 1)))
                    act.activation(gates[:], v1[:, :, 384:396], ACT.Exp, scale=-1.0).then_inc(*did("cmp_s", "g"))
            elif stage == "cmp_down":
                copy_out("cmp_k", cmp_k[:, 0, 0:N_CMP], ps("cmp_k")[:, 0:N_CMP])
            elif stage == "cmp_up":
                kv = step[2]
                if step[3] < 3:
                    continue
                for c in range(2):
                    act.wait_ge(*full(("cmp_h", kv, c)))
                    act.activation(cmp_h[:, 2 * kv + c, 0:N_CMP], ps(("cmp_h", kv, c))[:, 0:N_CMP], ACT.Exp,
                                   scale=-1.0).then_inc(*did("cmp_s", kv, c))
            elif stage == "nsa_apply" and step[1] == "ksw":
                act.wait_ge(*after("rstd_used", "ksw"))
                act.dma_start(ks_d[HD:P], ks_d[0:HD]).then_inc(C.sem["ksw_in"], 16)
                act.dma_start(kw_d[0:HD], kw_d[HD:P]).then_inc(C.sem["ksw_in"], 16)
            elif stage == "cmp_scores":
                act.wait_ge(*after("cmp_v", "l"))
                act.activation(cmp_p[:, :, :, 0:N_CMP], cmp_p[:, :, :, 0:N_CMP], ACT.Exp).then_inc(*did("cmp_s", "exp"))
            elif stage == "cmp_turn":
                copy_out("cmp_pt", cmp_pt[:].rearrange("p t q -> p (t q)"), ps("cmp_pt")[:])
            elif stage == "att_scores":
                u = step[1]
                A = att(u)
                n = att_at[u]
                act.wait_ge(*after("att_n", u))
                L, sm = att_l[:, n % 3, 0:A["w"]], small[:, n % 4]
                act.activation(L, L, ACT.Exp, bias=sm[:, 1:2], accum_out=sm[:, 2:3]).then_inc(*did("att_exp", u))
                if "sink" in A:
                    act.activation(sm[:, 5:6], A["sink"], ACT.Exp, bias=sm[:, 1:2]).then_inc(*did("swa_s", u))
            elif stage == "att_turn":
                u = step[1]
                A = att(u)
                n = att_at[u]
                act.wait_ge(*full(("pt", u)))
                if n >= 2:
                    v = att_order[n - 2]
                    act.wait_ge(*(full(att(v)["out"]) if att(v)["bank_last"] else after("att_done", v)))
                act.activation(att_pt[:, n % 2, 0:A["w"]], ps(("pt", u))[:, 0:A["w"]], ACT.Copy)\
                   .then_inc(*release(("pt", u)))
            elif stage == "att_pv":
                u = step[1]
                A = att(u)
                if A["bank_last"]:
                    if u[0] == "swa":
                        copy_out(A["out"], swa_o[:, u[1]], ps(A["out"])[:])
                    else:
                        g = 1 if u[0] == "win" else 2
                        copy_out(A["out"], y[:, 2 * g + A["out"][1]], ps(A["out"])[:])
            elif stage == "mla_v":
                for n in range(2):
                    copy_out(("mv", n), mv[:, 2 * n:2 * n + 2], ps(("mv", n))[:].rearrange("p (t c) -> p t c", t=2))
            elif stage == "sb_scores":
                _, h, kt = step
                w = T - kt * P
                n = sb_order.index((h, kt))
                act.wait_ge(*full(("z", h, kt)))
                if n == 0:
                    act.wait_ge(*full(("nsa_o", 1)))
                if n >= 2:
                    act.wait_ge(*after("sb_sp", *sb_order[n - 2]))
                e = sb_e[:, n % 2, 0:w]
                chain(act.activation(e, ps(("z", h, kt))[:, 0:w], ACT.Abs))
                chain(act.activation(e, e, ACT.Exp, scale=-1.0))
                act.activation(e, e, ACT.Ln, bias=1.0).then_inc(*did("sb_exp", h, kt))
            elif stage == "sb_exp":
                _, h, kt = step
                w = T - kt * P
                act.wait_ge(*full(("r", h, kt)))
                if h >= 2:
                    act.wait_ge(*full(("sb_o", h - 2)))
                act.activation(sb_a[:, h % 2, SB_OFF[kt]:SB_OFF[kt] + w], ps(("r", h, kt))[:, 0:w], ACT.Exp)\
                   .then_inc(*release(("r", h, kt)))
            elif stage == "sb_pv":
                h = step[1]
                half = slice(HD * (h % 2), HD * (h % 2) + HD)
                copy_out(("sb_o", h), y[half, 6 + h // 2], ps(("sb_o", h))[half, :])
            elif stage == "x_again":
                act.wait_ge(*full(("nsa_o", 1) if step[1] == 0 else ("r", NH - 1, 0)))
                cc = slice(4 * step[1], 4 * step[1] + 4)
                act.dma_start(x_sb[:, cc], a["x"][:, cc]).then_inc(C.sem["x_back"], 16)
            elif stage == "ret_pv":
                h = step[1]
                for e in range(2):
                    if h >= 1:
                        act.wait_ge(*after("ret_d", h - 1, e))
                    copy_out(("ret_o", h, e), mix_o[:, e], ps(("ret_o", h, e))[:])
            elif stage == "gla_decay":
                h = step[1]
                if h >= 1:
                    act.wait_ge(*evacuated(("kv", h - 1, NGC - 2)))
                g0 = g_ln
                act.wait_ge(*full(("gz", h)))
                chain(act.activation(g0, ps(("gz", h))[:], ACT.Abs, bias=col("b_alpha", h)))
                chain(act.activation(g0, g0, ACT.Exp, scale=-1.0))
                act.activation(g0, g0, ACT.Ln, bias=1.0).then_inc(*did("gla_s", "ln", h))
                act.wait_ge(*after("gla_v", "d", h))
                act.activation(g_eb, g_b, ACT.Exp).then_inc(*did("gla_s", "eb", h))
                act.activation(gk_i[:], g_b, ACT.Exp, scale=-1.0).then_inc(*did("gla_s", "enb", h))
                act.activation(g_ed[:], g_ed[:], ACT.Exp).then_inc(*did("gla_s", "ed", h))
            elif stage == "gla_turn":
                h = step[1]
                if h >= 1:
                    act.wait_ge(*full(("kv", h - 1, NGC - 2)))
                copy_out(("kdt", h), gk_t, ps(("kdt", h))[:].rearrange("p (m k) -> p m k", m=NT))
            elif stage == "gla_chunks":
                h = step[1]
                for e in range(2):
                    if h >= 1:
                        act.wait_ge(*after("gla_done", h - 1, e))
                    copy_out(("gla_o", h, e), mix_o[:, e], ps(("gla_o", h, e))[:])

    @block.vector
    def _(dve):
        def chain(ins):
            ins.then_inc(C.sem["v_chain"], 1)
            C.n["v_chain"] = C.n.get("v_chain", 0) + 1
            dve.wait_ge(C.sem["v_chain"], C.n["v_chain"])

        def own(name, *key):
            dve.wait_ge(*after(name, *key))

        def split(t, hi, lo, *event):
            chain(dve.tensor_copy(hi, t))
            dve.tensor_tensor(lo, t, hi.bitcast(F32), ALU.subtract).then_inc(*did(*event))
            own(*event)

        def squares(key, c):
            srcs, parts, cols, *_ = norms[key]
            if c and key not in PE_SUM:
                own("sq_s", key, c)
                b = [sq[0:parts, sq_use[(key, x)] % 2, 0:cols] for x in (c - 1, c)]
                if c == 1:
                    for k2 in reversed(norm_order[:norm_at[key]]):
                        if len(norms[k2][0]) > 1 and k2 not in PE_SUM:
                            dve.wait_ge(*full(("ms", k2)))
                            break
                else:
                    own("sq_v", key, c - 1)
                dve.tensor_tensor(sq_sum[0:parts, 0:cols], b[0] if c == 1 else sq_sum[0:parts, 0:cols], b[1],
                                  ALU.add).then_inc(*did("sq_v", key, c))

        def scaled(key, dst, src, w, parts=P):
            return dve.scalar_tensor_tensor(out=dst, in0=src, scalar=w, in1=rstd(key), op0=ALU.mult, op1=ALU.mult)

        for i, v in enumerate(EPS_VAL):
            ins = dve.memset(epst[:, i:i + 1], v)
        ins.then_inc(*did("table", "eps"))
        dve.wait_ge(C.sem["const_in"], 16 * N_CONST)
        last_h = None
        for step in ORDER:
            stage = step[0]
            if stage == "bias_tables":
                dve.wait_ge(C.sem["misc_in"], 16 * N_MISC)
                dve.memset(rb[N_BUCKETS:N_BUCKETS + 1, :], NEG).then_inc(*did("bcast_v"))
                dve.memset(y[:, 5:8], 0.0).then_inc(*did("zeros"))
                for n, (c0, w) in enumerate(TAB):
                    dve.wait_ge(*full(("tab", n)))
                    dve.tensor_copy(tab[:, c0:c0 + w], ps(("tab", n))[0:NH, 0:w]).then_inc(*release(("tab", n)))
            elif stage == "sq":
                squares(*step[1:])
            elif stage in ("apply_h", "y_out"):
                key = step[1] if stage == "apply_h" else "y"
                if last_h is not None:
                    dve.wait_ge(*full(last_h))
                for c in range(KD) if stage == "apply_h" else (2 * step[1], 2 * step[1] + 1):
                    if stage == "y_out":
                        nk, src, w = ("y", c // 2), y[:, c], col("out_norm", c)
                    else:
                        nk, src, w = key, x_sb[:, c], col(step[2], c)
                    if stage == "y_out" or c == 0:
                        own("rstd", nk)
                    t = tmp[:, c % 2]
                    ins = scaled(nk, t, src, w)
                    if (stage == "y_out" and c % 2 == 1) or (stage == "apply_h" and c == KD - 1):
                        ins.then_inc(*did("rstd_used", nk))
                        own("rstd_used", nk)
                    else:
                        chain(ins)
                    split(t, h_hi[:, c], h_lo[:, c], "h_ready", key, c)
            elif stage == "fm":
                name, src = step[1], step[2]
                if src == "h":
                    last_h = name
                key = name[0] if isinstance(name, tuple) else name
                if name == "kvc":
                    dve.wait_ge(*full(name))
                    dve.wait_ge(*evacuated(("tab", 3)))
                    chain(dve.tensor_copy(kv_raw[0:HD, 0], ps(name)[0:HD, :]))
                    chain(dve.tensor_copy(kv_raw[HD:P, 1, 0:T - 1], ps(name)[HD:P, 1:T]))
                    dve.tensor_copy(att_l[HD:P, 0], ps(name)[HD:P, :]).then_inc(*release(name))
                    dve.wait_ge(*evacuated(name))
                elif key in ("ac", "au", "ab"):
                    c = name[1]
                    dve.wait_ge(*full(name))
                    v = conv_t[:, 0, 2:2 + T]
                    if key == "ac":
                        if c == 0:
                            chain(dve.memset(conv_t[:], 0.0))
                        ins = dve.tensor_copy(conv_t[:, 1, 2:2 + T], ps(name)[:])
                    elif key == "au":
                        ins = dve.tensor_tensor(v, ps(name)[:], conv_t[:, 1, 2:2 + T], ALU.mult)
                    else:
                        yc = y[:, c]
                        w = [col("conv_w", 2 * k + c) for k in range(3)]
                        chain(dve.tensor_scalar(yc, conv_t[:, 0, 2:2 + T], w[2], col("conv_b", c), ALU.mult, ALU.add))
                        for k in (1, 0):
                            chain(dve.scalar_tensor_tensor(out=yc, in0=conv_t[:, 0, k:k + T], scalar=w[k], in1=yc,
                                                           op0=ALU.mult, op1=ALU.add))
                        ins = dve.tensor_tensor(conv_t[:, 1, 2:2 + T], ps(name)[:], yc, ALU.mult)
                    ins.then_inc(*release(name))
                    dve.wait_ge(*evacuated(name))
                    if key == "ab":
                        dve.tensor_copy(y[:, c], conv_t[:, 1, 2:2 + T]).then_inc(*did("conv_v", c))
                        own("conv_v", c)
                elif key == "wout":
                    c = name[1]
                    if c == 0:
                        dve.wait_ge(C.sem["x_back"], 16 * 2)
                    dve.wait_ge(*full(name))
                    dve.tensor_tensor(x_sb[:, c], ps(name)[:], x_sb[:, c], ALU.add).then_inc(*release(name))
                elif key == "wout2":
                    c = name[1]
                    dve.wait_ge(*full(name))
                    dve.tensor_copy(merged[:, c], ps(name)[:]).then_inc(*release(name))
                elif key == "up1":
                    _, half, c = name
                    own("hid_s", name)
                    if half == 1 and c == 0:
                        dve.wait_ge(*full(("down1", 0, KD - 1)))
                    if half == 0 and c == 0:
                        dve.wait_ge(*full(("wout", KD - 1)))
                    split(r1[:, (half * HALF1 + c) % 2], hid1[0][:, c], hid1[1][:, c], "hid", "down1", half, c)
                elif key in ("rg", "gg"):
                    _, h, e = name
                    n = sig_at[name]
                    own("gate_s", name)
                    dve.tensor_tensor(silu[:, e], ps(name)[:], sig[:, n % 2], ALU.mult).then_inc(*release(name))
                    dve.wait_ge(*evacuated(name))
                elif key == "br":
                    _, b, m = name
                    n = sig_at[("gate", b, m)]
                    dve.wait_ge(*full(name))
                    dve.wait_ge(*evacuated(("gate", b, m)))
                    t = merged[:, m] if b == 0 else tmp[:, n % 2]
                    ins = dve.tensor_tensor(t, ps(name)[:], sig[:, n % 2], ALU.mult)
                    ins.then_inc(*release(name))
                    dve.wait_ge(*evacuated(name))
                    if b:
                        chain(dve.tensor_tensor(merged[:, m], merged[:, m], t, ALU.add))
                    if b == 2:
                        split(merged[:, m], m_hl[0][:, m], m_hl[1][:, m], "m_ready", m)
                elif key == "fu":
                    _, half, c = name
                    n = half * HALF2 + c
                    own("gate_s", ("fg", half, c))
                    if half == 1 and c == 0:
                        dve.wait_ge(*full(("down2", 0, KD - 1)))
                    s = sig2[:, n % 2]
                    dve.tensor_tensor(s, ps(("fg", half, c))[:], s, ALU.mult).then_inc(*release(("fg", half, c)))
                    dve.wait_ge(*evacuated(("fg", half, c)))
                    dve.wait_ge(*full(name))
                    t = tmp[:, n % 2]
                    dve.tensor_tensor(t, ps(name)[:], s, ALU.mult).then_inc(*release(name))
                    dve.wait_ge(*evacuated(name))
                    split(t, hid2[0][:, c], hid2[1][:, c], "hid", "down2", half, c)
            elif stage == "tm" and step[4] < step[5] - 1:
                continue
            elif stage == "tm" and step[2] == "v1":
                last_h = ("v1", NT - 1)
                own("cmp_s", "g")
                chain(dve.tensor_scalar(gates[:], gates[:], 1.0, None, ALU.add))
                dve.reciprocal(gates[:], gates[:]).then_inc(*did("gate_v"))
                own("gate_v")
            elif stage == "tm":
                last_h = (step[2], NT - 1)
            elif stage == "down":
                _, name, nk, o = step
                nm = (name[0], name[1], o)
                dve.wait_ge(*full(nm))
                if name[0] == "down1" or name[1] == 1:
                    dst = x_sb[:, o] if name[0] == "down1" else f_acc[:, o]
                    if nm[0] == "down2":
                        dve.wait_ge(*evacuated(("down2", 0, o)))
                    dve.tensor_tensor(dst, ps(nm)[:], dst, ALU.add).then_inc(*release(nm))
                else:
                    dve.tensor_copy(f_acc[:, o], ps(nm)[:]).then_inc(*release(nm))
            elif stage == "cmp_x":
                kv = step[1]
                if kv == 0:
                    dve.wait_ge(C.sem["kv_in"], 16 * 2)
                    dve.wait_ge(C.sem["table_out"], 16)
                v4 = kv_raw[:, kv].rearrange("p (n j two) -> p j two n", j=8, two=2)
                pos = par[:, PCOL["pos"] + 16 * kv:PCOL["pos"] + 16 * (kv + 1)]
                t = tmp[:, 0].rearrange("p (j n) -> p j n", n=32)
                chain(dve.memset(tmp[:, 0], 0.0))
                for half in range(2):
                    ins = dve.tensor_tensor(t[:, 8 * half:8 * half + 8, 0:N_CMP],
                                            v4[:, :, 0, half:half + N_CMP],
                                            pos[:, 8 * half:8 * half + 8, None].to_broadcast([P, 8, N_CMP]), ALU.add)
                chain(ins)
                split(tmp[:, 0], cmp_x[0][:, kv].rearrange("p j n -> p (j n)"),
                      cmp_x[1][:, kv].rearrange("p j n -> p (j n)"), "cmpx", kv)
            elif stage == "nsa_apply" and step[1] == "ksw":
                own("rstd", "ksw")
                rs = rstd("ksw")
                for dst, p0 in ((kw_d, HD), (ks_d, 0)):
                    ins = dve.scalar_tensor_tensor(out=dst[p0:p0 + HD], in0=ks_d[p0:p0 + HD], scalar=col("nsa_k", 1)[p0:p0 + HD],
                                                   in1=rs[p0:p0 + HD], op0=ALU.mult, op1=ALU.mult)
                    if p0:
                        chain(ins)
                ins.then_inc(*did("rstd_used", "ksw"))
                own("rstd_used", "ksw")
            elif stage == "nsa_apply":
                name = step[1]
                own("rstd", name)
                dst = nq[:, int(name[2])]
                scaled(name, dst, dst, col("nsa_q")).then_inc(*did("rstd_used", name))
                own("rstd_used", name)
            elif stage == "cmp_down":
                dve.wait_ge(*full("cmp_vt"))
                dve.tensor_tensor(cmp_vt[:], ps("cmp_vt")[:, None, 0:HD].to_broadcast([P, NH, HD]),
                                  col("head_of", 0, NH)[:, :, None].to_broadcast([P, NH, HD]), ALU.mult)\
                    .then_inc(*release("cmp_vt"))
            elif stage == "cmp_up":
                kv = step[2]
                if step[3] < 3:
                    continue
                for c in range(2):
                    own("cmp_s", kv, c)
                    hcol = cmp_h[:, 2 * kv + c, 0:N_CMP]
                    chain(dve.tensor_scalar(hcol, hcol, 1.0, None, ALU.add))
                    chain(dve.reciprocal(hcol, hcol))
                    dve.tensor_tensor(hcol, ps(("cmp_h", kv, c))[:, 0:N_CMP], hcol, ALU.mult)\
                       .then_inc(*release(("cmp_h", kv, c)))
                    dve.wait_ge(*evacuated(("cmp_h", kv, c)))
                if kv == 1:
                    chain(dve.memset(cmp_hv[:], 0.0))
                    dve.tensor_copy(cmp_hv[:, :, :, 0:N_CMP], cmp_h[:, 2:4, None, 0:N_CMP]
                                    .to_broadcast([P, 2, NH, N_CMP])).then_inc(*did("cmp_v", "hv"))
                    own("cmp_v", "hv")
            elif stage == "cmp_apply":
                own("rstd", "kcmp")
                scaled("kcmp", cmp_k[:, 1, 0:N_CMP], cmp_k[:, 0, 0:N_CMP], col("nsa_k", 0))\
                    .then_inc(*did("rstd_used", "kcmp"))
                own("rstd_used", "kcmp")
            elif stage == "cmp_bias":
                dve.wait_ge(*full("cmp_bias"))
                dve.tensor_copy(cmp_bias[:].rearrange("p a b c -> p (a b c)"),
                                ps("cmp_bias")[:, 0:NT * NH * N_CMP]).then_inc(*release("cmp_bias"))
                dve.wait_ge(*evacuated("cmp_bias"))
            elif stage == "cmp_scores":
                chain(dve.memset(cmp_p[:], 0.0))
                p3 = cmp_p[:].rearrange("p a b c -> p (a b) c")[:, :, 0:N_CMP]
                bc = lambda i: cmp_s[:, i].rearrange("p a b -> p (a b)")[:, :, None].to_broadcast([P, NT * NH, N_CMP])
                dve.wait_ge(*evacuated("cmp_bias"))
                for hf in range(2):
                    n = ("cmp_sc", hf)
                    dve.wait_ge(*full(n))
                    dve.tensor_tensor(cmp_p[:, :, hf:NH:2, 0:N_CMP], ps(n)[:, 0:NT * 2 * N_CMP]
                                      .rearrange("p (a b c) -> p a b c", a=NT, b=2), cmp_bias[:, :, hf:NH:2],
                                      ALU.add).then_inc(*release(n))
                dve.wait_ge(*evacuated(n))
                chain(dve.tensor_reduce(cmp_s[:, 0].rearrange("p a b -> p (a b)"), p3, AX, ALU.max))
                chain(dve.tensor_scalar(cmp_s[:, 0], cmp_s[:, 0], NEG / 10, None, ALU.max))
                dve.tensor_tensor(p3, p3, bc(0), ALU.subtract).then_inc(*did("cmp_v", "l"))
                own("cmp_s", "exp")
                chain(dve.tensor_reduce(cmp_s[:, 1].rearrange("p a b -> p (a b)"), p3, AX, ALU.add))
                chain(dve.tensor_scalar(cmp_s[:, 1], cmp_s[:, 1], 1e-30, None, ALU.max))
                chain(dve.reciprocal(cmp_s[:, 2], cmp_s[:, 1]))
                chain(dve.tensor_tensor(cmp_s[:, 3], cmp_s[:, 2],
                                        gates[:].rearrange("p t (h c) -> p t h c", c=3)[:, :, :, 0], ALU.mult))
                dve.tensor_tensor(p3, p3, bc(3), ALU.mult).then_inc(*did("cmp_v", "p"))
                own("cmp_v", "p")
            elif stage == "att_scores":
                u = step[1]
                A = att(u)
                n = att_at[u]
                L, sm = att_l[:, n % 3, 0:A["w"]], small[:, n % 4]
                dve.wait_ge(*full(("sc", u)))
                if n >= 3:
                    dve.wait_ge(*full(("pt", att_order[n - 3])))
                if n >= 4:
                    own("att_p", att_order[n - 4])
                if n == 0:
                    dve.wait_ge(C.sem["bias_in"], 16 * 2 * NH)
                if u[0] == "swa" and u[2:] == (0, 0):
                    dve.wait_ge(C.sem[f"alibi_in{u[1]}"], 16)
                dve.tensor_tensor_reduce(L, ps(("sc", u))[:, 0:A["w"]], A["bias"], 1.0, -3.0e38, ALU.add, ALU.max,
                                         sm[:, 0:1]).then_inc(*release(("sc", u)))
                dve.wait_ge(*evacuated(("sc", u)))
                if "sink" in A:
                    dve.tensor_scalar(sm[:, 1:2], sm[:, 0:1], A["sink"], -1.0, ALU.max, ALU.mult)\
                       .then_inc(*did("att_n", u))
                else:
                    dve.tensor_scalar(sm[:, 1:2], sm[:, 0:1], -1.0, None, ALU.mult).then_inc(*did("att_n", u))
            elif stage == "att_norm":
                u = step[1]
                A = att(u)
                n = att_at[u]
                L, sm = att_l[:, n % 3, 0:A["w"]], small[:, n % 4]
                if "sink" in A:
                    own("swa_s", u)
                    chain(dve.tensor_tensor(sm[:, 2:3], sm[:, 2:3], sm[:, 5:6], ALU.add))
                else:
                    own("att_exp", u)
                chain(dve.reciprocal(sm[:, 3:4], sm[:, 2:3]))
                if A["gate"] is not None:
                    dve.tensor_scalar(L, L, sm[:, 3:4], A["gate"], ALU.mult, ALU.mult).then_inc(*did("att_p", u))
                else:
                    dve.tensor_scalar(L, L, sm[:, 3:4], None, ALU.mult).then_inc(*did("att_p", u))
            elif stage == "swa_split":
                dve.wait_ge(*full(("br", 1, KD - 1)))
                dve.wait_ge(*evacuated(("swa_o", KD - 1)))
                for c in range(KD):
                    split(swa_o[:, c], o_hl[0][:, c], o_hl[1][:, c], "o_ready", 2, c)
            elif stage == "mla_lora":
                own("rstd", "cq")
                for c in range(2):
                    ins = scaled("cq", cq[:, c], cq[:, c], col("mla_qa", c))
                ins.then_inc(*did("rstd_used", "cq"))
                own("rstd_used", "cq")
                own("rstd", "ckv")
                scaled("ckv", ckv[:], ckv[:], col("mla_kv")).then_inc(*did("rstd_used", "ckv"))
                own("rstd_used", "ckv")
            elif stage == "mla_rope_k":
                dve.wait_ge(C.sem["kr_in"], 16 * 2)
                dve.wait_ge(C.sem["mixer_in"], 16 * N_MIXER)
                dve.tensor_tensor(kr[:, 0], kr[:, 0], rope_c[:], ALU.mult)
                chain(dve.tensor_tensor(kr[:, 1], kr[:, 1], rope_s[:], ALU.mult))
                chain(dve.tensor_tensor(kr[:, 0], kr[:, 0], kr[:, 1], ALU.add))
            elif stage == "mla_qk":
                h = step[1]
                dve.wait_ge(*full(("mk", h)))
                dve.tensor_tensor(mk[0:QKD, h], ps(("mk", h))[0:QKD, :], kr[:, 0], ALU.add).then_inc(*release(("mk", h)))
                dve.wait_ge(*evacuated(("mk", h)))
                dve.wait_ge(*full(("mq", h, 1)))
                dve.tensor_tensor(mq[0:QKD, h], ps(("mq", h, 0))[0:QKD, :], rope_c[:], ALU.mult)\
                   .then_inc(*release(("mq", h, 0)))
                dve.tensor_tensor(tmp[0:QKD, 0], ps(("mq", h, 1))[0:QKD, :], rope_s[:], ALU.mult)\
                   .then_inc(*release(("mq", h, 1)))
                dve.wait_ge(*evacuated(("mq", h, 0)))
                dve.wait_ge(*evacuated(("mq", h, 1)))
                dve.tensor_tensor(mq[0:QKD, h], mq[0:QKD, h], tmp[0:QKD, 0], ALU.add).then_inc(*did("mla_q", h))
                own("mla_q", h)
            elif stage == "mla_scale":
                h = step[1]
                own("rstd", ("mk", h))
                scaled(("mk", h), mk[0:QKD, h], mk[0:QKD, h], col("mla_k", parts=QKD)).then_inc(*did("rstd_used", ("mk", h)))
                own("rstd", ("mq", h))
                scaled(("mq", h), mq[0:QKD, h], mq[0:QKD, h], col("mla_q", parts=QKD)).then_inc(*did("rstd_used", ("mq", h)))
                own("rstd_used", ("mq", h))
            elif stage == "sb_scores":
                _, h, kt = step
                w = T - kt * P
                n = sb_order.index((h, kt))
                own("sb_exp", h, kt)
                if h >= 2 and kt == NT - 1:
                    dve.wait_ge(*full(("r", h - 2, 0)))
                sp = sb_sp[:, h % 2, SB_OFF[kt]:SB_OFF[kt] + w]
                dve.scalar_tensor_tensor(out=sp, in0=ps(("z", h, kt))[:, 0:w], scalar=0.0,
                                         in1=sb_e[:, n % 2, 0:w], op0=ALU.max, op1=ALU.add)\
                   .then_inc(*release(("z", h, kt)))
                dve.wait_ge(*evacuated(("z", h, kt)))
                dve.tensor_tensor(sp[:, 0:P], sp[:, 0:P], sbm[:, 2], ALU.mult).then_inc(*did("sb_sp", h, kt))
            elif stage == "ret_scores":
                _, h, jt = step
                w = T - jt * P
                dve.wait_ge(*full(("rs", h, jt)))
                if h >= 1:
                    dve.wait_ge(*full(("ret_o", h - 1, 1)))
                if h == 0 and jt == 0:
                    dve.wait_ge(C.sem["late_in"], 16)
                dve.tensor_tensor(ret_a[:, SB_OFF[jt]:SB_OFF[jt] + w], ps(("rs", h, jt))[:, 0:w], decay[:, h, 0:w],
                                  ALU.mult).then_inc(*release(("rs", h, jt)))
            elif stage == "ret_mean":
                h = step[1]
                dve.wait_ge(*full(("mean", h)))
                dve.tensor_scalar(tmp[:, 0], ps(("mean", h))[:], -1 / 256, None, ALU.mult).then_inc(*release(("mean", h)))
                dve.wait_ge(*evacuated(("mean", h)))
                for e in range(2):
                    if h >= 1:
                        own("ret_done", h - 1, e)
                    dve.tensor_tensor(ret_d[:, e], mix_o[:, e], tmp[:, 0], ALU.add).then_inc(*did("ret_d", h, e))
                own("ret_d", h, 1)
            elif stage in ("ret_out", "gla_out"):
                h = step[1]
                ret = stage == "ret_out"
                key = ("ret" if ret else "gla", h)
                own("rstd", key)
                if not ret and h == 0:
                    dve.wait_ge(*full(("br", 0, KD - 1)))
                for e in range(2):
                    c = 2 * h + e
                    src = ret_d[:, e] if ret else mix_o[:, e]
                    t = tmp[:, e]
                    ins = scaled(key, t, src, col("ret_w" if ret else "gla_w", c))
                    ins.then_inc(*did("ret_done" if ret else "gla_done", h, e))
                    own("ret_done" if ret else "gla_done", h, e)
                    if ret:
                        ins = dve.scalar_tensor_tensor(out=t, in0=t, scalar=col("ret_b", c), in1=silu[:, e],
                                                       op0=ALU.add, op1=ALU.mult)
                    else:
                        ins = dve.tensor_tensor(t, t, silu[:, e], ALU.mult)
                    if e == 1:
                        ins.then_inc(*did("rstd_used", key))
                        own("rstd_used", key)
                    else:
                        chain(ins)
                    split(t, o_hl[0][:, c], o_hl[1][:, c], "o_ready", 0 if ret else 1, c)
            elif stage == "gla_decay":
                h = step[1]
                own("gla_s", "ln", h)
                dve.wait_ge(C.sem["late_in"], 16 * 4)
                g0, g1 = g_ln, g_b
                dve.tensor_scalar(g_eb, ps(("gz", h))[:], col("b_alpha", h), 0.0, ALU.add, ALU.min)\
                   .then_inc(*release(("gz", h)))
                dve.wait_ge(*evacuated(("gz", h)))
                chain(dve.tensor_tensor(g0, g_eb, g0, ALU.subtract))
                chain(dve.tensor_scalar(g0, g0, 1 / 16.0, -1.0, ALU.mult, ALU.max))
                chain(dve.tensor_tensor_scan(g1, gscan[:], g0, 0.0, ALU.mult, ALU.add))
                b4 = g1.rearrange("p (n c) -> p n c", c=GC)
                dve.tensor_tensor(g_ed[:].rearrange("p (n c) -> p n c", c=GC),
                                  b4[:, :, GC - 1:GC].to_broadcast([P, NGC, GC]), b4, ALU.subtract)\
                   .then_inc(*did("gla_v", "d", h))
            elif stage == "gla_scale":
                h = step[1]
                if h >= 1:
                    dve.wait_ge(*full(("gla_o", h - 1, 1)))
                own("gla_s", "eb", h)
                dve.tensor_tensor(qf[:, h % 2], qf[:, h % 2], g_eb, ALU.mult)
                own("gla_s", "enb", h)
                dve.tensor_tensor(gk_i[:], kf[:, h % 2], gk_i[:], ALU.mult)
                own("gla_s", "ed", h)
                dve.tensor_tensor(kf[:, h % 2], kf[:, h % 2], g_ed[:], ALU.mult).then_inc(*did("gla_v", "kd", h))
                own("gla_v", "kd", h)
            elif stage == "gla_turn":
                h = step[1]
                dve.wait_ge(*full(("ga_s", h)))
                dve.tensor_tensor(ga_m, ps(("ga_s", h))[:].rearrange("p (m i) -> p m i", m=NT),
                                  gmask[:, None, :].to_broadcast([P, NT, P]), ALU.mult).then_inc(*release(("ga_s", h)))
            elif stage == "gla_chunks":
                h = step[1]
                for n in range(NGC - 1):
                    dve.wait_ge(*full(("kv", h, n)))
                    src = ps(("kv", h, n))[:, 0:256]
                    if n == 0:
                        ins = dve.tensor_copy(g_st[:, 0], src)
                    else:
                        dve.wait_ge(*evacuated(("kv", h, n - 1)))
                        a_n = g_eb[:, (n + 1) * GC - 1:(n + 1) * GC]
                        ins = dve.scalar_tensor_tensor(out=g_st[:, n], in0=g_st[:, n - 1], scalar=a_n, in1=src,
                                                       op0=ALU.mult, op1=ALU.add)
                    ins.then_inc(*release(("kv", h, n)))
            elif stage == "residual":
                _, key, c = step
                own("rstd", key)
                if c >= 2:
                    own("x_ready", key, c - 2)
                t = tmp[:, c % 2]
                ins = scaled(key, t, merged[:, c], col(key, c))
                if c == KD - 1:
                    ins.then_inc(*did("rstd_used", key))
                    own("rstd_used", key)
                else:
                    chain(ins)
                dve.tensor_tensor(x_sb[:, c], x_sb[:, c], t, ALU.add).then_inc(*did("x_ready", key, c))
                if c == KD - 1:
                    own("x_ready", key, KD - 1)

    @block.gpsimd
    def _(pool):
        for i in range(N_SLOTS):
            pool.wait_ge(C.sem[f"w_landed{i % RAW}"], 16 * (i // RAW + 1))
            if i >= SPL:
                pool.wait_ge(*slot_done[i - SPL])
            hi, lo, raw = w_hi[:, i % SPL], w_lo[:, i % SPL], w_raw[:, i % RAW]
            pool.tensor_scalar(hi, raw, 1.0, 0.0, ALU.mult, ALU.add).then_inc(*did("w_hi", i))
            pool.wait_ge(*after("w_hi", i))
            pool.tensor_tensor(lo, raw, hi.bitcast(F32), ALU.subtract).then_inc(*did("w_lo", i))

    @block.sync
    def _(sp):
        for g in range(4):
            sp.dma_start(x_sb[:, 2 * g:2 * g + 2], a["x"][:, 2 * g:2 * g + 2]).then_inc(C.sem[f"x_in{g}"], 16)
        n = 0

        def bias_tables(part):
            if part == 0:
                for nn in range(len(TAB)):
                    sp.wait_ge(*evacuated(("tab", nn)))
                sp.dma_start(a["table"], tab[:]).then_inc(C.sem["table_out"], 16)
                return
            if part == 1:
                sp.wait_ge(C.sem["table_out"], 16)
                for k, (c0, w) in enumerate(((0, 640), (640, 1024))):
                    rows = P if k == 0 else N_CMP
                    dst = a["scratch"][:, k, 0:rows * w].rearrange("h (p w) -> h p w", w=w)
                    sp.dma_start(dst, a["table"][:, None, c0:c0 + w].to_broadcast([NH, rows, w]))\
                      .then_inc(C.sem["bias_out0"], 16)
                return
            sp.wait_ge(C.sem["bias_out0"], 16 * 2)
            t = a["scratch"].tensor
            for h in range(NH):
                sp.dma_start(toep[:, h], bass.AP(tensor=t, offset=(2 * h) * P * 1024 + P - 1,
                                                 ap=[[640 - 1, P], [1, T]])).then_inc(C.sem["bias_in"], 16)
                sp.dma_start(cb_t[:, h], bass.AP(tensor=t, offset=(2 * h + 1) * P * 1024 + T - CMP_LEN + 1,
                                                 ap=[[1024 - CMP_STRIDE, N_CMP], [1, T]]))\
                  .then_inc(C.sem["bias_in"], 16)

        for step in ORDER:
            stage = step[0]
            name = step[1]
            if stage in ("fm", "tm", "cmp_up") or (stage == "down" and step[3] == 0):
                for _ in range(SLOTS[name][1]):
                    if n >= RAW:
                        sp.wait_ge(*after("w_lo", n - RAW))
                    sp.dma_start(w_raw[:, n % RAW], a["w"][n]).then_inc(C.sem[f"w_landed{n % RAW}"], 16)
                    n += 1
                    if n in (4, 5, 7):
                        bias_tables((4, 5, 7).index(n))
            if name == (("rv", 0), "s", 0):
                sp.wait_ge(*full(("down1", 1, KD - 1)))
                sp.dma_start(decay[:], a["decay"]).then_inc(C.sem["late_in"], 16)
            if name == ("br", 0, 2):
                sp.wait_ge(*after("o_ready", 0, KD - 1))
                sp.wait_ge(C.sem["late_in"], 16)
                for t, src in ((wa2, "wa2"), (gscan, "gscan"), (gmask, "gmask")):
                    sp.dma_start(t[:], a[src]).then_inc(C.sem["late_in"], 16)
                sp.wait_ge(C.sem["late_in"], 16 * 4)
            if stage == "tm" and name == ("wv", "s", 0):
                sp.wait_ge(*full(("gla_o", 3, 1)))
                sp.wait_ge(*after("o_ready", 1, KD - 1))
                for c in range(8):
                    sp.dma_start(alibi[:, 2 * c:2 * c + 2], a["alibi"][:, 2 * c:2 * c + 2])\
                      .then_inc(C.sem[f"alibi_in{c}"], 16)
        for g in range(4):
            sp.wait_ge(*after("x_ready", "fpost", 2 * g + 1))
            sp.dma_start(a["y"][:, 2 * g:2 * g + 2], x_sb[:, 2 * g:2 * g + 2]).then_inc(C.sem["y_out"], 16)
        sp.wait_ge(C.sem["y_out"], 16 * 4)

    return C.at


N_CONST = 3
N_MISC = 2
N_MIXER = 10


def _constants():
    f = np.float32
    i = np.arange(P)
    c = {}
    c["ones"] = np.ones((P, P), f)
    c["ones64"] = (i[:, None] // HD == i[None] // HD).astype(f)
    c["ident"] = np.eye(P, dtype=f)
    x = np.arange(T)
    c["causal"] = np.where(x[None] - (T - P) <= i[:, None], 0.0, NEG).astype(f)
    c["sbm"] = np.stack([-(i[:, None] >= i[None]).astype(f), -np.ones((P, P), f), (i[None] > i[:, None]).astype(f),
                         np.where(i[None] > i[:, None], 0.0, NEG).astype(f)], axis=1)
    exact = N_BUCKETS // 2
    dist = np.concatenate([T - 1 - np.arange(640), np.arange(1024) - T])
    d = np.maximum(dist, 1).astype(f)
    large = exact + (np.log(d / f(exact)) / f(np.log(128 / exact)) * f(N_BUCKETS - exact)).astype(np.int32)
    bucket = np.where(dist < exact, dist, np.minimum(large, N_BUCKETS - 1))
    bucket = np.where(dist < 0, N_BUCKETS, bucket)
    c["onehot"] = (np.arange(N_BUCKETS + 1)[:, None] == bucket[None]).astype(f)
    inv = (1.0 / (f(10000.0) ** (np.arange(0, 32, 2, dtype=f) / f(32)))).astype(f)
    ang = np.arange(T, dtype=f)[None] * inv[:, None]
    cos, sin = np.cos(ang), np.sin(ang)
    c["rope_c"] = np.concatenate([np.ones((HD, T), f), cos, cos]).astype(f)
    c["rope_s"] = np.concatenate([np.zeros((HD, T), f), -sin, sin]).astype(f)
    log_g = np.log1p(-np.exp2(-5.0 - np.arange(4)))
    rel = (x[None] - i[:, None])
    c["decay"] = np.stack([np.where(rel >= 0, np.exp(rel * g), 0.0) * P ** -0.5 for g in log_g], axis=1).astype(f)
    c["gscan"] = np.broadcast_to((x % GC != 0).astype(f), (P, T))
    c["gmask"] = ((i[:, None] // GC == i[None] // GC) & (i[:, None] <= i[None])).astype(f)
    slope = np.exp2(-8.0 * np.arange(1, 17) / 16)
    dd = P + i[:, None] - np.arange(2 * P)[None]
    c["alibi"] = np.stack([np.where((dd >= 0) & (dd < P), -slope[SWA_HEAD[k // 2][k % 2]] * dd, NEG)
                           for k in range(16)], axis=1).astype(f)
    return c


def _fm(w):
    n = w.shape[1] // P
    return w.reshape(KD, P, n, P).transpose(2, 1, 0, 3).reshape(n, P, 1024)


def _tm(w, per):
    w = np.pad(w, ((0, 0), (0, 1024 // per - w.shape[1])))
    return w.reshape(KD // per, per, P, 1024 // per).transpose(0, 2, 1, 3).reshape(KD // per, P, 1024)


def _down(w):
    nk = w.shape[0] // P
    blocks = w.reshape(nk, P, KD, P).transpose(2, 0, 1, 3).reshape(KD * nk, P, P)
    return blocks.reshape(-1, 8, P, P).transpose(0, 2, 1, 3).reshape(-1, P, 1024)


def _weights(v):
    w1 = v["w_in"][0]
    sizes = [256] * 3 + [256] + [64] * 6 + [12] + [192, 128, 32] + [256] * 3
    at = np.concatenate([[0], np.cumsum(sizes)])
    ab, ac, au, nq, kc, vc, ks, vs, kw, vw, ng, cq, ckv, kr, sq, sk, sv = [
        w1[:, at[i]:at[i + 1]] for i in range(len(sizes))]
    zeros = lambda n: np.zeros((D, n), w1.dtype)
    one = lambda w: _fm(w)[0]
    slot = {"kvc": one(np.concatenate([kc, vc], 1)), "ksw": one(np.concatenate([ks, kw], 1)),
            "cq0": one(cq[:, :P]), "cqr": one(np.concatenate([cq[:, P:], kr, zeros(32)], 1)), "ckv": one(ckv)}
    for c in range(2):
        cc = slice(c * P, (c + 1) * P)
        slot.update({f"nq{c}": one(nq[:, cc]), f"sq{c}": one(sq[:, cc]), f"sk{c}": one(sk[:, cc]),
                     ("ab", c): one(ab[:, cc]), ("ac", c): one(ac[:, cc]), ("au", c): one(au[:, cc])})
    slot["v1"] = _tm(np.concatenate([vs, vw, sv, ng], 1), 2)
    for kv in range(2):
        for s, w in enumerate(v["cmp_w1"][0, kv].reshape(4, 4, P, 256).transpose(0, 2, 1, 3).reshape(4, P, 1024)):
            slot[("cmp", kv, s)] = w
    for c, s in enumerate(_fm(v["w_out"][0])):
        slot[("wout", c)] = s
    for half in range(2):
        for c in range(HALF1):
            g = half * HALF1 + c
            slot[("up1", half, c)] = one(v["ffn_w1"][0][:, g * P:(g + 1) * P])
        slot[("down1", half)] = _down(v["ffn_w2"][0][half * HALF1 * P:(half + 1) * HALF1 * P])
    w2 = v["w_in_2"][0]
    sizes = [512, 512, 1024, 1024, 512, 512, 1024, 1024, 16, 1024, 256, 256, 3072]
    at = np.concatenate([[0], np.cumsum(sizes)])
    rq, rk, rv, rg, gq, gk, gv, gg, ga, sq, sk, sv, gate = [w2[:, at[i]:at[i + 1]] for i in range(len(sizes))]
    for h in range(4):
        for name, w in (("rq", rq), ("rk", rk), ("gq", gq), ("gk", gk)):
            slot[(name, h)] = one(w[:, h * P:(h + 1) * P])
        for name, w in (("rg", rg), ("gg", gg)):
            for e in range(2):
                slot[(name, h, e)] = one(w[:, (2 * h + e) * P:(2 * h + e + 1) * P])
    for g in range(2):
        slot[("rv", g)] = _tm(rv[:, g * 512:(g + 1) * 512], 2)
        slot[("gv", g)] = _tm(gv[:, g * 512:(g + 1) * 512], 2)
    slot["ga"] = one(np.concatenate([ga, zeros(P - 16)], 1))
    pairs = [h for c in SWA_HEAD for h in c]
    sq = sq.reshape(D, 16, HD)[:, pairs].reshape(D, 1024)
    for c in range(8):
        slot[("wq", c)] = one(sq[:, c * P:(c + 1) * P])
    for c in range(2):
        slot[("wk", c)] = one(sk[:, c * P:(c + 1) * P])
    slot["wv"] = _tm(sv, 4)
    for b in range(3):
        wb = v["w_branch_2"][0, b]
        if b == 2:
            wb = wb.reshape(16, HD, D)[pairs].reshape(1024, D)
        for m in range(KD):
            mm = slice(m * P, (m + 1) * P)
            slot[("gate", b, m)] = one(gate[:, b * D:(b + 1) * D][:, mm])
            slot[("br", b, m)] = one(wb[:, mm])
    for c, s in enumerate(_fm(v["w_out_2"][0])):
        slot[("wout2", c)] = s
    for half in range(2):
        for c in range(HALF2):
            g = slice((half * HALF2 + c) * P, (half * HALF2 + c + 1) * P)
            slot[("fg", half, c)] = one(v["ffn_w_gate_2"][0][:, g])
            slot[("fu", half, c)] = one(v["ffn_w_up_2"][0][:, g])
        slot[("down2", half)] = _down(v["ffn_w_down_2"][0][half * HALF2 * P:(half + 1) * HALF2 * P])
    def of(name, n):
        if isinstance(name, tuple) and name[-2:-1] == ("s",):
            return slot[name[0]].reshape(-1, P, 1024)[name[-1]][None]
        return slot[name].reshape(n, P, 1024)

    return np.concatenate([of(name, n) for name, (_, n) in SLOTS.items()])


def _params(v):
    f = v["x"].dtype
    cols = lambda w: np.pad(w, (0, -len(w) % P)).reshape(-1, P).T
    twice = lambda w: np.concatenate([w, w])[:, None]
    pos = v["cmp_pos"][0].reshape(2, 16, P)
    parts = [cols(v["norm1_w"][0]),
             np.concatenate([cols(v["conv_w"][0, k]) for k in range(3)], 1), cols(v["conv_b"][0]),
             twice(v["nsa_q_norm"][0]), twice(v["nsa_k_norm"][0, 0]),
             v["nsa_k_norm"][0, 1:3].reshape(P, 1),
             cols(v["mla_q_a_norm"][0]), cols(v["mla_kv_norm"][0]), cols(v["mla_q_norm"][0]),
             cols(v["mla_k_norm"][0]), cols(v["out_norm_w"][0]), cols(v["norm2_w"][0]),
             pos.reshape(32, P).T, cols(v["norm_mix_pre_2"][0]), cols(v["norm_mix_post_2"][0]),
             cols(v["ret_norm_w_2"][0]), cols(v["ret_norm_b_2"][0]), cols(v["gla_b_alpha_2"][0]),
             cols(v["gla_norm_w_2"][0]), cols(v["norm_ffn_pre_2"][0]), cols(v["norm_ffn_post_2"][0]),
             np.broadcast_to(v["attn_sinks_2"][0][[h for c in SWA_HEAD for h in c]][None], (P, 16)),
             np.arange(P)[:, None] // 32 == np.arange(NH)]
    return np.ascontiguousarray(np.concatenate(parts, axis=1).astype(f))


def _arrays(v):
    f = np.float32
    out = dict(_constants())
    out["x"] = v["x"][0].reshape(T, KD, P).transpose(2, 1, 0)
    out["w"] = _weights(v)
    out["par"] = _params(v)
    out["rel_bias"] = v["rel_bias"]
    w2 = v["cmp_w2"][0]
    out["w2k"] = np.concatenate([w2[0], w2[0]], 1).reshape(2, P, P).transpose(1, 0, 2)
    out["w2v"] = w2[1].reshape(2, P, HD).transpose(1, 0, 2)
    wqb = v["mla_wq_b"][0].reshape(192, NH, QKD)
    turned = np.concatenate([wqb[:, :, :HD], wqb[:, :, HD + 16:], wqb[:, :, HD:HD + 16]], axis=2)
    both = np.pad(np.stack([wqb, turned], 1), ((0, 64), (0, 0), (0, 0), (0, 0)))
    out["wqb"] = both.reshape(2, P, 2, NH, QKD).transpose(1, 0, 2, 3, 4)
    wkv = v["mla_wkv_b"][0].reshape(P, NH, 2 * HD)
    out["wkb"] = np.pad(wkv[:, :, :HD], ((0, 0), (0, 0), (0, 32)))
    out["wvb"] = wkv[:, :, HD:].reshape(P, NH * HD)
    out["wa2"] = v["gla_w_alpha2_2"][0]
    return {k: np.ascontiguousarray(t) for k, t in out.items()}


def _program_in(nc, arrays, known):
    a = {k: nc.dram_tensor(f"in_{k}", t.shape, mybir.dt.from_np(t.dtype), kind="ExternalInput").ap()
         for k, t in arrays.items()}
    a["scratch"] = nc.dram_tensor("scratch", (NH, 2, P * 1024), F32, kind="Internal").ap()
    a["table"] = nc.dram_tensor("table", (NH, 640 + 1024), F32, kind="Internal").ap()
    a["y"] = nc.dram_tensor("out_y", (P, KD, T), F32, kind="ExternalOutput").ap()
    return build(nc, a, known)


def kernel(**inputs):
    import concourse.bacc as _bacc
    from concourse.bass_utils import run_bass_kernel_spmd as _run

    arrays = _arrays({k: np.asarray(t) for k, t in inputs.items()})
    counting = _bacc.Bacc("TRN2", target_bir_lowering=False, num_devices=1)
    counts = _program_in(counting, arrays, {})
    nc = _bacc.Bacc("TRN2", target_bir_lowering=False, num_devices=1)
    _program_in(nc, arrays, counts)
    r = _run(nc, [{f"in_{k}": t for k, t in arrays.items()}], core_ids=[0])
    y = r.results[0]["out_y"]
    return np.ascontiguousarray(y.transpose(2, 1, 0).reshape(1, T, D))
```

```python
from contextlib import ExitStack

import numpy as np

import concourse.bass as bass
from concourse import mybir

ALU = mybir.AluOpType
ACT = mybir.ActivationFunctionType
F32 = mybir.dt.float32
F32R = mybir.dt.float32r
AX = mybir.AxisListType.X

P = 128
T = 512
NT = T // P
D = 1024
KD = D // P
EPS = 1e-6
GN_EPS = 1e-5
NEG = -1.0e30
CMP_LEN, CMP_STRIDE = 32, 16
N_CMP = (T - CMP_LEN) // CMP_STRIDE + 1
NH = 4
HD = 64
N_BUCKETS = 32
QKD = 96
F1 = 4 * D // P
HALF1 = F1 // 2
F2 = 2816 // P
HALF2 = F2 // 2
GC = 64
NGC = T // GC
RAW = 3
SPL = 3
POOLED = (4, 7)
POOLED_ORDER = (0, 1, 2, 4, 3, 5, 7, 6)

PCOL = {}


def _columns():
    at = 0
    for name, n in (("norm1", 8), ("conv_w", 6), ("conv_b", 2), ("nsa_q", 1), ("nsa_k", 2), ("mla_qa", 2),
                    ("mla_kv", 1), ("mla_q", 1), ("mla_k", 1), ("out_norm", 8), ("norm2", 8), ("pos", 32),
                    ("pre", 8), ("post", 8), ("ret_w", 8), ("ret_b", 8), ("b_alpha", 4), ("gla_w", 8),
                    ("fpre", 8), ("fpost", 8), ("sinks", 16), ("head_of", 4)):
        PCOL[name] = at
        at += n
    return at


NPCOL = _columns()
SWA_HEAD = [[(2 * (c // 4) + hf) * 4 + c % 4 for hf in range(2)] for c in range(8)]


def plan():
    order, slots = [], {}

    def lin(name, kind, n_slots, *args):
        slots[name] = (sum(n for _, n in slots.values()), n_slots)
        order.append((kind, name) + args)

    def fm(name, src="h"):
        lin(name, "fm", 1, src)

    def together(names, src="h"):
        first = len(order)
        for name in names:
            fm(name, src)
        ends = order[first:]
        del order[first:]
        return (lambda k0, k1: ("fmk", tuple(names), src, k0, k1)), ends

    def quarters(name, src="h"):
        def quarter(k):
            if k == 0:
                held.extend(together([name], src))
            order.append(held[0](k, k + 2))
            if k + 2 == KD:
                order.extend(held[1])
        held = []
        return [lambda k=k: quarter(k) for k in range(0, KD, 2)]

    def tm(name, ns, cols):
        return [lambda s=s: lin((name, "s", s), "tm", 1, name, cols, s, ns) for s in range(ns)]

    def sqs(key, n):
        return [("sq", key, c) for c in range(n)]

    def attention(pairs):
        n, steps = len(pairs), []
        for i in range(n + 2):
            for lag, stage in ((0, "att_scores"), (0, "att_norm"), (1, "att_turn"), (2, "att_pv")):
                if 0 <= i - lag < n:
                    steps.append((stage, pairs[i - lag]))
        return steps

    def weave(main, filler):
        n = 0
        for i, step in enumerate(main):
            put(step)
            while n < len(filler) and n * len(main) < (i + 1) * len(filler):
                put(filler[n])
                n += 1
        for step in filler[n:]:
            put(step)

    def put(step):
        if callable(step):
            step()
        else:
            order.append(step)

    def F(name, src="h"):
        return lambda: fm(name, src)

    def run(steps):
        for step in steps:
            put(step)

    def down(name, nk, key):
        slots[name] = (sum(n for _, n in slots.values()), KD * nk // 8)
        for o in range(KD):
            order.append(("down", name, nk, o))
            if name[1] == 1:
                order.append(("sq", key, o))

    run(sqs("n1", KD) + [("norm", "n1"), ("apply_h", "n1", "norm1"), ("bias_tables", 0)])
    part, ends = together(("kvc", "ksw", "nq0"))
    run([part(0, KD)] + ends)

    def U(kv, s):
        return lambda: lin(("cmp", kv, s), "cmp_up", 1, kv, s)

    v1 = tm("v1", 4, 396)
    run([("sq", "ksw", 0), F("nq1"), ("sq", "nq0", 0), ("norm", "ksw"), ("cmp_x", 0), ("nsa_apply", "ksw"),
         F("cq0"), ("sq", "nq1", 0), ("norm", "nq0"), ("cmp_x", 1), ("nsa_apply", "nq0"),
         U(0, 0), F("cqr"), ("norm", "nq1"), ("nsa_apply", "nq1"), ("sq", "cq", 0), ("sq", "cq", 1),
         U(0, 1), F("ckv"), ("norm", "cq"), ("sq", "ckv", 0),
         U(0, 2), F("sq0"), ("norm", "ckv"), ("mla_lora", 0), U(0, 3), F("sq1"), ("mla_rope_k", 0),
         U(1, 0), F("sk0"), U(1, 1), F("sk1"), U(1, 2), v1[0], U(1, 3), v1[1], v1[2],
         ("cmp_turn_h", 0), v1[3]])
    filler = []
    for h in range(NH):
        lin4 = quarters((("ac", 0), ("au", 0), ("ab", 0), ("ac", 1))[h])
        filler += [("mla_qk", h), ("sq", ("mk", h), 0)] + lin4[:2] + [("mla_rope_q", h), ("sq", ("mq", h), 0),
                   ("norm", ("mk", h))] + lin4[2:] + [("norm", ("mq", h)), ("mla_scale", h)]
    run([("cmp_bias", 0), ("cmp_down", 0), ("sq", "kcmp", 0), ("mla_v", 0)] + filler[:5] + [("norm", "kcmp"), ("cmp_apply", 0)] +
        filler[5:10] + [("cmp_scores", 0)] + filler[10:16] + [("cmp_turn", 0)])
    filler = filler[16:]

    def halves(kind, pair, qt):
        return tuple((kind, 2 * pair + hf, qt) for hf in range(2))

    weave(attention([halves(kind, pair, qt) for pair in range(2) for qt in range(NT) for kind in ("slc", "win")]), filler)
    order.append(("x_again", 0))
    tiles = [(pair, kt) for pair in range(2) for kt in reversed(range(NT))]
    sbs = []
    for n in range(len(tiles) + 2):
        if n < len(tiles):
            sbs.append(("sb_scores",) + tiles[n])
        if n >= 2 and (n - 2) % NT == NT - 1:
            sbs.append(("sb_pv", tiles[n - 2][0]))
        if 1 <= n <= len(tiles):
            sbs.append(("sb_exp",) + tiles[n - 1])
    cut = len(sbs) - 7
    conv = quarters(("au", 1)) + quarters(("ab", 1))
    mixed = []
    for n in range(4):
        mixed += sbs[n:n + 1] + conv[2 * n:2 * n + 2]
    mixed += sbs[4:5] + sqs(("y", 0), 2) + sbs[5:6] + [("norm", ("y", 0))] + sqs(("y", 1), 2) + sbs[6:7]
    mixed += [("y_out", 0), ("norm", ("y", 1))] + sbs[7:8] + [("y_out", 1)] + sbs[8:cut]
    weave(attention([halves("mla", pair, qt) for pair in range(2) for qt in range(NT)]), mixed)
    run(sbs[cut:cut + 1] + sqs(("y", 2), 2) + sbs[cut + 1:cut + 3] + [("norm", ("y", 2))] + sbs[cut + 3:cut + 4] +
        [("y_out", 2)] + sbs[cut + 4:-2])
    part, ends = together([("wout", c) for c in range(3)])
    run([part(0, 2), sbs[-2], part(2, 3), sbs[-1], ("x_again", 1)] + sqs(("y", 3), 2) +
        [part(3, 6), ("norm", ("y", 3)), ("y_out", 3), part(6, KD)])
    for c in range(KD):
        run(ends[c:c + 1] or [F(("wout", c))])
        order.append(("sq", "n2", c))
    order.append(("norm", "n2"))
    order.append(("apply_h", "n2", "norm2"))
    part, ends = together([("up1", 0, c) for c in range(3)])
    run([part(0, KD)] + ends)
    for half in range(2):
        for c in range(3 * (half == 0), HALF1):
            fm(("up1", half, c))
        down(("down1", half), HALF1, "pre")

    def branch(b, after_gates=(), whole=lambda name, src="h": [F(name, src)]):
        steps = whole(("gate", b, 0)) + whole(("gate", b, 1)) + list(after_gates)
        for m in range(KD):
            steps += whole(("br", b, m), "o")
            if m + 2 < KD:
                steps += whole(("gate", b, m + 2))
        return steps

    order.append(("norm", "pre"))
    order.append(("apply_h", "pre", "pre"))
    part, ends = together([("rq", 0), ("rk", 0), ("rq", 1)])
    run([part(0, KD)] + ends + tm(("rv", 0), 4, 512))
    for h in range(4):
        run([("ret_scores", h, jt) for jt in range(NT)])
        if h:
            put(("ret_out", h - 1))
        run([F(("rg", h, 0)), ("ret_pv", h), ("ret_sum", h), F(("rg", h, 1)), ("ret_mean", h)])
        if h < 3:
            run(([F(("rq", h + 1))] if h else []) + sqs(("ret", h), 2) + [F(("rk", h + 1)), ("norm", ("ret", h))])
        if h == 1:
            run(tm(("rv", 1), 4, 512))
    steps = branch(0)
    run(steps[:1] + sqs(("ret", 3), 2) + steps[1:2] + [("norm", ("ret", 3)), ("ret_out", 3), F("ga"), F(("gq", 0))] +
        steps[2:] + tm(("gv", 0), 4, 512) + [F(("gk", 0)), ("gla_decay", 0), ("gla_scale", 0)])
    for h in range(4):
        nxt = (("gq", h + 1), ("gk", h + 1)) if h < 3 else (("gate", 1, 0), ("wq", 0))
        run([F(("gg", h, 0)), F(("gg", h, 1)), ("gla_turn", h), F(nxt[0]), ("gla_chunks", h)])
        if h == 1:
            run(tm(("gv", 1), 4, 512))
        run(sqs(("gla", h), 2))
        if h < 3:
            put(("gla_decay", h + 1))
        run([F(nxt[1]), ("norm", ("gla", h))])
        if h < 3:
            put(("gla_scale", h + 1))
        put(("gla_out", h))
    run([F(("wk", c)) for c in range(2)] + tm("wv", 2, 256))
    filler = branch(1, whole=quarters)[4:]
    for c, at in ((1, 0), (2, 3), (3, 5), (4, 8), (5, 10), (6, 13), (7, 15)):
        filler[4 * at:4 * at] = quarters(("wq", c))
    weave(attention([tuple(("swa", c, hf, qt) for hf in range(2)) for c in range(8) for qt in range(NT)]), filler)
    run(branch(2, [("swa_split", 0)]))
    for c in range(KD):
        run([F(("wout2", c), "m"), ("sq", "post", c)])
    order.append(("norm", "post"))
    for c in POOLED_ORDER:
        run([("residual", "post", c), ("sq", "fpre", c)])
    order.append(("norm", "fpre"))
    order.append(("apply_h", "fpre", "fpre"))
    part, ends = together([("fg", 0, 0), ("fu", 0, 0), ("fg", 0, 1)])
    run([part(0, KD)] + ends + [F(("fu", 0, 1))])
    for half in range(2):
        for c in range(2 * (half == 0), HALF2):
            fm(("fg", half, c))
            fm(("fu", half, c))
        down(("down2", half), HALF2, "fpost")
    order.append(("norm", "fpost"))
    for c in POOLED_ORDER:
        order.append(("residual", "fpost", c))
    return order, slots


ORDER, SLOTS = plan()
N_SLOTS = sum(n for _, n in SLOTS.values())
TOGETHER = {name for step in ORDER if step[0] == "fmk" for name in step[1]}
PE_SUM = ("fpre",)

SEMAPHORES = {
    "const_in": "the constants that the first norm needs", "misc_in": "the bias tables' operands",
    "mixer_in": "block 1's small weights and tables", "late_in": "block 2's tables",
    "x_back": "x again, for the output projection", "kv_in": "the compressor's shifted K and V",
    "ksw_in": "NSA's keys in the other half", "kr_in": "rotary halves exchanged",
    "table_out": "the bias tables are in DRAM", "bias_out": "their rows are", "bias_in": "the biases are back",
    "y_out": "a chunk of the output is written",
    "w_hi": "a slot's hi", "w_lo": "a slot's lo, and so the slot", "slot_used": "a split slot is multiplied",
    "h_t": "a normed chunk", "h_hi": "its hi", "h_ready": "its lo, and so the chunk",
    "o_ready": "a chunk of a branch's output", "m_ready": "a chunk of the merged branches",
    "hid_s": "a squared hidden chunk", "hid": "a split hidden chunk",
    "x_ready": "a chunk of x by VectorE", "x_pool": "a chunk of x by GpSimd",
    "v_chain": "VectorE", "s_chain": "ScalarE", "p_chain": "GpSimd",
    "sq_s": "a chunk's squares", "sq_v": "their sum so far", "sq_pe": "a chunk's squares are summed on TensorE",
    "rstd": "1 / rms", "rstd_used": "it has been applied", "table": "the epsilons",
    "far_row": "the masked row of the bias table", "zeros": "the latents' unused rows", "gate_v": "the gates",
    "cmpx": "the compressor's operand", "cmp_s": "ScalarE's exps", "cmp_v": "VectorE's parts",
    "att_n": "a unit's negated maxima", "att_exp": "its exps", "att_p": "its weights", "att_done": "its V product",
    "swa_s": "the sink's exp",
    "mla_k": "the rotary key", "mla_q": "a head's rotated query", "sb_exp": "ln(1 + exp(-|z|))", "conv_v": "a chunk",
    "gate_s": "a sigmoid", "ret_s": "retention's chunks summed", "ret_d": "its deviations", "ret_done": "they are read",
    "gla_s": "GLA's exps and logarithms", "gla_v": "VectorE's parts", "gla_done": "its output is read",
}


class Counts:

    def __init__(self, known):
        self.known = known
        self.at = {}
        self.n = {}
        self.sem = {}

    def did(self, name, *key, by=1):
        self.n[name] = self.n.get(name, 0) + by
        assert (name, key) not in self.at, (name, key)
        self.at[(name, key)] = self.n[name]
        return self.sem[name], by

    def after(self, name, *key):
        v = self.at.get((name, key)) or self.known.get((name, key))
        assert v or not self.known, (name, key)
        return self.sem[name], v or 1


def build(nc, a, known):
    ctx = ExitStack()
    with ctx:
        return _program(ctx, nc, a, known)


def _program(ctx, nc, a, known):
    C = Counts(known)
    did, after = C.did, C.after
    for name in SEMAPHORES:
        C.sem[name] = ctx.enter_context(nc.semaphore(name))
    for s in range(RAW):
        C.sem[f"w_landed{s}"] = ctx.enter_context(nc.semaphore(f"w_landed{s}"))
    for g in range(4):
        C.sem[f"x_in{g}"] = ctx.enter_context(nc.semaphore(f"x_in{g}"))
    for c in range(8):
        C.sem[f"alibi_in{c}"] = ctx.enter_context(nc.semaphore(f"alibi_in{c}"))
    for b in range(8):
        for what in ("bank_full", "bank_free"):
            C.sem[f"{what}{b}"] = ctx.enter_context(nc.semaphore(f"{what}{b}"))

    def sb(name, shape, dt=F32):
        return ctx.enter_context(nc.sbuf_tensor(name, shape, dt))

    bank = [ctx.enter_context(nc.psum_tensor(f"bank{b}", [P, 512], F32)) for b in range(8)]

    x_sb = sb("x_sb", [P, KD, T])
    h_hi, h_lo = sb("h_hi", [P, KD, T], F32R), sb("h_lo", [P, KD, T], F32R)
    w_raw = sb("w_raw", [P, RAW, 1024])
    w_hi, w_lo = sb("w_hi_t", [P, SPL, 1024], F32R), sb("w_lo_t", [P, SPL, 1024], F32R)
    par = sb("par", [P, NPCOL])
    ones = sb("ones", [P, P])
    ident = sb("ident", [P, P])
    causal = sb("causal", [P, T])
    sq = sb("sq", [P, 2, T])
    sq_sum = sb("sq_sum", [P, T])
    rstd_t = sb("rstd_t", [P, 3, T])
    tmp = sb("tmp", [P, 2, T])
    att_l = sb("att_l_t", [P, 4, T])
    att_pt = sb("att_pt", [P, 2, T])
    small = sb("small", [P, 4, 8])
    epst = sb("epst", [P, 8])

    area = ExitStack()

    def sa(name, shape, dt=F32):
        return area.enter_context(nc.sbuf_tensor(name, shape, dt))

    ones64 = sa("ones64", [P, P])
    y = sa("y", [P, KD, T])
    v1 = sa("v1", [P, NT, 396])
    gates = sa("gates", [P, NT, 12])
    rb = sa("rb", [N_BUCKETS + 1, NH])
    w2k, w2v = sa("w2k", [P, 2, P]), sa("w2v", [P, 2, HD])
    wqb = sa("wqb", [P, 2, NH, QKD])
    wkb = sa("wkb", [P, NH, QKD])
    wvb = sa("wvb", [P, NH * HD])
    rope_c, rope_s = sa("rope_c", [QKD, T]), sa("rope_s", [QKD, T])
    sbm = sa("sbm", [P, 3, P])
    part = ExitStack()

    def sp_(name, shape, dt=F32):
        return part.enter_context(nc.sbuf_tensor(name, shape, dt))

    nq, ks_d, kw_d, s_qk = x_sb[:, 0:2], x_sb[:, 2], x_sb[:, 3], x_sb[:, 4:8]
    cq, kr = y[:, 4:6], y[0:QKD, 6:8]
    conv_t = sa("conv_t", [P, 2, 2 + T])
    cmp_pt = sa("cmp_pt_t", [P, NT, P])
    tab = sp_("tab", [NH, 640 + 1024])
    part.close()
    cmp_x = [sp_("cmp_xh", [P, 2 * 16 * 32], F32R), sp_("cmp_xl", [P, 2 * 16 * 32], F32R)]
    mla_first = ExitStack()

    def sm_(name, shape, dt=F32):
        return mla_first.enter_context(nc.sbuf_tensor(name, shape, dt))

    onehot = sm_("onehot", [N_BUCKETS + 1, 640 + 1024])
    cb_t = sm_("cb_t", [N_CMP, NH, T])
    mla_first.close()
    kv_raw = sm_("kv_raw", [P, 2, T])
    mla_first.close()
    part.close()
    mk = sp_("mk", [P, NH, T])
    mv = sp_("mv", [P, NT, NH * HD])
    ckv = sp_("ckv", [P, T])
    sp_("rest of onehot", [P, 640 + 1024 - 1536])
    mq = sp_("mq", [P, NH, T])
    nsa = ExitStack()

    def sn(name, shape, dt=F32):
        return nsa.enter_context(nc.sbuf_tensor(name, shape, dt))

    toep = sn("toep", [P, NH, T])
    cmp_bias = sn("cmp_bias_t", [P, NT, NH, N_CMP])
    cmp_t = sn("cmp_t", [P, 256])
    cmp_h = sn("cmp_h", [P, 4, 32])
    cmp_k = sn("cmp_k_t", [P, 2, 32])
    cmp_hv = sn("cmp_hv", [P, 2, NH, 32])
    cmp_vt = sn("cmp_vt_t", [P, NH, HD])
    cmp_p = sn("cmp_p", [P, NT, NH, 32])
    cmp_s = sn("cmp_s_t", [P, 4, NT, NH])
    nsa.close()
    sb_e = sn("sb_e", [P, 2, T])
    sb_sp = sn("sb_sp_t", [P, 2, 1280])
    sb_a = sn("sb_a_t", [P, 2, 1280])
    nsa.close()
    part.close()
    area.close()

    hid1 = [area.enter_context(nc.sbuf_tensor(n, [P, HALF1, T], F32R)) for n in ("hid1_hi", "hid1_lo")]
    r1 = sa("r1", [P, 2, T])
    area.close()

    merged = sa("merged_t", [P, KD, T])
    sig = sa("sig", [P, 2, T])
    mixers = ExitStack()
    o_hl = [mixers.enter_context(nc.sbuf_tensor(n, [P, KD, T], F32R)) for n in ("o_hi", "o_lo")]
    inner = ExitStack()

    def si(name, shape, dt=F32):
        return inner.enter_context(nc.sbuf_tensor(name, shape, dt))

    qf, kf = si("qf", [P, 2, T]), si("kf", [P, 2, T])
    vt = si("vt", [P, NT, 512])
    silu = si("silu", [P, 2, T])
    mix_o = si("mix_o", [P, 2, T])
    fp = ExitStack()

    def sg(name, shape, dt=F32):
        return fp.enter_context(nc.sbuf_tensor(name, shape, dt))

    decay = sg("decay", [P, 4, T])
    ret_a = sg("ret_a_t", [P, 1280])
    ret_d = att_pt
    fp.close()
    ga_t = sg("ga_t", [16, T])
    wa2 = sg("wa2", [16, T])
    gscan = sg("gscan", [P, T])
    gmask = sg("gmask", [P, P])
    gk_i = sg("gk_i", [P, T])
    g_st = sg("g_st", [P, NGC - 1, 256])
    fp.close()
    g_ln, g_b, g_eb, g_ed = att_l[:, 0], att_l[:, 1], att_l[:, 2], att_l[:, 3]
    gk_t = att_pt[:, 0].rearrange("p (m k) -> p m k", m=NT)
    ga_m = att_pt[:, 1].rearrange("p (m i) -> p m i", m=NT)
    inner.close()
    wq = si("wq", [P, 8, T])
    wk = si("wk", [P, 2, T])
    wv = si("wv", [P, NT, 256])
    alibi = si("alibi", [P, 16, 256])
    swa_o = wq
    inner.close()
    m_hl = [si("m_hi", [P, KD, T], F32R), si("m_lo", [P, KD, T], F32R)]
    inner.close()
    mixers.close()
    f_acc = merged
    hid2 = [si("hid2_hi", [P, HALF2, T], F32R), si("hid2_lo", [P, HALF2, T], F32R)]
    sig2 = si("sig2", [P, 2, T])
    inner.close()
    area.close()

    lin_src = {"h": (h_hi, h_lo), "o": o_hl, "m": m_hl}

    def col(name, c=0, n=1, parts=P):
        return par[0:parts, PCOL[name] + c:PCOL[name] + c + n]

    tenants = {}
    n_tenants = [0] * 8

    def full(name):
        b, k = tenants[name]
        return C.sem[f"bank_full{b}"], k + 1

    def evacuated(name):
        b, k = tenants[name]
        return C.sem[f"bank_free{b}"], k + 1

    def release(name):
        return C.sem[f"bank_free{tenants[name][0]}"], 1

    def ps(name):
        return bank[tenants[name][0]]

    slot_done = {}

    def ev(name):
        return ("bank", name)

    norms = {
        "n1": ([x_sb[:, c] for c in range(KD)], P, T, ones, 1 / D, "eps", [("x", c // 2) for c in range(KD)]),
        "n2": ([x_sb[:, c] for c in range(KD)], P, T, ones, 1 / D, "eps", [ev(("wout", c)) for c in range(KD)]),
        "pre": ([x_sb[:, c] for c in range(KD)], P, T, ones, 1 / D, "eps",
                [ev(("down1", 1, c)) for c in range(KD)]),
        "post": ([merged[:, c] for c in range(KD)], P, T, ones, 1 / D, "eps",
                 [ev(("wout2", c)) for c in range(KD)]),
        "fpre": ([x_sb[:, c] for c in range(KD)], P, T, ones, 1 / D, "eps",
                 [("ev", "x_pool" if c in POOLED else "x_ready", "post", c) for c in range(KD)]),
        "fpost": ([f_acc[:, c] for c in range(KD)], P, T, ones, 1 / D, "eps",
                  [ev(("down2", 1, c)) for c in range(KD)]),
        "ksw": ([ks_d], P, T, ones64, 1 / HD, "eps", [ev("ksw")]),
        "nq0": ([nq[:, 0]], P, T, ones64, 1.0, "eps*64", [ev("nq0")]),
        "nq1": ([nq[:, 1]], P, T, ones64, 1.0, "eps*64", [ev("nq1")]),
        "kcmp": ([cmp_k[:, 0, 0:N_CMP]], P, N_CMP, ones64, 1 / HD, "eps", [ev("cmp_k")]),
        "cq": ([cq[:, c] for c in range(2)], P, T, ones, 1 / 192, "eps", [ev("cq0"), ev("cqr")]),
        "ckv": ([ckv[:]], P, T, ones, 1 / P, "eps", [ev("ckv")]),
    }
    for h in range(NH):
        norms[("mk", h)] = ([mk[0:QKD, h]], QKD, T, ones, 1 / QKD, "eps", [ev(("mk", h))])
        norms[("mq", h)] = ([mq[0:QKD, h]], QKD, T, ones, 1.0, "eps*96", [("ev", "mla_q", h)])
        norms[("ret", h)] = ([ret_d[:, e] for e in range(2)], P, T, ones, 1 / 256, "gn_eps",
                             [("ev", "ret_d", h, e) for e in range(2)])
        norms[("gla", h)] = ([mix_o[:, e] for e in range(2)], P, T, ones, 1 / 256, "eps",
                             [ev(("gla_o", h, e)) for e in range(2)])
    for g in range(4):
        srcs = ([("ev", "conv_v", c) for c in range(2)] if g == 0 else
                [ev(({1: "nsa_o", 2: "mla_o"}[g], c) if g < 3 else ("sb_o", c)) for c in range(2)])
        norms[("y", g)] = ([y[:, 2 * g + c] for c in range(2)], P, T, ones, 1 / 256, "eps", srcs)
    EPS_COL = {"eps": 0, "eps*64": 1, "eps*96": 2, "gn_eps": 3}
    EPS_VAL = [EPS, EPS * HD, EPS * QKD, GN_EPS]

    norm_order = []
    for step in ORDER:
        if step[0] == "norm":
            norm_order.append(step[1])
    norm_at = {k: i for i, k in enumerate(norm_order)}
    sq_use = {}
    for step in ORDER:
        if step[0] == "sq":
            sq_use[step[1:]] = len(sq_use)
    sq_uses = list(sq_use)

    def rstd(key):
        _, parts, cols, *_ = norms[key]
        return rstd_t[0:parts, norm_at[key] % 3, 0:cols]

    def wait_src(eng, w):
        if w[0] == "bank":
            eng.wait_ge(*evacuated(w[1]))
        elif w[0] == "ev":
            eng.wait_ge(*after(w[1], *w[2:]))
        else:
            eng.wait_ge(C.sem[f"x_in{w[1]}"], 16)

    def att(u):
        kind = u[0]
        if kind in ("slc", "win"):
            _, h, qt = u
            pb = HD * (h % 2)
            k = ks_d if kind == "slc" else kw_d
            v0 = 0 if kind == "slc" else HD
            g = 3 * h + (1 if kind == "slc" else 2)
            return dict(q=nq[pb:pb + HD, h // 2, qt * P:(qt + 1) * P], k=k[pb:pb + HD, 0:(qt + 1) * P],
                        w=(qt + 1) * P, bias=toep[:, h, (NT - 1 - qt) * P:T],
                        v=[v1[:, kt, v0:v0 + HD] for kt in range(qt + 1)],
                        out=("nsa_o", h // 2), pb=pb, qt=qt, first=False, last=kind == "win",
                        bank_first=(kind == "slc" and h % 2 == 0 and qt == 0),
                        bank_last=(kind == "win" and h % 2 == 1 and qt == NT - 1),
                        gate=gates[:, qt, g:g + 1])
        if kind == "mla":
            _, h, qt = u
            return dict(q=mq[0:QKD, h, qt * P:(qt + 1) * P], k=mk[0:QKD, h, 0:(qt + 1) * P], w=(qt + 1) * P,
                        bias=causal[:, (NT - 1 - qt) * P:T],
                        v=[mv[:, kt, h * HD:(h + 1) * HD] for kt in range(qt + 1)],
                        out=("mla_o", h // 2), pb=HD * (h % 2), qt=qt, first=True, last=True,
                        bank_first=(h % 2 == 0 and qt == 0), bank_last=(h % 2 == 1 and qt == NT - 1), gate=None)
        _, c, hf, qt = u
        pb, lo = HD * hf, max(0, qt - 1)
        kv = 2 * (c // 4) + hf
        return dict(q=wq[pb:pb + HD, c, qt * P:(qt + 1) * P], k=wk[pb:pb + HD, c // 4, lo * P:(qt + 1) * P],
                    w=(qt + 1 - lo) * P, bias=alibi[:, 2 * c + hf, (0 if qt else P):2 * P],
                    v=[wv[:, kt, kv * HD:(kv + 1) * HD] for kt in range(lo, qt + 1)],
                    out=("swa_o", c), pb=pb, qt=qt, first=True, last=True,
                    bank_first=(hf == 0 and qt == 0), bank_last=(hf == 1 and qt == NT - 1), gate=None,
                    sink=col("sinks", 2 * c + hf))

    att_order = [u for s in ORDER if s[0] == "att_scores" for u in s[1]]
    att_at = {u: i for i, u in enumerate(att_order)}

    sig_names = [s[1] for s in ORDER if s[0] == "fm" and isinstance(s[1], tuple) and s[1][0] in ("rg", "gg", "gate")]
    sig_at = {name: i for i, name in enumerate(sig_names)}

    def sig_user(n):
        name = sig_names[n]
        return ("br",) + name[1:] if name[0] == "gate" else name

    TAB = ((0, 512), (512, 128), (640, 512), (1152, 512))
    SB_OFF = [0, 512, 896, 1152]
    sb_order = [(2 * s[1] + hf, s[2]) for s in ORDER if s[0] == "sb_scores" for hf in range(2)]

    block = ctx.enter_context(nc.Block())

    @block.tensor
    def _(pe):
        filled = list(range(8))

        def take(name):
            b = filled.pop(0)
            if n_tenants[b]:
                pe.wait_ge(C.sem[f"bank_free{b}"], n_tenants[b])
            tenants[name] = (b, n_tenants[b])
            n_tenants[b] += 1
            return bank[b]

        def fill(name, ins, keep=False):
            b = tenants[name][0]
            ins.then_inc(C.sem[f"bank_full{b}"], 1)
            if not keep:
                filled.append(b)

        def take_over(name, old):
            b = tenants[old][0]
            pe.wait_ge(C.sem[f"bank_free{b}"], n_tenants[b])
            tenants[name] = (b, n_tenants[b])
            n_tenants[b] += 1
            return bank[b]

        def mm(out, lhs, rhs, start, stop, **kw):
            return pe.matmul(out, lhs, rhs, start=start, stop=stop, **kw)

        def mm3(out, wh, wl, xh, xl, start, stop):
            mm(out, wh, xh, start, False)
            mm(out, wh, xl, False, False)
            return mm(out, wl, xh, False, stop)

        def slot_ready(i):
            pe.wait_ge(*after("w_lo", i))

        def slot_free(i, ins=None, name=None):
            if name is not None:
                slot_done[i] = full(name)
            else:
                ins.then_inc(*did("slot_used", i))
                slot_done[i] = after("slot_used", i)

        def ms(key, n_src):
            srcs, parts, cols, one, *_ = norms[key]
            if key in PE_SUM:
                return
            out = take(("ms", key))
            if n_src == 1:
                pe.wait_ge(*after("sq_s", key, 0))
                rhs = sq[0:parts, sq_use[(key, 0)] % 2, 0:cols]
            elif n_src == KD:
                pe.wait_ge(*after("sq_v", key, KD - 2))
                mm(out[:], one[:], sq_sum[:], True, False)
                pe.wait_ge(*after("sq_s", key, KD - 1))
                fill(("ms", key), mm(out[:], one[:], sq[:, sq_use[(key, KD - 1)] % 2], False, True))
                return
            else:
                pe.wait_ge(*after("sq_v", key, n_src - 1))
                rhs = sq_sum[0:parts, 0:cols]
            fill(("ms", key), mm(out[0:parts, 0:cols], one[0:parts, 0:parts], rhs, True, True))

        def x_chunk_ready(src, name, k):
            chunk = {"h": ("h_ready", seen_h, k), "o": ("o_ready", name[1], k), "m": ("m_ready", k)}[src]
            if chunk not in chunks_seen:
                chunks_seen.add(chunk)
                pe.wait_ge(*after(*chunk))

        pe.wait_ge(C.sem["const_in"], 16 * N_CONST)
        seen_h, chunks_seen = None, set()
        for step in ORDER:
            stage = step[0]
            if stage == "bias_tables":
                pe.wait_ge(C.sem["misc_in"], 16 * N_MISC)
                pe.wait_ge(*after("far_row"))
                for n, (c0, w) in enumerate(TAB):
                    out = take(("tab", n))
                    fill(("tab", n), mm(out[0:NH, 0:w], rb[:], onehot[:, c0:c0 + w], True, True))
            elif stage == "norm":
                ms(step[1], len(norms[step[1]][0]))
            elif stage == "sq" and step[1] in PE_SUM:
                _, key, c = step
                first, final = c == POOLED_ORDER[0], c == POOLED_ORDER[-1]
                out = take(("ms", key)) if first else ps(("ms", key))
                pe.wait_ge(*after("sq_s", key, c))
                ins = mm(out[:], ones[:], sq[:, sq_use[(key, c)] % 2], first, final)
                if final:
                    fill(("ms", key), ins)
                else:
                    ins.then_inc(*did("sq_pe", key, c))
            elif stage == "apply_h":
                seen_h = step[1]
            elif stage == "y_out":
                seen_h = "y"
            elif stage == "fmk":
                _, names, src, k0, k1 = step
                for name in names:
                    if k0 == 0:
                        slot_ready(SLOTS[name][0])
                        take(name)
                xh, xl = lin_src[src]
                blocks = [(k, name) for k in range(k0, min(k1, KD - 2)) for name in names]
                blocks += [(k, name) for name in names for k in range(max(k0, KD - 2), k1)]
                for k, name in blocks:
                    i = SLOTS[name][0]
                    wsl = slice(k * P, (k + 1) * P)
                    wh, wl = w_hi[:, i % SPL, wsl], w_lo[:, i % SPL, wsl]
                    if src == "h" and ("h_ready", seen_h, k) not in chunks_seen:
                        pe.wait_ge(*after("h_hi", seen_h, k))
                        mm(ps(name)[:], wh, xh[:, k], k == 0, False)
                        mm(ps(name)[:], wl, xh[:, k], False, False)
                        x_chunk_ready(src, name, k)
                        last = mm(ps(name)[:], wh, xl[:, k], False, k == KD - 1)
                    else:
                        x_chunk_ready(src, name, k)
                        last = mm3(ps(name)[:], wh, wl, xh[:, k], xl[:, k], k == 0, k == KD - 1)
                    if k == KD - 1:
                        fill(name, last)
                        slot_free(i, name=name)
            elif stage == "fm" and step[1] not in TOGETHER:
                _, name, src = step
                i = SLOTS[name][0]
                xh, xl = lin_src[src]
                slot_ready(i)
                out = take(name)
                for k in range(KD):
                    x_chunk_ready(src, name, k)
                    wsl = slice(k * P, (k + 1) * P)
                    last = mm3(out[:], w_hi[:, i % SPL, wsl], w_lo[:, i % SPL, wsl], xh[:, k], xl[:, k],
                               k == 0, k == KD - 1)
                fill(name, last)
                slot_free(i, name=name)
            elif stage == "tm":
                _, slot, name, cols, s, ns = step
                i = SLOTS[slot][0]
                if s == 0:
                    for t in range(NT):
                        take((name, t))
                per = KD // ns
                slot_ready(i)
                for t in range(NT):
                    for kk in range(per):
                        k = s * per + kk
                        x_chunk_ready("h", name, k)
                        wsl = slice(kk * (1024 // per), kk * (1024 // per) + cols)
                        ts = slice(t * P, (t + 1) * P)
                        wh, wl = w_hi[:, i % SPL, wsl], w_lo[:, i % SPL, wsl]
                        o = ps((name, t))[:, 0:cols]
                        mm(o, h_hi[:, k, ts], wh, k == 0, False)
                        mm(o, h_hi[:, k, ts], wl, False, False)
                        last = mm(o, h_lo[:, k, ts], wh, False, k == KD - 1)
                    if s == ns - 1:
                        fill((name, t), last)
                if s == ns - 1:
                    slot_free(i, name=(name, NT - 1))
                else:
                    slot_free(i, last)
            elif stage == "down":
                _, name, nk, o = step
                i0 = SLOTS[name][0]
                hh, hl = hid1 if name[0] == "down1" else hid2
                nm = (name[0], name[1], o)
                out = take(nm)
                for k in range(nk):
                    g = o * nk + k
                    i = i0 + g // 8
                    if g % 8 == 0:
                        slot_ready(i)
                    if o == 0:
                        pe.wait_ge(*after("hid", name[0], name[1], k))
                    wsl = slice(g % 8 * P, g % 8 * P + P)
                    last = mm3(out[:], w_hi[:, i % SPL, wsl], w_lo[:, i % SPL, wsl], hh[:, k], hl[:, k],
                               k == 0, k == nk - 1)
                    if k == nk - 1:
                        fill(nm, last)
                        if g % 8 == 7:
                            slot_free(i, name=nm)
                    elif g % 8 == 7:
                        slot_free(i, last)
            elif stage == "cmp_up":
                _, name, kv, s = step
                i = SLOTS[name][0]
                if s == 0:
                    for k in range(2):
                        pe.wait_ge(*after("cmpx", k))
                    take(("cmp_u", kv))
                slot_ready(i)
                for j in range(4 * s, 4 * s + 4):
                    c0 = 32 * j if kv == 0 else 512 + 32 * j - 96
                    xh, xl = cmp_x[0][:, c0:c0 + P], cmp_x[1][:, c0:c0 + P]
                    wsl = slice((j % 4) * 256, (j % 4) * 256 + 256)
                    out = ps(("cmp_u", kv))[:, 0:256]
                    mm(out, xh, w_hi[:, i % SPL, wsl], j == 0, False)
                    mm(out, xh, w_lo[:, i % SPL, wsl], False, False)
                    last = mm(out, xl, w_hi[:, i % SPL, wsl], False, j == 15)
                if s == 3:
                    fill(("cmp_u", kv), last)
                    slot_free(i, name=("cmp_u", kv))
                else:
                    slot_free(i, last)
            elif stage == "cmp_turn_h":
                for kv in range(2):
                    out = take(("cmp_h", kv))
                    pe.wait_ge(*evacuated(("cmp_u", kv)))
                    rows = slice(96 * kv, 96 * kv + 32)
                    for c in range(2):
                        last = pe.transpose(out[:, c * 32:(c + 1) * 32], cmp_t[rows, c * P:(c + 1) * P],
                                            ident[rows, rows])
                    fill(("cmp_h", kv), last)
            elif stage == "cmp_down":
                pe.wait_ge(C.sem["mixer_in"], 16 * N_MIXER)
                pe.wait_ge(*evacuated(("cmp_h", 0)))
                pe.wait_ge(*after("cmp_v", "hv"))
                out = take("cmp_k")
                for c in range(2):
                    last = mm(out[:, 0:N_CMP], w2k[:, c], cmp_h[:, c, 0:N_CMP], c == 0, c == 1)
                fill("cmp_k", last)
                out = take("cmp_vt")
                for c in range(2):
                    last = mm(out[:, 0:HD], cmp_hv[:, c].rearrange("p h n -> p (h n)"), w2v[:, c], c == 0, c == 1)
                fill("cmp_vt", last)
            elif stage == "cmp_bias":
                pe.wait_ge(C.sem["bias_in"], 16 * 2 * NH)
                pe.wait_ge(C.sem["mixer_in"], 16 * N_MIXER)
                out = take("cmp_bias")
                for qt in range(NT):
                    for h in range(NH):
                        last = pe.transpose(out[:, (qt * NH + h) * N_CMP:(qt * NH + h + 1) * N_CMP],
                                            cb_t[:, h, qt * P:(qt + 1) * P], ident[0:N_CMP, 0:N_CMP])
                fill("cmp_bias", last)
            elif stage == "cmp_scores":
                pe.wait_ge(*after("rstd_used", "kcmp"))
                pe.wait_ge(*after("rstd_used", "nq1"))
                for hf in range(2):
                    take(("cmp_sc", hf))
                for qt in range(NT):
                    for j in range(2):
                        for hf in range(2):
                            pb = HD * hf
                            last = mm(ps(("cmp_sc", hf))[:, (qt * 2 + j) * N_CMP:(qt * 2 + j + 1) * N_CMP],
                                      nq[pb:pb + HD, j, qt * P:(qt + 1) * P], cmp_k[pb:pb + HD, 1, 0:N_CMP],
                                      True, True, skip_group_check=True)
                            if (qt, j) == (NT - 1, 1):
                                fill(("cmp_sc", hf), last)
            elif stage == "cmp_turn":
                pe.wait_ge(*after("cmp_v", "p"))
                out = take("cmp_pt")
                for qt in range(NT):
                    last = pe.transpose(out[:, qt * P:(qt + 1) * P], cmp_p[:, qt].rearrange("p h n -> p (h n)"), ident[:])
                fill("cmp_pt", last)
            elif stage == "att_scores":
                for u in step[1]:
                    if u[0] in ("slc", "win"):
                        pe.wait_ge(*after("rstd_used", "nq1"))
                        pe.wait_ge(C.sem["ksw_in"], 16 * 2)
                    elif u[0] == "mla":
                        pe.wait_ge(*after("rstd_used", ("mq", u[1])))
                    else:
                        pe.wait_ge(*evacuated(("wk", 1)))
                        pe.wait_ge(*evacuated(("wq", u[1])))
                    take(("sc", u))
                for u in step[1]:
                    A = att(u)
                    fill(("sc", u), mm(ps(("sc", u))[:, 0:A["w"]], A["q"], A["k"], True, True))
            elif stage == "att_turn":
                for u in step[1]:
                    A = att(u)
                    pe.wait_ge(*after("att_p", u))
                    out = take(("pt", u))
                    for b in range(A["w"] // P):
                        last = pe.transpose(out[:, b * P:(b + 1) * P], att_l[:, att_at[u] % 4, b * P:(b + 1) * P],
                                            ident[:])
                    fill(("pt", u), last)
            elif stage == "att_pv":
                units = [(u, att(u)) for u in step[1]]
                for u, A in units:
                    if A["bank_first"]:
                        take(A["out"])
                outs = [ps(A["out"])[A["pb"]:A["pb"] + HD, A["qt"] * P:(A["qt"] + 1) * P] for _, A in units]
                kind = units[0][0][0]
                if kind == "slc":
                    pe.wait_ge(*evacuated("cmp_pt"))
                    pe.wait_ge(*evacuated("cmp_vt"))
                    for (u, A), out in zip(units, outs):
                        mm(out, cmp_vt[:, u[1]], cmp_pt[:, u[2]], True, False)
                pe.wait_ge(*evacuated({"slc": ("v1", NT - 1), "win": ("v1", NT - 1), "mla": ("mv", 1),
                                       "swa": ("wv", NT - 1)}[kind]))
                for u, A in units:
                    pe.wait_ge(*evacuated(("pt", u)))
                n = len(units[0][1]["v"])
                for b in range(n):
                    for (u, A), out in zip(units, outs):
                        last = mm(out, A["v"][b], att_pt[:, att_at[u] % 2, b * P:(b + 1) * P],
                                  A["first"] and b == 0, A["last"] and b == n - 1)
                        if b == n - 1:
                            if A["bank_last"]:
                                fill(A["out"], last)
                            else:
                                last.then_inc(*did("att_done", u))
            elif stage == "mla_v":
                pe.wait_ge(*after("rstd_used", "ckv"))
                for n in range(2):
                    out = take(("mv", n))
                    for t in range(2):
                        tt = 2 * n + t
                        last = mm(out[:, t * 256:(t + 1) * 256], ckv[:, tt * P:(tt + 1) * P], wvb[:], True, True,
                                  skip_group_check=True)
                    fill(("mv", n), last)
            elif stage == "mla_qk":
                h = step[1]
                out = take(("mk", h))
                fill(("mk", h), mm(out[0:QKD, :], wkb[:, h], ckv[:], True, True))
                pe.wait_ge(*after("rstd_used", "cq"))
                out = take(("mq", h))
                mm(out[0:QKD, :], wqb[:, 0, h], cq[:, 0], True, False)
                fill(("mq", h), mm(out[0:QKD, :], wqb[0:HD, 1, h], cq[0:HD, 1], False, True))
            elif stage == "sb_scores":
                _, pair, kt = step
                pe.wait_ge(*evacuated("sk1"))
                for h in (2 * pair, 2 * pair + 1):
                    pb = HD * (h % 2)
                    out = take(("z", h, kt))
                    mm(out[:, 0:T - kt * P], s_qk[pb:pb + HD, 2 + pair, kt * P:(kt + 1) * P],
                       s_qk[pb:pb + HD, pair, kt * P:T], True, False, skip_group_check=True)
                for h in (2 * pair, 2 * pair + 1):
                    fill(("z", h, kt), mm(ps(("z", h, kt))[:, 0:P], ident[:], sbm[:, 2], False, False,
                                          skip_group_check=True), keep=True)
            elif stage == "sb_exp":
                _, pair, kt = step
                w = T - kt * P
                for h in (2 * pair, 2 * pair + 1):
                    out = take_over(("r", h, kt), ("z", h, kt))
                    for j in range(NT - 1, kt, -1):
                        mm(out[:, (j - kt) * P:w], sbm[:, 1], sb_sp[:, h % 2, SB_OFF[j]:SB_OFF[j] + T - j * P],
                           False, False, skip_group_check=True)
                    last = mm(out[:, 0:w], sbm[:, 0], sb_sp[:, h % 2, SB_OFF[kt]:SB_OFF[kt] + w], False, True,
                              skip_group_check=True)
                    fill(("r", h, kt), last)
            elif stage == "sb_pv":
                pair = step[1]
                out = take(("sb_o", pair))
                for h in (2 * pair, 2 * pair + 1):
                    pe.wait_ge(*evacuated(("r", h, 0)))
                for kt in range(NT):
                    w = T - kt * P
                    for h in (2 * pair, 2 * pair + 1):
                        pb = HD * (h % 2)
                        last = mm(out[pb:pb + HD, kt * P:T], v1[:, kt, 2 * HD + h * HD:2 * HD + (h + 1) * HD],
                                  sb_a[:, h % 2, SB_OFF[kt]:SB_OFF[kt] + w], kt == 0, kt == NT - 1)
                fill(("sb_o", pair), last)
            elif stage == "ret_scores":
                _, h, jt = step
                pe.wait_ge(*evacuated(("rk", h)))
                out = take(("rs", h, jt))
                fill(("rs", h, jt), mm(out[:, 0:T - jt * P], kf[:, h % 2, jt * P:(jt + 1) * P], qf[:, h % 2, jt * P:T],
                                       True, True))
            elif stage == "ret_pv":
                h = step[1]
                pe.wait_ge(*evacuated((("rv", h // 2), NT - 1)))
                pe.wait_ge(*evacuated(("rs", h, NT - 1)))
                for e in range(2):
                    out = take(("ret_o", h, e))
                    for jt in range(NT):
                        w = T - jt * P
                        last = mm(out[:, jt * P:T], vt[:, jt, h % 2 * 256 + e * P:h % 2 * 256 + (e + 1) * P],
                                  ret_a[:, SB_OFF[jt]:SB_OFF[jt] + w], jt == 0, jt == NT - 1)
                    fill(("ret_o", h, e), last)
            elif stage == "ret_mean":
                h = step[1]
                pe.wait_ge(*after("ret_s", h))
                fill(("mean", h), mm(take(("mean", h))[:], ones[:], tmp[:, 1], True, True))
            elif stage == "gla_decay":
                h = step[1]
                pe.wait_ge(*evacuated("ga"))
                pe.wait_ge(C.sem["late_in"], 16 * 4)
                out = take(("gz", h))
                fill(("gz", h), mm(out[:], wa2[:, h * P:(h + 1) * P], ga_t[:], True, True))
            elif stage == "gla_turn":
                h = step[1]
                pe.wait_ge(*after("gla_v", "kd", h))
                out = take(("kdt", h))
                for m in range(NT):
                    last = pe.transpose(out[:, m * P:(m + 1) * P], kf[:, h % 2, m * P:(m + 1) * P], ident[:])
                fill(("kdt", h), last)
                out = take(("ga_s", h))
                for m in range(NT):
                    ms_ = slice(m * P, (m + 1) * P)
                    last = mm(out[:, ms_], gk_i[:, ms_], qf[:, h % 2, ms_], True, True, skip_group_check=True)
                fill(("ga_s", h), last)
            elif stage == "gla_chunks":
                h = step[1]
                pe.wait_ge(*evacuated(("kdt", h)))
                pe.wait_ge(*evacuated((("gv", h // 2), NT - 1)))
                for n in range(NGC - 1):
                    out = take(("kv", h, n))
                    r = slice(GC * (n % 2), GC * (n % 2) + GC)
                    fill(("kv", h, n), mm(out[:, 0:256], gk_t[r, n // 2], vt[r, n // 2, h % 2 * 256:(h % 2 + 1) * 256],
                                          True, True))
                pe.wait_ge(*evacuated(("ga_s", h)))
                for e in range(2):
                    out = take(("gla_o", h, e))
                    for m in range(NT):
                        mm(out[:, m * P:(m + 1) * P], vt[:, m, h % 2 * 256 + e * P:h % 2 * 256 + (e + 1) * P], ga_m[:, m],
                           True, False, skip_group_check=True)
                        for n in (2 * m, 2 * m + 1):
                            if n == 0:
                                continue
                            pe.wait_ge(*evacuated(("kv", h, n - 1)))
                            last = mm(out[:, n * GC:(n + 1) * GC], g_st[:, n - 1, e * P:(e + 1) * P],
                                      qf[:, h % 2, n * GC:(n + 1) * GC], False, n % 2 == 1, skip_group_check=True)
                    fill(("gla_o", h, e), last)

    @block.scalar
    def _(act):
        loaded = []

        def functions(which):
            if loaded[-1:] != [which]:
                loaded.append(which)
                if which == "exp_ln":
                    act.preload_act_table_set("natural_log_exp_and_others")

        functions("exp_ln")
        act.dma_start(par[:], a["par"]).then_inc(C.sem["const_in"], 16)
        for t, src in ((ones, "ones"), (ones64, "ones64")):
            act.dma_start(t[:], a[src]).then_inc(C.sem["const_in"], 16)
        act.dma_start(onehot[:], a["onehot"]).then_inc(C.sem["misc_in"], 16)
        act.dma_start(rb[0:N_BUCKETS, :], a["rel_bias"]).then_inc(C.sem["misc_in"], 16)

        def chain(ins):
            ins.then_inc(C.sem["s_chain"], 1)
            C.n["s_chain"] = C.n.get("s_chain", 0) + 1
            act.wait_ge(C.sem["s_chain"], C.n["s_chain"])

        def copy_out(name, dst, src_ap, scale=1.0):
            act.wait_ge(*full(name))
            act.activation(dst, src_ap, ACT.Copy, scale=scale).then_inc(*release(name))

        def sq_free(key, c):
            u = sq_use[(key, c)]
            if u >= 2:
                k2, c2 = sq_uses[u - 2]
                if len(norms[k2][0]) == 1 or c2 == (POOLED_ORDER[-1] if k2 in PE_SUM else KD - 1):
                    act.wait_ge(*full(("ms", k2)))
                elif k2 in PE_SUM:
                    act.wait_ge(*after("sq_pe", k2, c2))
                else:
                    act.wait_ge(*after("sq_v", k2, max(c2, 1)))

        def square(key, c):
            srcs, parts, cols, one, scale, eps, waits = norms[key]
            wait_src(act, waits[c])
            sq_free(key, c)
            act.activation(sq[0:parts, sq_use[(key, c)] % 2, 0:cols], srcs[c], ACT.Square)\
               .then_inc(*did("sq_s", key, c))

        def norm(key):
            srcs, parts, cols, one, scale, eps, waits = norms[key]
            functions("exp_ln")
            act.wait_ge(*full(("ms", key)))
            r = norm_at[key]
            if r >= 3:
                act.wait_ge(*after("rstd_used", norm_order[r - 3]))
            if r == 0:
                act.wait_ge(*after("table", "eps"))
            e = EPS_COL[eps]
            act.activation(rstd(key), ps(("ms", key))[0:parts, 0:cols], ACT.Ln, scale=scale,
                           bias=epst[0:parts, e:e + 1]).then_inc(*release(("ms", key)))
            act.wait_ge(*evacuated(("ms", key)))
            act.activation(rstd(key), rstd(key), ACT.Exp, scale=-0.5).then_inc(*did("rstd", key))

        for step in ORDER:
            stage = step[0]
            if stage == "norm":
                norm(step[1])
                if step[1] == "n1":
                    act.wait_ge(C.sem["const_in"], 16 * N_CONST)
                    for t, src in ((w2k, "w2k"), (w2v, "w2v"), (ident, "ident"), (rope_c, "rope_c"), (rope_s, "rope_s"),
                                   (wqb, "wqb"), (wkb, "wkb"), (wvb, "wvb"), (causal, "causal"), (sbm, "sbm")):
                        act.dma_start(t[:], a[src]).then_inc(C.sem["mixer_in"], 16)
            elif stage == "sq":
                square(*step[1:])
            elif stage == "fm":
                name = step[1]
                key = name[0] if isinstance(name, tuple) else name
                if name == "ksw":
                    copy_out(name, ks_d, ps(name)[:])
                elif name == "nq0" or name == "nq1":
                    copy_out(name, nq[:, int(name[2])], ps(name)[:])
                elif name == "cq0":
                    copy_out(name, cq[:, 0], ps(name)[:])
                elif name == "cqr":
                    act.wait_ge(*full(name))
                    act.wait_ge(*after("zeros"))
                    chain(act.activation(cq[0:HD, 1], ps(name)[0:HD, :], ACT.Copy))
                    act.activation(kr[HD:QKD, 0], ps(name)[HD:QKD, :], ACT.Copy).then_inc(*release(name))
                    act.wait_ge(*evacuated(name))
                    for dst, src in ((HD, HD + 16), (HD + 16, HD)):
                        act.dma_start(kr[dst:dst + 16, 1], kr[src:src + 16, 0]).then_inc(C.sem["kr_in"], 16)
                elif name == "ckv":
                    copy_out(name, ckv[:], ps(name)[:])
                elif name in ("sq0", "sq1", "sk0", "sk1"):
                    c = int(name[2]) + (2 if name[1] == "k" else 0)
                    copy_out(name, s_qk[:, c], ps(name)[:], scale=HD ** -0.5 if name[1] == "q" else 1.0)
                elif key == "up1":
                    _, half, c = name
                    n = half * HALF1 + c
                    act.wait_ge(*full(name))
                    if n == 0:
                        act.wait_ge(*after("h_ready", "n2", KD - 1))
                    if n >= 2:
                        act.wait_ge(*after("hid", "down1", (n - 2) // HALF1, (n - 2) % HALF1))
                    act.activation(r1[:, n % 2], ps(name)[:], ACT.Relu).then_inc(*release(name))
                    act.wait_ge(*evacuated(name))
                    act.activation(r1[:, n % 2], r1[:, n % 2], ACT.Square).then_inc(*did("hid_s", name))
                elif key in ("rq", "gq"):
                    h = name[1]
                    if key == "rq" and h >= 2:
                        act.wait_ge(*full(("rs", h - 2, NT - 1)))
                    if key == "gq" and h >= 2:
                        act.wait_ge(*full(("gla_o", h - 2, 1)))
                    copy_out(name, qf[:, h % 2], ps(name)[:], scale=P ** -0.5 if key == "gq" else 1.0)
                elif key in ("rk", "gk"):
                    copy_out(name, kf[:, name[1] % 2], ps(name)[:])
                elif key in ("rg", "gg"):
                    _, h, e = name
                    n = sig_at[name]
                    act.wait_ge(*full(name))
                    if n >= 2:
                        act.wait_ge(*evacuated(sig_user(n - 2)))
                    functions("sigmoid")
                    act.activation(sig[:, n % 2], ps(name)[:], ACT.Sigmoid).then_inc(*did("gate_s", name))
                elif key == "ga":
                    act.wait_ge(*after("o_ready", 0, KD - 1))
                    copy_out(name, ga_t[:], ps(name)[0:16, :])
                elif key == "gate":
                    _, b, m = name
                    n = sig_at[name]
                    act.wait_ge(*full(name))
                    act.wait_ge(*evacuated(sig_user(n - 2)))
                    functions("sigmoid")
                    act.activation(sig[:, n % 2], ps(name)[:], ACT.Sigmoid).then_inc(*release(name))
                elif key == "wq":
                    if name[1] == 0:
                        act.wait_ge(*full(("gla_o", 3, 1)))
                    copy_out(name, wq[:, name[1]], ps(name)[:], scale=HD ** -0.5)
                elif name == "kvc":
                    act.wait_ge(*evacuated(name))
                    act.dma_start(kv_raw[HD:P, 0, 0:T - 1], kv_raw[0:HD, 0, 1:T]).then_inc(C.sem["kv_in"], 16)
                    act.dma_start(kv_raw[0:HD, 1], att_l[HD:P, 0]).then_inc(C.sem["kv_in"], 16)
                elif key == "wk":
                    if name[1] == 0:
                        act.wait_ge(*after("o_ready", 1, KD - 1))
                    copy_out(name, wk[:, name[1]], ps(name)[:])
                elif key == "fg":
                    _, half, c = name
                    n = half * HALF2 + c
                    act.wait_ge(*full(name))
                    if n == 0:
                        act.wait_ge(*full(("swa_o", 7)))
                        act.wait_ge(*after("h_ready", "fpre", KD - 1))
                    if n >= 2:
                        act.wait_ge(*evacuated(("fu", (n - 2) // HALF2, (n - 2) % HALF2)))
                    functions("sigmoid")
                    act.activation(sig2[:, n % 2], ps(name)[:], ACT.Sigmoid).then_inc(*did("gate_s", name))
            elif stage == "tm":
                _, _, name, _, s, ns = step
                if s < ns - 1:
                    continue
                if name == ("rv", 0):
                    act.wait_ge(*full(("down1", 1, KD - 1)))
                elif name in (("rv", 1), ("gv", 0), ("gv", 1)):
                    act.wait_ge(*full({"rv1": ("ret_o", 1, 1), "gv0": ("ret_o", 3, 1),
                                       "gv1": ("gla_o", 1, 1)}[name[0] + str(name[1])]))
                for t in range(NT):
                    if name == "v1":
                        copy_out((name, t), v1[:, t], ps((name, t))[:, 0:396])
                    elif name == "wv":
                        copy_out((name, t), wv[:, t], ps((name, t))[:, 0:256])
                    else:
                        copy_out((name, t), vt[:, t], ps((name, t))[:])
                if name == "v1":
                    act.wait_ge(*evacuated(("v1", NT - 1)))
                    act.activation(gates[:], v1[:, :, 384:396], ACT.Exp, scale=-1.0).then_inc(*did("cmp_s", "g"))
            elif stage == "cmp_down":
                copy_out("cmp_k", cmp_k[:, 0, 0:N_CMP], ps("cmp_k")[:, 0:N_CMP])
            elif stage == "cmp_up":
                kv = step[2]
                if step[3] < 3:
                    continue
                rows = slice(96 * kv, 96 * kv + 32)
                act.wait_ge(*full(("cmp_u", kv)))
                act.activation(cmp_t[rows], ps(("cmp_u", kv))[rows, 0:256], ACT.Exp,
                               scale=-1.0).then_inc(*did("cmp_s", kv))
            elif stage == "mla_qk":
                h = step[1]
                copy_out(("mq", h), mq[0:QKD, h], ps(("mq", h))[0:QKD, :])
                act.wait_ge(*evacuated(("mq", h)))
                act.wait_ge(*after("mla_q", h - 1) if h else after("mla_k"))
                for dst, src in ((HD, HD + 16), (HD + 16, HD)):
                    act.dma_start(kr[dst:dst + 16, 1], mq[src:src + 16, h]).then_inc(C.sem["kr_in"], 16)
            elif stage == "nsa_apply" and step[1] == "ksw":
                act.wait_ge(*after("rstd_used", "ksw"))
                act.dma_start(ks_d[HD:P], ks_d[0:HD]).then_inc(C.sem["ksw_in"], 16)
                act.dma_start(kw_d[0:HD], kw_d[HD:P]).then_inc(C.sem["ksw_in"], 16)
            elif stage == "cmp_scores":
                act.wait_ge(*after("cmp_v", "l"))
                act.activation(cmp_p[:, :, :, 0:N_CMP], cmp_p[:, :, :, 0:N_CMP], ACT.Exp).then_inc(*did("cmp_s", "exp"))
            elif stage == "cmp_turn":
                copy_out("cmp_pt", cmp_pt[:].rearrange("p t q -> p (t q)"), ps("cmp_pt")[:])
            elif stage == "att_scores":
                functions("exp_ln")
                for u in step[1]:
                    A = att(u)
                    n = att_at[u]
                    act.wait_ge(*after("att_n", u))
                    L, sm = att_l[:, n % 4, 0:A["w"]], small[:, n % 4]
                    act.activation(L, L, ACT.Exp, bias=sm[:, 1:2], accum_out=sm[:, 2:3]).then_inc(*did("att_exp", u))
                    if "sink" in A:
                        act.activation(sm[:, 5:6], A["sink"], ACT.Exp, bias=sm[:, 1:2]).then_inc(*did("swa_s", u))
            elif stage == "att_turn":
                for u in step[1]:
                    A = att(u)
                    n = att_at[u]
                    act.wait_ge(*full(("pt", u)))
                    if n >= 2:
                        v = att_order[n - 2]
                        act.wait_ge(*(full(att(v)["out"]) if att(v)["bank_last"] else after("att_done", v)))
                    act.activation(att_pt[:, n % 2, 0:A["w"]], ps(("pt", u))[:, 0:A["w"]], ACT.Copy)\
                       .then_inc(*release(("pt", u)))
            elif stage == "att_pv":
                for u in step[1]:
                    A = att(u)
                    if A["bank_last"]:
                        if u[0] == "swa":
                            copy_out(A["out"], swa_o[:, u[1]], ps(A["out"])[:])
                        else:
                            g = 1 if u[0] == "win" else 2
                            copy_out(A["out"], y[:, 2 * g + A["out"][1]], ps(A["out"])[:])
            elif stage == "mla_v":
                for n in range(2):
                    copy_out(("mv", n), mv[:, 2 * n:2 * n + 2], ps(("mv", n))[:].rearrange("p (t c) -> p t c", t=2))
            elif stage == "sb_scores":
                _, pair, kt = step
                w = T - kt * P
                for h in (2 * pair, 2 * pair + 1):
                    n = sb_order.index((h, kt))
                    act.wait_ge(*full(("z", h, kt)))
                    if n == 0:
                        act.wait_ge(*full(("nsa_o", 1)))
                    if n >= 2:
                        act.wait_ge(*evacuated(("z",) + sb_order[n - 2]))
                    e = sb_e[:, n % 2, 0:w]
                    chain(act.activation(e, ps(("z", h, kt))[:, 0:w], ACT.Abs))
                    chain(act.activation(e, e, ACT.Exp, scale=-1.0))
                    act.activation(e, e, ACT.Ln, bias=1.0).then_inc(*did("sb_exp", h, kt))
            elif stage == "sb_exp":
                _, pair, kt = step
                w = T - kt * P
                for h in (2 * pair, 2 * pair + 1):
                    act.wait_ge(*full(("r", h, kt)))
                    if h >= 2:
                        act.wait_ge(*full(("sb_o", 0)))
                    act.activation(sb_a[:, h % 2, SB_OFF[kt]:SB_OFF[kt] + w], ps(("r", h, kt))[:, 0:w], ACT.Exp)\
                       .then_inc(*release(("r", h, kt)))
            elif stage == "sb_pv":
                copy_out(("sb_o", step[1]), y[:, 6 + step[1]], ps(("sb_o", step[1]))[:])
            elif stage == "x_again":
                act.wait_ge(*full(("nsa_o", 1) if step[1] == 0 else ("r", NH - 1, 0)))
                cc = slice(4 * step[1], 4 * step[1] + 4)
                act.dma_start(x_sb[:, cc], a["x"][:, cc]).then_inc(C.sem["x_back"], 16)
            elif stage == "ret_pv":
                h = step[1]
                for e in range(2):
                    if h >= 1:
                        act.wait_ge(*after("ret_d", h - 1, e))
                    copy_out(("ret_o", h, e), mix_o[:, e], ps(("ret_o", h, e))[:])
            elif stage == "gla_decay":
                functions("exp_ln")
                h = step[1]
                if h >= 1:
                    act.wait_ge(*evacuated(("kv", h - 1, NGC - 2)))
                g0 = g_ln
                act.wait_ge(*full(("gz", h)))
                chain(act.activation(g0, ps(("gz", h))[:], ACT.Abs, bias=col("b_alpha", h)))
                chain(act.activation(g0, g0, ACT.Exp, scale=-1.0))
                act.activation(g0, g0, ACT.Ln, bias=1.0).then_inc(*did("gla_s", "ln", h))
                act.wait_ge(*after("gla_v", "d", h))
                act.activation(g_eb, g_b, ACT.Exp).then_inc(*did("gla_s", "eb", h))
                act.activation(gk_i[:], g_b, ACT.Exp, scale=-1.0).then_inc(*did("gla_s", "enb", h))
                act.activation(g_ed[:], g_ed[:], ACT.Exp).then_inc(*did("gla_s", "ed", h))
            elif stage == "gla_turn":
                h = step[1]
                if h >= 1:
                    act.wait_ge(*full(("kv", h - 1, NGC - 2)))
                copy_out(("kdt", h), gk_t, ps(("kdt", h))[:].rearrange("p (m k) -> p m k", m=NT))
            elif stage == "gla_chunks":
                h = step[1]
                for e in range(2):
                    if h >= 1:
                        act.wait_ge(*after("gla_done", h - 1, e))
                    copy_out(("gla_o", h, e), mix_o[:, e], ps(("gla_o", h, e))[:])

    @block.vector
    def _(dve):
        def chain(ins):
            ins.then_inc(C.sem["v_chain"], 1)
            C.n["v_chain"] = C.n.get("v_chain", 0) + 1
            dve.wait_ge(C.sem["v_chain"], C.n["v_chain"])

        def own(name, *key):
            dve.wait_ge(*after(name, *key))

        def split(t, hi, lo, *event):
            chain(dve.tensor_copy(hi, t))
            dve.tensor_tensor(lo, t, hi.bitcast(F32), ALU.subtract).then_inc(*did(*event))
            own(*event)

        def squares(key, c):
            srcs, parts, cols, *_ = norms[key]
            if 0 < c < KD - 1 and key not in PE_SUM:
                own("sq_s", key, c)
                b = [sq[0:parts, sq_use[(key, x)] % 2, 0:cols] for x in (c - 1, c)]
                if c == 1:
                    for k2 in reversed(norm_order[:norm_at[key]]):
                        if len(norms[k2][0]) > 1 and k2 not in PE_SUM:
                            dve.wait_ge(*full(("ms", k2)))
                            break
                else:
                    own("sq_v", key, c - 1)
                dve.tensor_tensor(sq_sum[0:parts, 0:cols], b[0] if c == 1 else sq_sum[0:parts, 0:cols], b[1],
                                  ALU.add).then_inc(*did("sq_v", key, c))

        def scaled(key, dst, src, w, parts=P):
            return dve.scalar_tensor_tensor(out=dst, in0=src, scalar=w, in1=rstd(key), op0=ALU.mult, op1=ALU.mult)

        for i, v in enumerate(EPS_VAL):
            ins = dve.memset(epst[:, i:i + 1], v)
        ins.then_inc(*did("table", "eps"))
        dve.memset(rb[N_BUCKETS:N_BUCKETS + 1, :], NEG).then_inc(*did("far_row"))
        last_h = None
        for step in ORDER:
            stage = step[0]
            if stage == "bias_tables":
                dve.memset(y[:, 5:8], 0.0).then_inc(*did("zeros"))
                for n, (c0, w) in enumerate(TAB):
                    dve.wait_ge(*full(("tab", n)))
                    dve.tensor_copy(tab[:, c0:c0 + w], ps(("tab", n))[0:NH, 0:w]).then_inc(*release(("tab", n)))
            elif stage == "sq":
                squares(*step[1:])
            elif stage in ("apply_h", "y_out"):
                key = step[1] if stage == "apply_h" else "y"
                if key == "n1":
                    dve.wait_ge(C.sem["const_in"], 16 * N_CONST)
                if last_h is not None:
                    dve.wait_ge(*full(last_h))
                chunks = range(KD) if stage == "apply_h" else (2 * step[1], 2 * step[1] + 1)
                nk = step[1] if stage == "apply_h" else ("y", step[1])

                def normed(c):
                    src, w = (y[:, c], col("out_norm", c)) if key == "y" else (x_sb[:, c], col(step[2], c))
                    if key == "fpre" and c in POOLED:
                        dve.wait_ge(*after("x_pool", "post", c))
                    if c - 2 >= chunks[0]:
                        own("h_ready", key, c - 2)
                    event = ("rstd_used", nk) if c == chunks[-1] else ("h_t", key, c)
                    scaled(nk, tmp[:, c % 2], src, w).then_inc(*did(*event))
                    return event

                own("rstd", nk)
                event = normed(chunks[0])
                for c in chunks:
                    t = tmp[:, c % 2]
                    own(*event)
                    dve.tensor_copy(h_hi[:, c], t).then_inc(*did("h_hi", key, c))
                    if c != chunks[-1]:
                        event = normed(c + 1)
                    own("h_hi", key, c)
                    dve.tensor_tensor(h_lo[:, c], t, h_hi[:, c].bitcast(F32), ALU.subtract)\
                       .then_inc(*did("h_ready", key, c))
                own("h_ready", key, chunks[-1])
            elif stage == "fm":
                name, src = step[1], step[2]
                if src == "h":
                    last_h = name
                key = name[0] if isinstance(name, tuple) else name
                if name == "kvc":
                    dve.wait_ge(*full(name))
                    dve.wait_ge(*evacuated(("tab", 3)))
                    chain(dve.tensor_copy(kv_raw[0:HD, 0], ps(name)[0:HD, :]))
                    chain(dve.tensor_copy(kv_raw[HD:P, 1, 0:T - 1], ps(name)[HD:P, 1:T]))
                    dve.tensor_copy(att_l[HD:P, 0], ps(name)[HD:P, :]).then_inc(*release(name))
                    dve.wait_ge(*evacuated(name))
                elif key in ("ac", "au", "ab"):
                    c = name[1]
                    dve.wait_ge(*full(name))
                    v = conv_t[:, 0, 2:2 + T]
                    if key == "ac":
                        if c == 0:
                            chain(dve.memset(conv_t[:], 0.0))
                        ins = dve.tensor_copy(conv_t[:, 1, 2:2 + T], ps(name)[:])
                    elif key == "au":
                        ins = dve.tensor_tensor(v, ps(name)[:], conv_t[:, 1, 2:2 + T], ALU.mult)
                    else:
                        yc = y[:, c]
                        w = [col("conv_w", 2 * k + c) for k in range(3)]
                        chain(dve.tensor_scalar(yc, conv_t[:, 0, 2:2 + T], w[2], col("conv_b", c), ALU.mult, ALU.add))
                        for k in (1, 0):
                            chain(dve.scalar_tensor_tensor(out=yc, in0=conv_t[:, 0, k:k + T], scalar=w[k], in1=yc,
                                                           op0=ALU.mult, op1=ALU.add))
                        ins = dve.tensor_tensor(conv_t[:, 1, 2:2 + T], ps(name)[:], yc, ALU.mult)
                    ins.then_inc(*release(name))
                    dve.wait_ge(*evacuated(name))
                    if key == "ab":
                        dve.tensor_copy(y[:, c], conv_t[:, 1, 2:2 + T]).then_inc(*did("conv_v", c))
                        own("conv_v", c)
                elif key == "wout":
                    c = name[1]
                    if c == 0:
                        dve.wait_ge(C.sem["x_back"], 16 * 2)
                    dve.wait_ge(*full(name))
                    dve.tensor_tensor(x_sb[:, c], ps(name)[:], x_sb[:, c], ALU.add).then_inc(*release(name))
                elif key == "wout2":
                    c = name[1]
                    dve.wait_ge(*full(name))
                    dve.tensor_copy(merged[:, c], ps(name)[:]).then_inc(*release(name))
                elif key == "up1":
                    _, half, c = name
                    own("hid_s", name)
                    if half == 1 and c == 0:
                        dve.wait_ge(*full(("down1", 0, KD - 1)))
                    if half == 0 and c == 0:
                        dve.wait_ge(*full(("wout", KD - 1)))
                    split(r1[:, (half * HALF1 + c) % 2], hid1[0][:, c], hid1[1][:, c], "hid", "down1", half, c)
                elif key in ("rg", "gg"):
                    _, h, e = name
                    n = sig_at[name]
                    own("gate_s", name)
                    dve.tensor_tensor(silu[:, e], ps(name)[:], sig[:, n % 2], ALU.mult).then_inc(*release(name))
                    dve.wait_ge(*evacuated(name))
                elif key == "br":
                    _, b, m = name
                    n = sig_at[("gate", b, m)]
                    dve.wait_ge(*full(name))
                    dve.wait_ge(*evacuated(("gate", b, m)))
                    t = merged[:, m] if b == 0 else tmp[:, n % 2]
                    ins = dve.tensor_tensor(t, ps(name)[:], sig[:, n % 2], ALU.mult)
                    ins.then_inc(*release(name))
                    dve.wait_ge(*evacuated(name))
                    if b:
                        chain(dve.tensor_tensor(merged[:, m], merged[:, m], t, ALU.add))
                    if b == 2:
                        split(merged[:, m], m_hl[0][:, m], m_hl[1][:, m], "m_ready", m)
                elif key == "fu":
                    _, half, c = name
                    n = half * HALF2 + c
                    own("gate_s", ("fg", half, c))
                    if half == 1 and c == 0:
                        dve.wait_ge(*full(("down2", 0, KD - 1)))
                    s = sig2[:, n % 2]
                    dve.tensor_tensor(s, ps(("fg", half, c))[:], s, ALU.mult).then_inc(*release(("fg", half, c)))
                    dve.wait_ge(*evacuated(("fg", half, c)))
                    dve.wait_ge(*full(name))
                    t = tmp[:, n % 2]
                    dve.tensor_tensor(t, ps(name)[:], s, ALU.mult).then_inc(*release(name))
                    dve.wait_ge(*evacuated(name))
                    split(t, hid2[0][:, c], hid2[1][:, c], "hid", "down2", half, c)
            elif stage == "tm" and step[4] < step[5] - 1:
                continue
            elif stage == "tm" and step[2] == "v1":
                last_h = ("v1", NT - 1)
                own("cmp_s", "g")
                chain(dve.tensor_scalar(gates[:], gates[:], 1.0, None, ALU.add))
                dve.reciprocal(gates[:], gates[:]).then_inc(*did("gate_v"))
                own("gate_v")
            elif stage == "tm":
                last_h = (step[2], NT - 1)
            elif stage == "down":
                _, name, nk, o = step
                nm = (name[0], name[1], o)
                dve.wait_ge(*full(nm))
                if name[0] == "down1" or name[1] == 1:
                    dst = x_sb[:, o] if name[0] == "down1" else f_acc[:, o]
                    if nm[0] == "down2":
                        dve.wait_ge(*evacuated(("down2", 0, o)))
                    dve.tensor_tensor(dst, ps(nm)[:], dst, ALU.add).then_inc(*release(nm))
                else:
                    dve.tensor_copy(f_acc[:, o], ps(nm)[:]).then_inc(*release(nm))
            elif stage == "cmp_x":
                kv = step[1]
                if kv == 0:
                    dve.wait_ge(C.sem["kv_in"], 16 * 2)
                    dve.wait_ge(C.sem["table_out"], 16)
                v4 = kv_raw[:, kv].rearrange("p (n j two) -> p j two n", j=8, two=2)
                pos = par[:, PCOL["pos"] + 16 * kv:PCOL["pos"] + 16 * (kv + 1)]
                t = tmp[:, 0].rearrange("p (j n) -> p j n", n=32)
                chain(dve.memset(tmp[:, 0], 0.0))
                for half in range(2):
                    ins = dve.tensor_tensor(t[:, 8 * half:8 * half + 8, 0:N_CMP],
                                            v4[:, :, 0, half:half + N_CMP],
                                            pos[:, 8 * half:8 * half + 8, None].to_broadcast([P, 8, N_CMP]), ALU.add)
                chain(ins)
                cols = slice(512 * kv, 512 * kv + 512)
                split(tmp[:, 0], cmp_x[0][:, cols], cmp_x[1][:, cols], "cmpx", kv)
            elif stage == "nsa_apply" and step[1] == "ksw":
                own("rstd", "ksw")
                rs = rstd("ksw")
                for dst, p0 in ((kw_d, HD), (ks_d, 0)):
                    ins = dve.scalar_tensor_tensor(out=dst[p0:p0 + HD], in0=ks_d[p0:p0 + HD], scalar=col("nsa_k", 1)[p0:p0 + HD],
                                                   in1=rs[p0:p0 + HD], op0=ALU.mult, op1=ALU.mult)
                    if p0:
                        chain(ins)
                ins.then_inc(*did("rstd_used", "ksw"))
                own("rstd_used", "ksw")
            elif stage == "nsa_apply":
                name = step[1]
                own("rstd", name)
                dst = nq[:, int(name[2])]
                scaled(name, dst, dst, col("nsa_q")).then_inc(*did("rstd_used", name))
                own("rstd_used", name)
            elif stage == "cmp_down":
                dve.wait_ge(*full("cmp_vt"))
                dve.tensor_tensor(cmp_vt[:], ps("cmp_vt")[:, None, 0:HD].to_broadcast([P, NH, HD]),
                                  col("head_of", 0, NH)[:, :, None].to_broadcast([P, NH, HD]), ALU.mult)\
                    .then_inc(*release("cmp_vt"))
            elif stage == "cmp_up":
                kv = step[2]
                if step[3] < 3:
                    continue
                own("cmp_s", kv)
                rows = slice(96 * kv, 96 * kv + 32)
                chain(dve.tensor_scalar(cmp_t[rows], cmp_t[rows], 1.0, None, ALU.add))
                chain(dve.reciprocal(cmp_t[rows], cmp_t[rows]))
                dve.tensor_tensor(cmp_t[rows], ps(("cmp_u", kv))[rows, 0:256], cmp_t[rows], ALU.mult)\
                   .then_inc(*release(("cmp_u", kv)))
                dve.wait_ge(*evacuated(("cmp_u", kv)))
            elif stage == "cmp_turn_h":
                for kv in range(2):
                    dve.wait_ge(*full(("cmp_h", kv)))
                    dve.tensor_copy(cmp_h[:, 2 * kv:2 * kv + 2].rearrange("p c n -> p (c n)"),
                                    ps(("cmp_h", kv))[:, 0:2 * 32]).then_inc(*release(("cmp_h", kv)))
                dve.wait_ge(*evacuated(("cmp_h", 1)))
                dve.tensor_copy(cmp_hv[:], cmp_h[:, 2:4, None, :].to_broadcast([P, 2, NH, 32]))\
                   .then_inc(*did("cmp_v", "hv"))
                own("cmp_v", "hv")
            elif stage == "cmp_apply":
                own("rstd", "kcmp")
                scaled("kcmp", cmp_k[:, 1, 0:N_CMP], cmp_k[:, 0, 0:N_CMP], col("nsa_k", 0))\
                    .then_inc(*did("rstd_used", "kcmp"))
                own("rstd_used", "kcmp")
            elif stage == "cmp_bias":
                dve.wait_ge(*full("cmp_bias"))
                dve.tensor_copy(cmp_bias[:].rearrange("p a b c -> p (a b c)"),
                                ps("cmp_bias")[:, 0:NT * NH * N_CMP]).then_inc(*release("cmp_bias"))
                dve.wait_ge(*evacuated("cmp_bias"))
            elif stage == "cmp_scores":
                chain(dve.memset(cmp_p[:], 0.0))
                p3 = cmp_p[:].rearrange("p a b c -> p (a b) c")[:, :, 0:N_CMP]
                bc = lambda i: cmp_s[:, i].rearrange("p a b -> p (a b)")[:, :, None].to_broadcast([P, NT * NH, N_CMP])
                dve.wait_ge(*evacuated("cmp_bias"))
                for hf in range(2):
                    n = ("cmp_sc", hf)
                    dve.wait_ge(*full(n))
                    dve.tensor_tensor(cmp_p[:, :, hf:NH:2, 0:N_CMP], ps(n)[:, 0:NT * 2 * N_CMP]
                                      .rearrange("p (a b c) -> p a b c", a=NT, b=2), cmp_bias[:, :, hf:NH:2],
                                      ALU.add).then_inc(*release(n))
                dve.wait_ge(*evacuated(n))
                chain(dve.tensor_reduce(cmp_s[:, 0].rearrange("p a b -> p (a b)"), p3, AX, ALU.max))
                chain(dve.tensor_scalar(cmp_s[:, 0], cmp_s[:, 0], NEG / 10, None, ALU.max))
                dve.tensor_tensor(p3, p3, bc(0), ALU.subtract).then_inc(*did("cmp_v", "l"))
                own("cmp_s", "exp")
                chain(dve.tensor_reduce(cmp_s[:, 1].rearrange("p a b -> p (a b)"), p3, AX, ALU.add))
                chain(dve.tensor_scalar(cmp_s[:, 1], cmp_s[:, 1], 1e-30, None, ALU.max))
                chain(dve.reciprocal(cmp_s[:, 2], cmp_s[:, 1]))
                chain(dve.tensor_tensor(cmp_s[:, 3], cmp_s[:, 2],
                                        gates[:].rearrange("p t (h c) -> p t h c", c=3)[:, :, :, 0], ALU.mult))
                dve.tensor_tensor(p3, p3, bc(3), ALU.mult).then_inc(*did("cmp_v", "p"))
                own("cmp_v", "p")
            elif stage == "att_scores":
                for u in step[1]:
                    A = att(u)
                    n = att_at[u]
                    L, sm = att_l[:, n % 4, 0:A["w"]], small[:, n % 4]
                    dve.wait_ge(*full(("sc", u)))
                    if n >= 4:
                        dve.wait_ge(*full(("pt", att_order[n - 4])))
                        own("att_p", att_order[n - 4])
                    if n == 0:
                        dve.wait_ge(C.sem["bias_in"], 16 * 2 * NH)
                    if u[0] == "swa" and u[2:] == (0, 0):
                        dve.wait_ge(C.sem[f"alibi_in{u[1]}"], 16)
                    dve.tensor_tensor_reduce(L, ps(("sc", u))[:, 0:A["w"]], A["bias"], 1.0, -3.0e38, ALU.add, ALU.max,
                                             sm[:, 0:1]).then_inc(*release(("sc", u)))
                    dve.wait_ge(*evacuated(("sc", u)))
                    if "sink" in A:
                        dve.tensor_scalar(sm[:, 1:2], sm[:, 0:1], A["sink"], -1.0, ALU.max, ALU.mult)\
                           .then_inc(*did("att_n", u))
                    else:
                        dve.tensor_scalar(sm[:, 1:2], sm[:, 0:1], -1.0, None, ALU.mult).then_inc(*did("att_n", u))
            elif stage == "att_norm":
                for u in step[1]:
                    A = att(u)
                    n = att_at[u]
                    L, sm = att_l[:, n % 4, 0:A["w"]], small[:, n % 4]
                    if "sink" in A:
                        own("swa_s", u)
                        chain(dve.tensor_tensor(sm[:, 2:3], sm[:, 2:3], sm[:, 5:6], ALU.add))
                    else:
                        own("att_exp", u)
                    chain(dve.reciprocal(sm[:, 3:4], sm[:, 2:3]))
                    if A["gate"] is not None:
                        dve.tensor_scalar(L, L, sm[:, 3:4], A["gate"], ALU.mult, ALU.mult).then_inc(*did("att_p", u))
                    else:
                        dve.tensor_scalar(L, L, sm[:, 3:4], None, ALU.mult).then_inc(*did("att_p", u))
            elif stage == "swa_split":
                dve.wait_ge(*full(("br", 1, KD - 1)))
                dve.wait_ge(*evacuated(("swa_o", KD - 1)))
                for c in range(KD):
                    split(swa_o[:, c], o_hl[0][:, c], o_hl[1][:, c], "o_ready", 2, c)
            elif stage == "mla_lora":
                own("rstd", "cq")
                for c in range(2):
                    ins = scaled("cq", cq[:, c], cq[:, c], col("mla_qa", c))
                ins.then_inc(*did("rstd_used", "cq"))
                own("rstd_used", "cq")
                own("rstd", "ckv")
                scaled("ckv", ckv[:], ckv[:], col("mla_kv")).then_inc(*did("rstd_used", "ckv"))
                own("rstd_used", "ckv")
            elif stage == "mla_rope_k":
                dve.wait_ge(C.sem["kr_in"], 16 * 2)
                dve.wait_ge(C.sem["mixer_in"], 16 * N_MIXER)
                dve.tensor_tensor(kr[:, 0], kr[:, 0], rope_c[:], ALU.mult)
                chain(dve.tensor_tensor(kr[:, 1], kr[:, 1], rope_s[:], ALU.mult))
                dve.tensor_tensor(kr[:, 0], kr[:, 0], kr[:, 1], ALU.add).then_inc(*did("mla_k"))
                own("mla_k")
            elif stage == "mla_qk":
                h = step[1]
                dve.wait_ge(*full(("mk", h)))
                dve.tensor_tensor(mk[0:QKD, h], ps(("mk", h))[0:QKD, :], kr[:, 0], ALU.add).then_inc(*release(("mk", h)))
                dve.wait_ge(*evacuated(("mk", h)))
            elif stage == "mla_rope_q":
                h = step[1]
                dve.wait_ge(C.sem["kr_in"], 16 * (4 + 2 * h))
                chain(dve.tensor_tensor(mq[0:QKD, h], mq[0:QKD, h], rope_c[:], ALU.mult))
                chain(dve.tensor_tensor(kr[:, 1], kr[:, 1], rope_s[:], ALU.mult))
                dve.tensor_tensor(mq[0:QKD, h], mq[0:QKD, h], kr[:, 1], ALU.add).then_inc(*did("mla_q", h))
                own("mla_q", h)
            elif stage == "mla_scale":
                h = step[1]
                own("rstd", ("mk", h))
                scaled(("mk", h), mk[0:QKD, h], mk[0:QKD, h], col("mla_k", parts=QKD)).then_inc(*did("rstd_used", ("mk", h)))
                own("rstd", ("mq", h))
                scaled(("mq", h), mq[0:QKD, h], mq[0:QKD, h], col("mla_q", parts=QKD)).then_inc(*did("rstd_used", ("mq", h)))
                own("rstd_used", ("mq", h))
            elif stage == "sb_scores":
                _, pair, kt = step
                w = T - kt * P
                for h in (2 * pair, 2 * pair + 1):
                    n = sb_order.index((h, kt))
                    own("sb_exp", h, kt)
                    if h >= 2 and kt == NT - 1:
                        dve.wait_ge(*full(("r", h - 2, 0)))
                    sp = sb_sp[:, h % 2, SB_OFF[kt]:SB_OFF[kt] + w]
                    dve.scalar_tensor_tensor(out=sp, in0=ps(("z", h, kt))[:, 0:w], scalar=0.0,
                                             in1=sb_e[:, n % 2, 0:w], op0=ALU.max, op1=ALU.add)\
                       .then_inc(*release(("z", h, kt)))
                    dve.wait_ge(*evacuated(("z", h, kt)))
            elif stage == "ret_scores":
                _, h, jt = step
                w = T - jt * P
                dve.wait_ge(*full(("rs", h, jt)))
                if h >= 1:
                    dve.wait_ge(*full(("ret_o", h - 1, 1)))
                if h == 0 and jt == 0:
                    dve.wait_ge(C.sem["late_in"], 16)
                dve.tensor_tensor(ret_a[:, SB_OFF[jt]:SB_OFF[jt] + w], ps(("rs", h, jt))[:, 0:w], decay[:, h, 0:w],
                                  ALU.mult).then_inc(*release(("rs", h, jt)))
            elif stage == "ret_sum":
                h = step[1]
                for e in range(2):
                    dve.wait_ge(*evacuated(("ret_o", h, e)))
                dve.tensor_tensor(tmp[:, 1], mix_o[:, 0], mix_o[:, 1], ALU.add).then_inc(*did("ret_s", h))
            elif stage == "ret_mean":
                h = step[1]
                dve.wait_ge(*full(("mean", h)))
                dve.tensor_scalar(tmp[:, 0], ps(("mean", h))[:], -1 / 256, None, ALU.mult).then_inc(*release(("mean", h)))
                dve.wait_ge(*evacuated(("mean", h)))
                for e in range(2):
                    if h >= 1:
                        own("ret_done", h - 1, e)
                    dve.tensor_tensor(ret_d[:, e], mix_o[:, e], tmp[:, 0], ALU.add).then_inc(*did("ret_d", h, e))
                own("ret_d", h, 1)
            elif stage in ("ret_out", "gla_out"):
                h = step[1]
                ret = stage == "ret_out"
                key = ("ret" if ret else "gla", h)
                own("rstd", key)
                if not ret and h == 0:
                    dve.wait_ge(*full(("br", 0, KD - 1)))
                for e in range(2):
                    c = 2 * h + e
                    src = ret_d[:, e] if ret else mix_o[:, e]
                    t = tmp[:, e]
                    ins = scaled(key, t, src, col("ret_w" if ret else "gla_w", c))
                    ins.then_inc(*did("ret_done" if ret else "gla_done", h, e))
                    own("ret_done" if ret else "gla_done", h, e)
                    if ret:
                        ins = dve.scalar_tensor_tensor(out=t, in0=t, scalar=col("ret_b", c), in1=silu[:, e],
                                                       op0=ALU.add, op1=ALU.mult)
                    else:
                        ins = dve.tensor_tensor(t, t, silu[:, e], ALU.mult)
                    if e == 1:
                        ins.then_inc(*did("rstd_used", key))
                        own("rstd_used", key)
                    else:
                        chain(ins)
                    split(t, o_hl[0][:, c], o_hl[1][:, c], "o_ready", 0 if ret else 1, c)
            elif stage == "gla_decay":
                h = step[1]
                own("gla_s", "ln", h)
                dve.wait_ge(C.sem["late_in"], 16 * 4)
                g0, g1 = g_ln, g_b
                dve.tensor_scalar(g_eb, ps(("gz", h))[:], col("b_alpha", h), 0.0, ALU.add, ALU.min)\
                   .then_inc(*release(("gz", h)))
                dve.wait_ge(*evacuated(("gz", h)))
                chain(dve.tensor_tensor(g0, g_eb, g0, ALU.subtract))
                chain(dve.tensor_scalar(g0, g0, 1 / 16.0, -1.0, ALU.mult, ALU.max))
                chain(dve.tensor_tensor_scan(g1, gscan[:], g0, 0.0, ALU.mult, ALU.add))
                b4 = g1.rearrange("p (n c) -> p n c", c=GC)
                dve.tensor_tensor(g_ed[:].rearrange("p (n c) -> p n c", c=GC),
                                  b4[:, :, GC - 1:GC].to_broadcast([P, NGC, GC]), b4, ALU.subtract)\
                   .then_inc(*did("gla_v", "d", h))
            elif stage == "gla_scale":
                h = step[1]
                if h >= 1:
                    dve.wait_ge(*full(("gla_o", h - 1, 1)))
                dve.wait_ge(*evacuated(("gq", h)))
                dve.wait_ge(*evacuated(("gk", h)))
                own("gla_s", "eb", h)
                dve.tensor_tensor(qf[:, h % 2], qf[:, h % 2], g_eb, ALU.mult)
                own("gla_s", "enb", h)
                dve.tensor_tensor(gk_i[:], kf[:, h % 2], gk_i[:], ALU.mult)
                own("gla_s", "ed", h)
                dve.tensor_tensor(kf[:, h % 2], kf[:, h % 2], g_ed[:], ALU.mult).then_inc(*did("gla_v", "kd", h))
                own("gla_v", "kd", h)
            elif stage == "gla_turn":
                h = step[1]
                dve.wait_ge(*full(("ga_s", h)))
                dve.tensor_tensor(ga_m, ps(("ga_s", h))[:].rearrange("p (m i) -> p m i", m=NT),
                                  gmask[:, None, :].to_broadcast([P, NT, P]), ALU.mult).then_inc(*release(("ga_s", h)))
            elif stage == "gla_chunks":
                h = step[1]
                for n in range(NGC - 1):
                    dve.wait_ge(*full(("kv", h, n)))
                    src = ps(("kv", h, n))[:, 0:256]
                    if n == 0:
                        ins = dve.tensor_copy(g_st[:, 0], src)
                    else:
                        dve.wait_ge(*evacuated(("kv", h, n - 1)))
                        a_n = g_eb[:, (n + 1) * GC - 1:(n + 1) * GC]
                        ins = dve.scalar_tensor_tensor(out=g_st[:, n], in0=g_st[:, n - 1], scalar=a_n, in1=src,
                                                       op0=ALU.mult, op1=ALU.add)
                    ins.then_inc(*release(("kv", h, n)))
            elif stage == "residual" and step[2] not in POOLED:
                _, key, c = step
                own("rstd", key)
                mine = [k for k in POOLED_ORDER if k not in POOLED]
                n = mine.index(c)
                if n >= 2:
                    own("x_ready", key, mine[n - 2])
                t = tmp[:, n % 2]
                ins = scaled(key, t, merged[:, c], col(key, c))
                if c == mine[-1]:
                    ins.then_inc(*did("rstd_used", key))
                    own("rstd_used", key)
                else:
                    chain(ins)
                dve.tensor_tensor(x_sb[:, c], x_sb[:, c], t, ALU.add).then_inc(*did("x_ready", key, c))
                if c == mine[-1]:
                    own("x_ready", key, c)

    @block.gpsimd
    def _(pool):
        def residual(key):
            pool.wait_ge(*after("rstd", key))
            for c in POOLED:
                pool.tensor_tensor(sq_sum[:], merged[:, c], rstd(key), ALU.mult).then_inc(*did("p_chain", key, c, 0))
                pool.wait_ge(*after("p_chain", key, c, 0))
                pool.tensor_scalar(sq_sum[:], sq_sum[:], col(key, c), None, ALU.mult).then_inc(*did("p_chain", key, c, 1))
                pool.wait_ge(*after("p_chain", key, c, 1))
                pool.tensor_tensor(x_sb[:, c], x_sb[:, c], sq_sum[:], ALU.add).then_inc(*did("x_pool", key, c))
                pool.wait_ge(*after("x_pool", key, c))

        for i in range(N_SLOTS):
            if i == SLOTS[("fg", 0, 1)][0] + 1:
                residual("post")
            pool.wait_ge(C.sem[f"w_landed{i % RAW}"], 16 * (i // RAW + 1))
            if i >= SPL:
                pool.wait_ge(*slot_done[i - SPL])
            hi, lo, raw = w_hi[:, i % SPL], w_lo[:, i % SPL], w_raw[:, i % RAW]
            pool.tensor_scalar(hi, raw, 1.0, 0.0, ALU.mult, ALU.add).then_inc(*did("w_hi", i))
            pool.wait_ge(*after("w_hi", i))
            pool.tensor_tensor(lo, raw, hi.bitcast(F32), ALU.subtract).then_inc(*did("w_lo", i))
        residual("fpost")

    @block.sync
    def _(sp):
        for g in range(4):
            sp.dma_start(x_sb[:, 2 * g:2 * g + 2], a["x"][:, 2 * g:2 * g + 2]).then_inc(C.sem[f"x_in{g}"], 16)
        n = 0

        def bias_tables(part):
            if part == 0:
                for nn in range(len(TAB)):
                    sp.wait_ge(*evacuated(("tab", nn)))
                sp.dma_start(a["table"], tab[:]).then_inc(C.sem["table_out"], 16)
                return
            if part == 1:
                sp.wait_ge(C.sem["table_out"], 16)
                for k, (c0, w) in enumerate(((0, 640), (640, 1024))):
                    rows = P if k == 0 else N_CMP
                    dst = a["scratch"][:, k, 0:rows * w].rearrange("h (p w) -> h p w", w=w)
                    sp.dma_start(dst, a["table"][:, None, c0:c0 + w].to_broadcast([NH, rows, w]))\
                      .then_inc(C.sem["bias_out"], 16)
                return
            sp.wait_ge(C.sem["bias_out"], 16 * 2)
            t = a["scratch"].tensor
            for h in range(NH):
                sp.dma_start(toep[:, h], bass.AP(tensor=t, offset=(2 * h) * P * 1024 + P - 1,
                                                 ap=[[640 - 1, P], [1, T]])).then_inc(C.sem["bias_in"], 16)
                sp.dma_start(cb_t[:, h], bass.AP(tensor=t, offset=(2 * h + 1) * P * 1024 + T - CMP_LEN + 1,
                                                 ap=[[1024 - CMP_STRIDE, N_CMP], [1, T]]))\
                  .then_inc(C.sem["bias_in"], 16)

        for step in ORDER:
            stage = step[0]
            name = step[1]
            if stage in ("fm", "tm", "cmp_up") or (stage == "down" and step[3] == 0):
                for _ in range(SLOTS[name][1]):
                    if n >= RAW:
                        sp.wait_ge(*after("w_lo", n - RAW))
                    sp.dma_start(w_raw[:, n % RAW], a["w"][n]).then_inc(C.sem[f"w_landed{n % RAW}"], 16)
                    n += 1
                    if n in (4, 5, 7):
                        bias_tables((4, 5, 7).index(n))
            if name == (("rv", 0), "s", 0):
                sp.wait_ge(*full(("down1", 1, KD - 1)))
                sp.dma_start(decay[:], a["decay"]).then_inc(C.sem["late_in"], 16)
            if name == ("br", 0, 2):
                sp.wait_ge(*after("o_ready", 0, KD - 1))
                sp.wait_ge(C.sem["late_in"], 16)
                for t, src in ((wa2, "wa2"), (gscan, "gscan"), (gmask, "gmask")):
                    sp.dma_start(t[:], a[src]).then_inc(C.sem["late_in"], 16)
                sp.wait_ge(C.sem["late_in"], 16 * 4)
            if stage == "tm" and name == ("wv", "s", 1):
                sp.wait_ge(*full(("gla_o", 3, 1)))
                sp.wait_ge(*after("o_ready", 1, KD - 1))
                for c in range(8):
                    sp.dma_start(alibi[:, 2 * c:2 * c + 2], a["alibi"][:, 2 * c:2 * c + 2])\
                      .then_inc(C.sem[f"alibi_in{c}"], 16)
        for c in POOLED_ORDER:
            sp.wait_ge(*after("x_pool" if c in POOLED else "x_ready", "fpost", c))
            sp.dma_start(a["y"][:, c], x_sb[:, c]).then_inc(C.sem["y_out"], 16)
        sp.wait_ge(C.sem["y_out"], 16 * KD)

    return C.at


N_CONST = 3
N_MISC = 2
N_MIXER = 10


def _constants():
    f = np.float32
    i = np.arange(P)
    c = {}
    c["ones"] = np.ones((P, P), f)
    c["ones64"] = (i[:, None] // HD == i[None] // HD).astype(f)
    c["ident"] = np.eye(P, dtype=f)
    x = np.arange(T)
    c["causal"] = np.where(x[None] - (T - P) <= i[:, None], 0.0, NEG).astype(f)
    c["sbm"] = np.stack([-(i[:, None] >= i[None]).astype(f), -np.ones((P, P), f),
                         np.where(i[None] > i[:, None], 0.0, NEG).astype(f)], axis=1)
    exact = N_BUCKETS // 2
    dist = np.concatenate([T - 1 - np.arange(640), np.arange(1024) - T])
    d = np.maximum(dist, 1).astype(f)
    large = exact + (np.log(d / f(exact)) / f(np.log(128 / exact)) * f(N_BUCKETS - exact)).astype(np.int32)
    bucket = np.where(dist < exact, dist, np.minimum(large, N_BUCKETS - 1))
    bucket = np.where(dist < 0, N_BUCKETS, bucket)
    c["onehot"] = (np.arange(N_BUCKETS + 1)[:, None] == bucket[None]).astype(f)
    inv = (1.0 / (f(10000.0) ** (np.arange(0, 32, 2, dtype=f) / f(32)))).astype(f)
    ang = np.arange(T, dtype=f)[None] * inv[:, None]
    cos, sin = np.cos(ang), np.sin(ang)
    c["rope_c"] = np.concatenate([np.ones((HD, T), f), cos, cos]).astype(f)
    c["rope_s"] = np.concatenate([np.zeros((HD, T), f), -sin, sin]).astype(f)
    log_g = np.log1p(-np.exp2(-5.0 - np.arange(4)))
    rel = (x[None] - i[:, None])
    c["decay"] = np.stack([np.where(rel >= 0, np.exp(rel * g), 0.0) * P ** -0.5 for g in log_g], axis=1).astype(f)
    c["gscan"] = np.broadcast_to((x % GC != 0).astype(f), (P, T))
    c["gmask"] = ((i[:, None] // GC == i[None] // GC) & (i[:, None] <= i[None])).astype(f)
    slope = np.exp2(-8.0 * np.arange(1, 17) / 16)
    dd = P + i[:, None] - np.arange(2 * P)[None]
    c["alibi"] = np.stack([np.where((dd >= 0) & (dd < P), -slope[SWA_HEAD[k // 2][k % 2]] * dd, NEG)
                           for k in range(16)], axis=1).astype(f)
    return c


def _fm(w):
    n = w.shape[1] // P
    return w.reshape(KD, P, n, P).transpose(2, 1, 0, 3).reshape(n, P, 1024)


def _tm(w, per):
    w = np.pad(w, ((0, 0), (0, 1024 // per - w.shape[1])))
    return w.reshape(KD // per, per, P, 1024 // per).transpose(0, 2, 1, 3).reshape(KD // per, P, 1024)


def _down(w):
    nk = w.shape[0] // P
    blocks = w.reshape(nk, P, KD, P).transpose(2, 0, 1, 3).reshape(KD * nk, P, P)
    return blocks.reshape(-1, 8, P, P).transpose(0, 2, 1, 3).reshape(-1, P, 1024)


def _weights(v):
    w1 = v["w_in"][0]
    sizes = [256] * 3 + [256] + [64] * 6 + [12] + [192, 128, 32] + [256] * 3
    at = np.concatenate([[0], np.cumsum(sizes)])
    ab, ac, au, nq, kc, vc, ks, vs, kw, vw, ng, cq, ckv, kr, sq, sk, sv = [
        w1[:, at[i]:at[i + 1]] for i in range(len(sizes))]
    zeros = lambda n: np.zeros((D, n), w1.dtype)
    one = lambda w: _fm(w)[0]
    slot = {"kvc": one(np.concatenate([kc, vc], 1)), "ksw": one(np.concatenate([ks, kw], 1)),
            "cq0": one(cq[:, :P]), "cqr": one(np.concatenate([cq[:, P:], kr, zeros(32)], 1)), "ckv": one(ckv)}
    for c in range(2):
        cc = slice(c * P, (c + 1) * P)
        slot.update({f"nq{c}": one(nq[:, cc]), f"sq{c}": one(sq[:, cc]), f"sk{c}": one(sk[:, cc]),
                     ("ab", c): one(ab[:, cc]), ("ac", c): one(ac[:, cc]), ("au", c): one(au[:, cc])})
    slot["v1"] = _tm(np.concatenate([vs, vw, sv, ng], 1), 2)
    for kv in range(2):
        for s, w in enumerate(v["cmp_w1"][0, kv].reshape(4, 4, P, 256).transpose(0, 2, 1, 3).reshape(4, P, 1024)):
            slot[("cmp", kv, s)] = w
    for c, s in enumerate(_fm(v["w_out"][0])):
        slot[("wout", c)] = s
    for half in range(2):
        for c in range(HALF1):
            g = half * HALF1 + c
            slot[("up1", half, c)] = one(v["ffn_w1"][0][:, g * P:(g + 1) * P])
        slot[("down1", half)] = _down(v["ffn_w2"][0][half * HALF1 * P:(half + 1) * HALF1 * P])
    w2 = v["w_in_2"][0]
    sizes = [512, 512, 1024, 1024, 512, 512, 1024, 1024, 16, 1024, 256, 256, 3072]
    at = np.concatenate([[0], np.cumsum(sizes)])
    rq, rk, rv, rg, gq, gk, gv, gg, ga, sq, sk, sv, gate = [w2[:, at[i]:at[i + 1]] for i in range(len(sizes))]
    for h in range(4):
        for name, w in (("rq", rq), ("rk", rk), ("gq", gq), ("gk", gk)):
            slot[(name, h)] = one(w[:, h * P:(h + 1) * P])
        for name, w in (("rg", rg), ("gg", gg)):
            for e in range(2):
                slot[(name, h, e)] = one(w[:, (2 * h + e) * P:(2 * h + e + 1) * P])
    for g in range(2):
        slot[("rv", g)] = _tm(rv[:, g * 512:(g + 1) * 512], 2)
        slot[("gv", g)] = _tm(gv[:, g * 512:(g + 1) * 512], 2)
    slot["ga"] = one(np.concatenate([ga, zeros(P - 16)], 1))
    pairs = [h for c in SWA_HEAD for h in c]
    sq = sq.reshape(D, 16, HD)[:, pairs].reshape(D, 1024)
    for c in range(8):
        slot[("wq", c)] = one(sq[:, c * P:(c + 1) * P])
    for c in range(2):
        slot[("wk", c)] = one(sk[:, c * P:(c + 1) * P])
    slot["wv"] = _tm(sv, 4)
    for b in range(3):
        wb = v["w_branch_2"][0, b]
        if b == 2:
            wb = wb.reshape(16, HD, D)[pairs].reshape(1024, D)
        for m in range(KD):
            mm = slice(m * P, (m + 1) * P)
            slot[("gate", b, m)] = one(gate[:, b * D:(b + 1) * D][:, mm])
            slot[("br", b, m)] = one(wb[:, mm])
    for c, s in enumerate(_fm(v["w_out_2"][0])):
        slot[("wout2", c)] = s
    for half in range(2):
        for c in range(HALF2):
            g = slice((half * HALF2 + c) * P, (half * HALF2 + c + 1) * P)
            slot[("fg", half, c)] = one(v["ffn_w_gate_2"][0][:, g])
            slot[("fu", half, c)] = one(v["ffn_w_up_2"][0][:, g])
        slot[("down2", half)] = _down(v["ffn_w_down_2"][0][half * HALF2 * P:(half + 1) * HALF2 * P])
    def of(name, n):
        if isinstance(name, tuple) and name[-2:-1] == ("s",):
            return slot[name[0]].reshape(-1, P, 1024)[name[-1]][None]
        return slot[name].reshape(n, P, 1024)

    return np.concatenate([of(name, n) for name, (_, n) in SLOTS.items()])


def _params(v):
    f = v["x"].dtype
    cols = lambda w: np.pad(w, (0, -len(w) % P)).reshape(-1, P).T
    twice = lambda w: np.concatenate([w, w])[:, None]
    pos = v["cmp_pos"][0].reshape(2, 16, P)
    parts = [cols(v["norm1_w"][0]),
             np.concatenate([cols(v["conv_w"][0, k]) for k in range(3)], 1), cols(v["conv_b"][0]),
             twice(v["nsa_q_norm"][0]), twice(v["nsa_k_norm"][0, 0]),
             v["nsa_k_norm"][0, 1:3].reshape(P, 1),
             cols(v["mla_q_a_norm"][0]), cols(v["mla_kv_norm"][0]), cols(v["mla_q_norm"][0]),
             cols(v["mla_k_norm"][0]), cols(v["out_norm_w"][0]), cols(v["norm2_w"][0]),
             pos.reshape(32, P).T, cols(v["norm_mix_pre_2"][0]), cols(v["norm_mix_post_2"][0]),
             cols(v["ret_norm_w_2"][0]), cols(v["ret_norm_b_2"][0]), cols(v["gla_b_alpha_2"][0]),
             cols(v["gla_norm_w_2"][0]), cols(v["norm_ffn_pre_2"][0]), cols(v["norm_ffn_post_2"][0]),
             np.broadcast_to(v["attn_sinks_2"][0][[h for c in SWA_HEAD for h in c]][None], (P, 16)),
             np.arange(P)[:, None] // 32 == np.arange(NH)]
    return np.ascontiguousarray(np.concatenate(parts, axis=1).astype(f))


def _arrays(v):
    f = np.float32
    out = dict(_constants())
    out["x"] = v["x"][0].reshape(T, KD, P).transpose(2, 1, 0)
    out["w"] = _weights(v)
    out["par"] = _params(v)
    out["rel_bias"] = v["rel_bias"]
    w2 = v["cmp_w2"][0]
    out["w2k"] = np.concatenate([w2[0], w2[0]], 1).reshape(2, P, P).transpose(1, 0, 2)
    out["w2v"] = w2[1].reshape(2, P, HD).transpose(1, 0, 2)
    wqb = v["mla_wq_b"][0].reshape(192, NH, QKD)
    out["wqb"] = np.pad(wqb, ((0, 64), (0, 0), (0, 0))).reshape(2, P, NH, QKD).transpose(1, 0, 2, 3)
    wkv = v["mla_wkv_b"][0].reshape(P, NH, 2 * HD)
    out["wkb"] = np.pad(wkv[:, :, :HD], ((0, 0), (0, 0), (0, 32)))
    out["wvb"] = wkv[:, :, HD:].reshape(P, NH * HD)
    out["wa2"] = v["gla_w_alpha2_2"][0]
    return {k: np.ascontiguousarray(t) for k, t in out.items()}


def _program_in(nc, arrays, known):
    a = {k: nc.dram_tensor(f"in_{k}", t.shape, mybir.dt.from_np(t.dtype), kind="ExternalInput").ap()
         for k, t in arrays.items()}
    a["scratch"] = nc.dram_tensor("scratch", (NH, 2, P * 1024), F32, kind="Internal").ap()
    a["table"] = nc.dram_tensor("table", (NH, 640 + 1024), F32, kind="Internal").ap()
    a["y"] = nc.dram_tensor("out_y", (P, KD, T), F32, kind="ExternalOutput").ap()
    return build(nc, a, known)


def kernel(**inputs):
    import concourse.bacc as _bacc
    from concourse.bass_utils import run_bass_kernel_spmd as _run

    arrays = _arrays({k: np.asarray(t) for k, t in inputs.items()})
    counting = _bacc.Bacc("TRN2", target_bir_lowering=False, num_devices=1)
    counts = _program_in(counting, arrays, {})
    nc = _bacc.Bacc("TRN2", target_bir_lowering=False, num_devices=1)
    _program_in(nc, arrays, counts)
    r = _run(nc, [{f"in_{k}": t for k, t in arrays.items()}], core_ids=[0])
    y = r.results[0]["out_y"]
    return np.ascontiguousarray(y.transpose(2, 1, 0).reshape(1, T, D))
```
